# Optimizing a Trainium2 kernel written in Bass

```python
import math
import jax, jax.numpy as jnp
from jax import lax
import numpy as np

"""Hybrid autoregressive decoder block (parallel-branch, Griffin-style gated merge).

Per layer:
  u   = RMSNorm(x) * (1 + scale1(c)) + shift1(c)
  one combined input projection of u -> [attention q/k/v for 3 dilation head groups |
      mLSTM q/k/v/o/i/f | per-channel branch gates]
  branch A: causal dilated sliding-window attention (LongNet mixture of dilations),
            QK-norm, T5 relative-position bias, group outputs merged by softmax denominators
  branch B: mLSTM matrix memory (xLSTM), chunkwise-parallel with max stabiliser
  y   = W_out( sigmoid(g_A) * W_A(A) + sigmoid(g_B) * W_B(B) ),  x = x + gate1(c) * y
  u2  = RMSNorm(x) * (1 + scale2(c)) + shift2(c);  x = x + gate2(c) * W2(relu(W1 u2)^2)

Inputs: x (BATCH, SEQ, D_MODEL) f32, c (BATCH, D_MODEL) f32, per-layer weights with a
leading DEPTH axis, rel_bias (N_BUCKETS, N_ATT_HEADS) shared by all layers.
Output: (BATCH, SEQ, D_MODEL).
"""

D_MODEL = 1024
BATCH = 1
SEQ = 512
DEPTH = 1

ATT_GROUPS = ((128, 1), (512, 4), (2048, 16))
N_ATT_GROUPS = 3
ATT_HEADS_PER_GROUP = 4
ATT_HEAD_DIM = 128
N_ATT_HEADS = N_ATT_GROUPS * ATT_HEADS_PER_GROUP
ATT_GROUP_WIDTH = ATT_HEADS_PER_GROUP * ATT_HEAD_DIM
ATT_BLOCK = 128
ML_HEADS = 8
ML_QK_DIM = 64
ML_V_DIM = 128
ML_QK_WIDTH = ML_HEADS * ML_QK_DIM
ML_V_WIDTH = ML_HEADS * ML_V_DIM
ML_CHUNK = 64
CONV_WIDTH = 4
D_FF = 4 * D_MODEL
N_BUCKETS = 32
MAX_DISTANCE = 2048
N_BRANCHES = 2
EPS = 1e-6

IN_SPLITS = (
    N_ATT_GROUPS * ATT_GROUP_WIDTH,
    N_ATT_GROUPS * ATT_GROUP_WIDTH,
    N_ATT_GROUPS * ATT_GROUP_WIDTH,
    ML_QK_WIDTH,
    ML_QK_WIDTH,
    ML_V_WIDTH,
    ML_V_WIDTH,
    ML_HEADS,
    ML_HEADS,
    N_BRANCHES * D_MODEL,
)
D_IN = sum(IN_SPLITS)

kernel_name = 'hybrid_dilated_attn_mlstm_block'

def _rms_norm(x, gain):
    x32 = x.astype(jnp.float32)
    y = x32 * lax.rsqrt(jnp.mean(x32 * x32, axis=-1, keepdims=True) + EPS)
    return (y * gain.astype(jnp.float32)).astype(x.dtype)

def _t5_bucket(dist):
    max_exact = N_BUCKETS // 2
    d = jnp.maximum(dist, max_exact).astype(jnp.float32)
    large = max_exact + (jnp.log(d / max_exact) / math.log(MAX_DISTANCE / max_exact)
                         * (N_BUCKETS - max_exact)).astype(jnp.int32)
    large = jnp.minimum(large, N_BUCKETS - 1)
    return jnp.where(dist < max_exact, dist, large)

def _causal_conv(x, w, b):
    S = x.shape[1]
    xp = jnp.pad(x, ((0, 0), (CONV_WIDTH - 1, 0), (0, 0)))
    y = b
    for j in range(CONV_WIDTH):
        y = y + w[j] * xp[:, j:j + S]
    return y

def _dilated_attention(q, k, v, bias_table, window, dilation):
    B, S, H, dh = q.shape
    n_look = window // dilation
    n_sub = S // dilation
    nb = -(-n_sub // ATT_BLOCK)
    n_pad = nb * ATT_BLOCK

    def to_blocks(t):
        t = t.reshape(B, n_sub, dilation, H, dh).transpose(0, 2, 3, 1, 4)
        t = jnp.pad(t, ((0, 0), (0, 0), (0, 0), (0, n_pad - n_sub), (0, 0)))
        return t.astype(jnp.float32).reshape(B, dilation, H, nb, ATT_BLOCK, dh)

    def with_prev(t):
        prev = jnp.pad(t, ((0, 0), (0, 0), (0, 0), (1, 0), (0, 0), (0, 0)))[:, :, :, :-1]
        return jnp.concatenate([prev, t], axis=4)

    qb = to_blocks(q)
    kb = with_prev(to_blocks(k))
    vb = with_prev(to_blocks(v))

    i = jnp.arange(ATT_BLOCK)[:, None]
    j = jnp.arange(2 * ATT_BLOCK)[None, :]
    delta = ATT_BLOCK + i - j
    key_idx = jnp.arange(nb)[:, None, None] * ATT_BLOCK - ATT_BLOCK + j
    valid = (delta >= 0) & (delta <= n_look) & (key_idx >= 0)
    bucket = _t5_bucket(jnp.maximum(delta, 0) * dilation)
    bias = bias_table[bucket].astype(jnp.float32).transpose(2, 0, 1)

    s = jnp.einsum('brhnqd,brhnkd->brhnqk', qb, kb) * (dh ** -0.5) + bias[None, None, :, None]
    s = jnp.where(valid[None, None, None], s, -jnp.inf)
    m = jnp.max(s, axis=-1, keepdims=True)
    p = jnp.exp(s - m)
    l = jnp.sum(p, axis=-1, keepdims=True)
    o = jnp.einsum('brhnqk,brhnkd->brhnqd', p, vb) / l
    lse = (m + jnp.log(l))[..., 0]

    o = o.reshape(B, dilation, H, n_pad, dh)[:, :, :, :n_sub]
    o = o.transpose(0, 3, 1, 2, 4).reshape(B, S, H, dh)
    lse = lse.reshape(B, dilation, H, n_pad)[..., :n_sub]
    lse = lse.transpose(0, 3, 1, 2).reshape(B, S, H)
    return o, lse

def _mlstm_chunkwise(q, k, v, log_i, log_f):
    B, S, H, dk = q.shape
    dv = v.shape[-1]
    L = ML_CHUNK
    nc = S // L

    def chunks(t):
        rest = t.shape[3:]
        t = t.reshape((B, nc, L, H) + rest)
        return t.transpose((1, 0, 3, 2) + tuple(range(4, t.ndim)))

    causal = jnp.tril(jnp.ones((L, L), dtype=bool))

    def step(carry, xs):
        C, n, m = carry
        qc, kc, vc, li, lf = xs
        b = jnp.cumsum(lf, axis=-1)
        a = b + m[..., None]
        Dm = b[..., :, None] - b[..., None, :] + li[..., None, :]
        Dm = jnp.where(causal, Dm, -jnp.inf)
        m_t = jnp.maximum(a, jnp.max(Dm, axis=-1))
        w = jnp.einsum('bhtd,bhsd->bhts', qc, kc) * jnp.exp(Dm - m_t[..., None])
        inter = jnp.exp(a - m_t)
        num = jnp.einsum('bhts,bhsv->bhtv', w, vc) + inter[..., None] * jnp.einsum('bhtd,bhdv->bhtv', qc, C)
        nq = jnp.sum(w, axis=-1) + inter * jnp.einsum('bhtd,bhd->bht', qc, n)
        h = num / jnp.maximum(jnp.abs(nq), jnp.exp(-m_t))[..., None]
        b_end = b[..., -1]
        g = b_end[..., None] - b + li
        m_new = jnp.maximum(b_end + m, jnp.max(g, axis=-1))
        decay = jnp.exp(b_end + m - m_new)
        wk = jnp.exp(g - m_new[..., None])
        C = decay[..., None, None] * C + jnp.einsum('bhs,bhsd,bhsv->bhdv', wk, kc, vc)
        n = decay[..., None] * n + jnp.einsum('bhs,bhsd->bhd', wk, kc)
        return (C, n, m_new), h

    init = (jnp.zeros((B, H, dk, dv), jnp.float32),
            jnp.zeros((B, H, dk), jnp.float32),
            jnp.zeros((B, H), jnp.float32))
    _, h = lax.scan(step, init, (chunks(q), chunks(k), chunks(v), chunks(log_i), chunks(log_f)))
    return h.transpose(1, 0, 3, 2, 4).reshape(B, S, H, dv)

def setup_inputs(seed: int = 0) -> dict:
    key = jax.random.key(seed)
    ks = jax.random.split(key, 20)
    f32 = jnp.float32

    def w(k, shape, fan_in, gain=1.0):
        return jax.random.normal(k, shape, f32) * (gain * fan_in ** -0.5)

    def gain_vec(k, shape):
        return 1.0 + 0.02 * jax.random.normal(k, shape, f32)

    gate_bias_offset = jnp.stack([jnp.zeros((ML_HEADS,), f32),
                                  jnp.linspace(3.0, 6.0, ML_HEADS, dtype=f32)])
    return {
        'x': jax.random.normal(ks[0], (BATCH, SEQ, D_MODEL), f32),
        'c': jax.random.normal(ks[1], (BATCH, D_MODEL), f32),
        'w_ada': w(ks[2], (DEPTH, D_MODEL, 6 * D_MODEL), D_MODEL, 0.5),
        'b_ada': 0.02 * jax.random.normal(ks[3], (DEPTH, 6 * D_MODEL), f32),
        'norm1_g': gain_vec(ks[4], (DEPTH, D_MODEL)),
        'norm2_g': gain_vec(ks[5], (DEPTH, D_MODEL)),
        'w_in': w(ks[6], (DEPTH, D_MODEL, D_IN), D_MODEL),
        'b_if': gate_bias_offset + 0.1 * jax.random.normal(ks[7], (DEPTH, 2, ML_HEADS), f32),
        'conv_w': w(ks[8], (DEPTH, CONV_WIDTH, 2 * ML_QK_WIDTH), CONV_WIDTH),
        'conv_b': 0.02 * jax.random.normal(ks[9], (DEPTH, 2 * ML_QK_WIDTH), f32),
        'q_norm_g': gain_vec(ks[10], (DEPTH, ATT_HEAD_DIM)),
        'k_norm_g': gain_vec(ks[11], (DEPTH, ATT_HEAD_DIM)),
        'rel_bias': 0.5 * jax.random.normal(ks[12], (N_BUCKETS, N_ATT_HEADS), f32),
        'mlstm_norm_g': gain_vec(ks[13], (DEPTH, ML_V_WIDTH)),
        'w_att_out': w(ks[14], (DEPTH, ATT_GROUP_WIDTH, D_MODEL), ATT_GROUP_WIDTH),
        'w_ml_out': w(ks[15], (DEPTH, ML_V_WIDTH, D_MODEL), ML_V_WIDTH),
        'w_out': w(ks[16], (DEPTH, D_MODEL, D_MODEL), D_MODEL),
        'w_ff1': w(ks[17], (DEPTH, D_MODEL, D_FF), D_MODEL),
        'w_ff2': w(ks[18], (DEPTH, D_FF, D_MODEL), D_FF),
    }

def reference(x, c, w_ada, b_ada, norm1_g, norm2_g, w_in, b_if, conv_w, conv_b,
              q_norm_g, k_norm_g, rel_bias, mlstm_norm_g, w_att_out, w_ml_out,
              w_out, w_ff1, w_ff2):
    B, S, _ = x.shape
    split_points = [int(p) for p in np.cumsum(IN_SPLITS)[:-1]]
    for l in range(DEPTH):
        ada = jax.nn.silu(c) @ w_ada[l] + b_ada[l]
        shift1, scale1, gate1, shift2, scale2, gate2 = [t[:, None, :] for t in jnp.split(ada, 6, axis=-1)]

        u = _rms_norm(x, norm1_g[l]) * (1 + scale1) + shift1
        proj = u @ w_in[l]
        aq, ak, av, mq, mk, mv, mo, mi, mf, gates = jnp.split(proj, split_points, axis=-1)

        aq = _rms_norm(aq.reshape(B, S, N_ATT_HEADS, ATT_HEAD_DIM), q_norm_g[l])
        ak = _rms_norm(ak.reshape(B, S, N_ATT_HEADS, ATT_HEAD_DIM), k_norm_g[l])
        av = av.reshape(B, S, N_ATT_HEADS, ATT_HEAD_DIM)
        outs, lses = [], []
        for g, (window, dilation) in enumerate(ATT_GROUPS):
            sl = slice(g * ATT_HEADS_PER_GROUP, (g + 1) * ATT_HEADS_PER_GROUP)
            o, lse = _dilated_attention(aq[:, :, sl], ak[:, :, sl], av[:, :, sl],
                                        rel_bias[:, sl], window, dilation)
            outs.append(o)
            lses.append(lse)
        wts = jax.nn.softmax(jnp.stack(lses, axis=0), axis=0)
        att = jnp.sum(wts[..., None] * jnp.stack(outs, axis=0), axis=0)
        y_att = att.reshape(B, S, ATT_GROUP_WIDTH).astype(x.dtype) @ w_att_out[l]

        qk = jax.nn.silu(_causal_conv(jnp.concatenate([mq, mk], axis=-1), conv_w[l], conv_b[l]))
        mq, mk = jnp.split(qk.astype(jnp.float32), 2, axis=-1)
        mq = mq.reshape(B, S, ML_HEADS, ML_QK_DIM)
        mk = mk.reshape(B, S, ML_HEADS, ML_QK_DIM) * (ML_QK_DIM ** -0.5)
        mv = mv.astype(jnp.float32).reshape(B, S, ML_HEADS, ML_V_DIM)
        log_i = mi.astype(jnp.float32) + b_if[l, 0].astype(jnp.float32)
        log_f = jax.nn.log_sigmoid(mf.astype(jnp.float32) + b_if[l, 1].astype(jnp.float32))
        h = _mlstm_chunkwise(mq, mk, mv, log_i, log_f)
        h = _rms_norm(h, mlstm_norm_g[l].reshape(ML_HEADS, ML_V_DIM)).reshape(B, S, ML_V_WIDTH)
        h = h * jax.nn.sigmoid(mo.astype(jnp.float32))
        y_ml = h.astype(x.dtype) @ w_ml_out[l]

        g_att, g_ml = jnp.split(jax.nn.sigmoid(gates), N_BRANCHES, axis=-1)
        y = (g_att * y_att + g_ml * y_ml) @ w_out[l]
        x = x + gate1 * y

        u2 = _rms_norm(x, norm2_g[l]) * (1 + scale2) + shift2
        hdn = jnp.square(jax.nn.relu(u2 @ w_ff1[l]))
        x = x + gate2 * (hdn @ w_ff2[l])
    return x


_drawn_inputs = setup_inputs


def setup_inputs(seed=0):
    import zlib

    import numpy as np

    out = dict(_drawn_inputs(seed))
    spreads = {}
    factors = {'norm1_g': 8.0,
     'norm2_g': 6.129,
     'conv_b': 64.0,
     'q_norm_g': 8.0,
     'k_norm_g': 8.0,
     'rel_bias': 4.803,
     'mlstm_norm_g': 38.786}
    for name, (base, spread) in spreads.items():
        noise = np.random.default_rng([zlib.crc32(name.encode()), seed]).standard_normal(out[name].shape)
        drawn = base * np.exp(spread * noise) if base else spread * noise
        out[name] = __import__('jax').numpy.asarray(drawn.astype(out[name].dtype))
    for name, factor in factors.items():
        out[name] = (out[name] * factor).astype(out[name].dtype)
    return out
```

```python
from contextlib import ExitStack
import math

import numpy as np

import concourse.bass as bass
from concourse import mybir

ALU = mybir.AluOpType
ACT = mybir.ActivationFunctionType
AX = mybir.AxisListType
F32 = mybir.dt.float32
F32R = mybir.dt.float32r

P = 128
KB = 1024
SEQ = 512
D = 1024
DC = D // P
TT = SEQ // P
D_FF = 4 * D
NBUCK = 32
MAXDIST = 2048
GROUPS = ((128, 1), (512, 4), (2048, 16))
NG = 3
AH = 4
DH = 128
MLH = 8
DK = 64
DV = 128
TAPS = 4
EPS = 1e-6
NEG = -1e30
C_AQ, C_AK, C_AV = 0, NG * AH * DH, 2 * NG * AH * DH
C_MQ = 3 * NG * AH * DH
C_MV = C_MQ + 2 * MLH * DK
C_MO = C_MV + MLH * DV
C_MI = C_MO + MLH * DV
C_MF = C_MI + MLH
C_GA = C_MF + MLH
C_GB = C_GA + D
TW = (3 * P - 1, 2 * P - 1, 2 * P - 1)
TO = (0, TW[0], TW[0] + TW[1])
TSUM = sum(TW)

U_CONV = 0
U_MO = 8
U_MV = 16
U_ATT = 24
U_YML = 60
U_YATT = 76
U_OUT = 92
U_FF = 100
N_UNITS = 164
RING = 4


def bucket_of(dist):
    exact = NBUCK // 2
    d = np.maximum(dist, exact).astype(np.float32)
    large = exact + (np.log(d / np.float32(exact)) / np.float32(math.log(MAXDIST / exact))
                     * np.float32(NBUCK - exact)).astype(np.int32)
    return np.where(dist < exact, dist, np.minimum(large, NBUCK - 1))


def bucket_one_hot():
    m = np.zeros((NBUCK + 1, TSUM), np.float32)
    for g, (window, dil) in enumerate(GROUPS):
        for x in range(TW[g]):
            delta = (2 * P - 1 if g == 0 else P - 1) - x
            if 0 <= delta <= window // dil:
                m[int(bucket_of(np.array(delta * dil))), TO[g] + x] = 1.0
            else:
                m[NBUCK, TO[g] + x] = NEG
    return m


def block_kernel(nc, x, c, w_ada, b_ada, norm1_g, norm2_g, w_in, b_if, conv_w, conv_b, q_norm_g, k_norm_g,
                 rel_bias, mlstm_norm_g, w_att_out, w_ml_out, w_out, w_ff1, w_ff2, one_hot, out):
    base = nc.sbuf_base + (-nc.sbuf_base) % 64
    limit = nc.sbuf_usable_end

    def at(name, kb, shape, dt=F32):
        off = base + int(kb * KB)
        assert off + 4 * int(np.prod(shape[1:])) <= limit, name
        return nc.alloc_sbuf_tensor_at(name, shape, dt, offset=off)

    xT = at("xT", 0, [P, DC, SEQ])
    wraw = at("wraw", 16, [P, RING, DC, P])
    whi = at("whi", 32, [P, RING, DC, P], F32R)
    wlo = at("wlo", 48, [P, RING, DC, P], F32R)
    uhi = at("uhi", 64, [P, DC, SEQ], F32R)
    ulo = at("ulo", 80, [P, DC, SEQ], F32R)
    hhi = at("hhi", 96, [P, DC, SEQ], F32R)
    hlo = at("hlo", 112, [P, DC, SEQ], F32R)
    ada1 = at("ada1", 96, [P, 2 * D])
    ada2 = at("ada2", 104, [P, 4 * D])
    vrows = at("vrows", 120, [P, P])
    rows = at("rows", 120.5, [P, 3, SEQ])
    onehot = at("onehot", 160, [NBUCK + 1, TSUM])
    relb = at("relb", 164, [NBUCK + 1, NG * AH])
    xtok = at("xtok", 128, [P, TT, D])
    ifraw = at("ifraw", 144, [P, DC, P])
    ifhi = at("ifhi", 148, [P, DC, P], F32R)
    iflo = at("iflo", 152, [P, DC, P], F32R)
    stage = at("stage", 144, [P, AH, 4 * P])
    n1sq = at("n1sq", 184, [P, 2, SEQ])
    n1t = at("n1t", 188, [P, 2, SEQ])
    n1rs = at("n1rs", 192, [P, SEQ])
    adabuf = at("adabuf", 160, [P, 3, 2 * D])
    mqk = at("mqk", 128, [P, DC, SEQ])
    mo = at("mo", 144, [P, DC, SEQ])
    cpad = at("cpad", 184, [P, 2, SEQ + TAPS - 1])
    cacc = at("cacc", 188.0625, [P, 2, SEQ])
    csig = at("csig", 192.0625, [P, SEQ])
    frow = at("frow", 156, [NG * AH, TSUM])
    negM = at("negM", 194.125, [MLH, SEQ])
    EW = (0, 512, 896, 1152, 1280)
    expd = at("expd", 160, [P, TT, SEQ])
    dcl = at("dcl", 168, [P, TT, P])
    wts = at("wts", 170, [P, 2, EW[4]])
    vext = at("vext", 180, [P, 2, TT, DV + 1])
    mvT = at("mvT", 184.125, [P, SEQ])
    hn = at("hn", 186.125, [P, TT, DV])
    hg = at("hg", 188.125, [P, SEQ])
    qf = at("qf", 128, [P, 2, SEQ])
    sqb = at("sqb", 132, [P, 2, SEQ])
    rsb = at("rsb", 136, [P, 2, SEQ])
    qn = at("qn", 140, [P, SEQ])
    kn = at("kn", 142, [P, SEQ])
    outT = at("outT", 144, [P, NG * AH, SEQ])
    vTp = at("vTp", 168, [P, SEQ])
    vtok = at("vtok", 170, [P, 2, TT, DH])
    sbias = at("sbias", 174, [P, TT, 2 * P])
    prob = at("prob", 178, [P, TT, 2 * P])
    probT = at("probT", 182, [P, 7, P])
    bias0 = at("bias0", 196.125, [P, AH, 2 * P])
    bias1 = at("bias1", 200.125, [P, AH, P])
    bias2 = at("bias2", 202.125, [P, AH, P])
    ahi = at("ahi", 128, [P, AH, SEQ], F32R)
    alo = at("alo", 136, [P, AH, SEQ], F32R)
    mrow = at("mrow", 168, [AH, NG, SEQ])
    lrow = at("lrow", 174, [AH, NG, SEQ])
    mtop = at("mtop", 180, [AH, SEQ])
    mrec = at("mrec", 182, [AH, SEQ])
    mtmp = at("mtmp", 174, [P, 3, SEQ])
    gsig = at("gsig", 186, [P, SEQ])
    yml = at("yml", 188, [P, DC, SEQ])
    yhi = at("yhi", 144, [P, DC, SEQ], F32R)
    ylo = at("ylo", 160, [P, DC, SEQ], F32R)
    ybuf = at("ybuf", 176, [P, 2, SEQ])
    sq2 = at("sq2", 128, [P, 2, SEQ])
    rs2 = at("rs2", 132, [P, SEQ])
    n2t = at("n2t", 134, [P, 2, SEQ])
    rbuf = at("rbuf", 138, [P, 2, SEQ])
    r2buf = at("r2buf", 142, [P, SEQ])
    obuf = at("obuf", 144, [P, 2, TT, P])
    CO = 204.25
    ident = at("ident", CO, [P, P])
    ones = at("ones", CO + 0.5, [P, P])
    cols = at("cols", CO + 1, [P, P])
    adac = at("adac", CO + 1.5, [P, 48])
    small = at("small", CO + 1.75, [P, 112])
    eT = at("eT", CO + 2.25, [P, 2, TT, MLH])
    stats = at("stats", CO + 2.5, [P, 2, NG, TT, AH])
    colb = at("colb", CO + 2.875, [P, 32])
    flip = at("flip", CO + 3, [P, P])

    sc = small[:, 0:8]
    scE = small[:, 8:16]
    a1, sh1 = small[:, 16:24], small[:, 24:32]
    a2, sh2 = small[:, 32:40], small[:, 40:48]
    gate1, gate2 = small[:, 48:56], small[:, 56:64]
    qgs = small[:, 64:65]
    emT = small[:, 72:104].rearrange("p (t h) -> p t h", t=TT)
    bif = small[:, 104:105]
    mx = small[:, 105:109]
    nq, nd, nr, ss, nv = (colb[:, 4 * i:4 * i + 4] for i in range(5))
    nf = colb[:, 20:24]

    K_C, K_BADA, K_N1, K_N2, K_CW, K_CB, K_QG, K_KG, K_MG = 0, 8, 56, 64, 72, 104, 112, 113, 114
    N_VEC = 122

    ps = nc.alloc_psum_tensor("ps", [P, 8, 512], F32)
    f_dram = nc.dram_tensor("toeplitz_rows", (NG * AH, TSUM), F32)

    with ExitStack() as ctx:
        def sem(name):
            return ctx.enter_context(nc.semaphore(name))

        vec_in, x_in, oh_in, if_in, bif_in = sem("vec_in"), sem("x_in"), sem("oh_in"), sem("if_in"), sem("bif_in")
        ada_in = [sem(f"ada_in{i}") for i in range(3)]
        w_in_sem = [sem(f"w_landed{i}") for i in range(RING)]
        frow_out, stage_in = sem("frow_out"), sem("stage_in")
        out_done = [sem(f"out{i}_stored") for i in range(2)]
        consts, identity_ok, if_zero = sem("consts_set"), sem("identity_made"), sem("if_zeroed")
        w_hi, w_lo, unit_done = sem("w_hi_ready"), sem("w_lo_ready"), sem("unit_done")
        bank_read = [sem(f"bank{i}_read") for i in range(2)]
        vec_t, vec_c = sem("vec_transposed"), sem("vec_columns")
        silu_e, silu_c = sem("silu_exp"), sem("silu_ready")
        ada_acc, ada_t, ada_ok = sem("ada_accumulated"), sem("ada_transposed"), sem("ada_columns")
        x_t, x_sq, x_ss, x_rs = sem("x_transposed"), sem("x_squared"), sem("x_sumsq"), sem("x_rstd")
        u_f, u_hi, u_lo = sem("u_ready"), sem("u_hi"), sem("u_lo")
        if_hi, if_lo, if_mm = sem("if_hi"), sem("if_lo"), sem("if_product")
        lf_a, lf_b, rows_ok, eT_t, eT_ok = (sem("lf_abs"), sem("lf_log"), sem("rows_ready"), sem("e_transposed"),
                                            sem("e_columns"))
        em_ok = sem("exp_neg_m")
        fr_mm, fr_sb, flip_mm, bias_ok = sem("frow_product"), sem("frow_sbuf"), sem("bias_flipped"), sem("bias_ready")
        cv_acc, cv_sig, mqk_ok, mo_ok = sem("conv_sum"), sem("conv_sigmoid"), sem("mqk_ready"), sem("mo_ready")
        mv_t, vx_ok = sem("mv_transposed"), sem("v_ready")
        bc_mm, dc_ok, ex_dg, ex_ok, ex_msk = (sem("negM_broadcast"), sem("decay_clamped"), sem("decay_diagonal"),
                                               sem("decay_exp"), sem("decay_masked"))
        ms_mm, wt_ok, num_mm = sem("mscores"), sem("mweights"), sem("mnumerator")
        nq_ok, nsq, nrr, nrs, hn_ok = sem("nq_copied"), sem("num_squares"), sem("num_var"), sem("num_rstd"), sem("hn_ready")
        ht_mm, hg_ok, h_hi, h_lo = sem("h_transposed"), sem("h_gated"), sem("h_hi"), sem("h_lo")
        qk_ss, qk_rs, qk_n = sem("qk_sumsq"), sem("qk_rstd"), sem("qk_normed")
        vt_mm, vt_ok = sem("v_transposed"), sem("v_tokens")
        sc_mm, mx_ok, pr_ok = sem("scores"), sem("row_max"), sem("probs")
        pt_mm, pt_ok, pv_mm, o_ok = sem("probs_transposed"), sem("probsT_ready"), sem("pv"), sem("o_copied")
        st_mm, st_ok, md_ok, me_ok, mw_ok = (sem("stats_turned"), sem("stats_rows"), sem("merge_diff"),
                                             sem("merge_exp"), sem("merge_weights"))
        mb_mm, mb_rd, att_f, a_hi, a_lo = (sem("weights_broadcast"), sem("broadcast_read"), sem("att_ready"),
                                           sem("att_hi"), sem("att_lo"))
        y_ok, y_hi, y_lo = sem("y_ready"), sem("y_hi"), sem("y_lo")
        s2_ok, s2_mm, r2_ok = sem("x1_squared"), sem("x1_sumsq"), sem("x1_rstd")
        v_f, v_hi, v_lo = sem("u2_ready"), sem("u2_hi"), sem("u2_lo")
        f_hi, f_lo = sem("hdn_hi"), sem("hdn_lo")
        xo_mm, xo_ok = sem("x2_transposed"), sem("out_tile")
        dve_step, act_step, pool_step = sem("dve_step"), sem("act_step"), sem("pool_step")

        w_in2 = w_in[0]

        def slab(u):
            def cols_of(w, c0, kc=DC, r0=0):
                return w[r0:r0 + kc * P, c0:c0 + P].rearrange("(k p) n -> p k n", p=P), kc
            if u < U_MO:
                return cols_of(w_in2, C_MQ + u * P)
            if u < U_MV:
                return cols_of(w_in2, C_MO + (u - U_MO) * P)
            if u < U_ATT:
                return cols_of(w_in2, C_MV + (u - U_MV) * P)
            if u < U_YML:
                j, part = divmod(u - U_ATT, 3)
                h, g = divmod(j, NG)
                return cols_of(w_in2, (C_AQ, C_AK, C_AV)[part] + (g * AH + h) * DH)
            if u < U_YATT:
                n, part = divmod(u - U_YML, 2)
                return cols_of(w_ml_out[0], n * P) if part else cols_of(w_in2, C_GB + n * P)
            if u < U_OUT:
                n, part = divmod(u - U_YATT, 2)
                return cols_of(w_att_out[0], n * P, AH) if part else cols_of(w_in2, C_GA + n * P)
            if u < U_FF:
                return cols_of(w_out[0], (u - U_OUT) * P)
            q, j = divmod(u - U_FF, 16)
            if j < 8:
                return cols_of(w_ff1[0], (q * 8 + j) * P)
            return cols_of(w_ff2[0], (j - 8) * P, DC, q * D)

        def kchunks(u):
            return AH if U_YATT <= u < U_OUT and (u - U_YATT) % 2 else DC

        def taken(eng, u):
            eng.wait_ge(bank_read[u % 2], u // 2 + 1)

        diagonal = bass.AP(tensor=expd[:].tensor, offset=expd[:].offset, ap=[expd[:].ap[0], [SEQ + P, TT], [1, P]])

        block = ctx.enter_context(nc.Block())

        @block.sync
        def _(sp):
            def rows_of(a, r0, n):
                sp.dma_start(vrows[r0:r0 + n, :], a).then_inc(vec_in, 16)
            rows_of(c.rearrange("b (a p) -> (b a) p", p=P), K_C, DC)
            rows_of(b_ada.rearrange("b (a p) -> (b a) p", p=P), K_BADA, 48)
            rows_of(norm1_g.rearrange("b (a p) -> (b a) p", p=P), K_N1, DC)
            rows_of(norm2_g.rearrange("b (a p) -> (b a) p", p=P), K_N2, DC)
            rows_of(conv_w[0].rearrange("t (a p) -> (t a) p", p=P), K_CW, TAPS * DC)
            rows_of(conv_b.rearrange("b (a p) -> (b a) p", p=P), K_CB, DC)
            rows_of(q_norm_g, K_QG, 1)
            rows_of(k_norm_g, K_KG, 1)
            rows_of(mlstm_norm_g.rearrange("b (a p) -> (b a) p", p=P), K_MG, DC)
            sp.dma_start(xtok[:], x[0].rearrange("(t p) d -> p t d", p=P)).then_inc(x_in, 16)
            sp.dma_start(bif[0:MLH, :], b_if[0, 0:1, :].rearrange("a h -> h a")).then_inc(bif_in, 16)
            sp.dma_start(bif[32:32 + MLH, :], b_if[0, 1:2, :].rearrange("a h -> h a")).then_inc(bif_in, 16)
            sp.wait_ge(if_zero, 2)
            sp.dma_start(onehot[:], one_hot).then_inc(oh_in, 16)
            sp.dma_start(relb[0:NBUCK, :], rel_bias).then_inc(oh_in, 16)

            def ada(i):
                if i >= 3:
                    sp.wait_ge(ada_acc, i - 2)
                else:
                    sp.wait_ge(fr_sb, 1)
                k, c0 = (i, 0) if i < 8 else ((i - 8) // 2, 2 * D * (1 + (i - 8) % 2))
                sp.dma_start(adabuf[:, i % 3, :], w_ada[0, k * P:(k + 1) * P, c0:c0 + 2 * D]).then_inc(
                    ada_in[i % 3], 16)

            def weights(u):
                if u >= RING:
                    sp.wait_ge(w_lo, u - RING + 1)
                src, kc = slab(u)
                sp.dma_start(wraw[:, u % RING, 0:kc, :], src).then_inc(w_in_sem[u % RING], 16)

            for i in range(8):
                ada(i)
                if i == 2:
                    sp.dma_start(ifraw[:, :, 0:MLH],
                                 w_in2[:, C_MI:C_MI + MLH].rearrange("(k p) n -> p k n", p=P)).then_inc(if_in, 16)
                    sp.dma_start(ifraw[:, :, 32:32 + MLH],
                                 w_in2[:, C_MF:C_MF + MLH].rearrange("(k p) n -> p k n", p=P)).then_inc(if_in, 16)
            for u in range(RING):
                weights(u)
            for u in range(RING, N_UNITS):
                if u - RING < 16:
                    ada(8 + u - RING)
                weights(u)
                if u == RING + 4:
                    sp.wait_ge(fr_sb, 1)
                    sp.dma_start(f_dram.ap(), frow[:]).then_inc(frow_out, 16)
                    sp.wait_ge(frow_out, 16)
                    sp.wait_ge(if_mm, 1)
                    for g, (w, c0) in enumerate(((2 * P, 0), (P, 2 * P), (P, 3 * P))):
                        src = bass.AP(tensor=f_dram.ap().tensor, offset=g * AH * TSUM + TO[g],
                                      ap=[[1, P], [TSUM, AH], [1, w]])
                        sp.dma_start(stage[:, :, c0:c0 + w], src).then_inc(stage_in, 16)
            out_tok = out[0].rearrange("(t p) d -> p t d", p=P)
            for n in range(DC):
                sp.wait_ge(xo_ok, n + 1)
                sp.dma_start(out_tok[:, :, n * P:(n + 1) * P], obuf[:, n % 2]).then_inc(out_done[n % 2], 16)
            for b in range(2):
                sp.wait_ge(out_done[b], 16 * DC // 2)

        @block.gpsimd
        def _(pool):
            nc.gpsimd.memset(ident[:], 0.0).then_inc(pool_step, 1)
            nc.gpsimd.memset(flip[:], 0.0).then_inc(pool_step, 1)
            pool.wait_ge(pool_step, 2)
            nc.gpsimd.affine_select(out=ident[:], in_=ident[:], compare_op=ALU.not_equal, fill=1.0, base=0,
                                    pattern=[[1, P]], channel_multiplier=-1).then_inc(identity_ok, 1)
            nc.gpsimd.affine_select(out=flip[:], in_=flip[:], compare_op=ALU.not_equal, fill=1.0, base=1 - P,
                                    pattern=[[1, P]], channel_multiplier=1).then_inc(identity_ok, 1)
            pool.wait_ge(if_hi, 1)
            nc.gpsimd.tensor_tensor(iflo[:], ifraw[:], ifhi[:].bitcast(F32), ALU.subtract).then_inc(if_lo, 1)

            def mask(h):
                pool.wait_ge(ex_dg, h + 1)
                nc.gpsimd.affine_select(out=diagonal, in_=diagonal, compare_op=ALU.is_ge, fill=0.0, base=0,
                                        pattern=[[0, TT], [1, P]], channel_multiplier=-1).then_inc(ex_msk, 1)

            for u in range(N_UNITS):
                pool.wait_ge(w_hi, u + 1)
                kc, s = kchunks(u), u % RING
                nc.gpsimd.tensor_tensor(wlo[:, s, 0:kc, :], wraw[:, s, 0:kc, :], whi[:, s, 0:kc, :].bitcast(F32),
                                        ALU.subtract).then_inc(w_lo, 1)
                if U_MV + 4 <= u < U_MV + 4 + MLH:
                    mask(u - U_MV - 4)

        @block.scalar
        def _(act):
            count = [0]

            def link(ins):
                count[0] += 1
                ins.then_inc(act_step, 1)
                act.wait_ge(act_step, count[0])

            def high(u):
                act.wait_ge(w_in_sem[u % RING], 16 * (u // RING + 1))
                if u >= RING:
                    act.wait_ge(unit_done, u - RING + 1)
                kc, s = kchunks(u), u % RING
                nc.scalar.copy(whi[:, s, 0:kc, :], wraw[:, s, 0:kc, :]).then_inc(w_hi, 1)

            G = lambda u: ps[:, u % 2, :]

            act.wait_ge(vec_c, 1)
            nc.scalar.activation(scE, cols[:, K_C:K_C + DC], ACT.Exp, scale=-1.0).then_inc(silu_e, 1)
            for d in range(DC):
                act.wait_ge(x_t, d + 1)
                nc.scalar.copy(xT[:, d, :], ps[:, d % 4, :])
                if d >= 2:
                    act.wait_ge(x_ss, d - 1)
                nc.scalar.activation(n1sq[:, d % 2, :], ps[:, d % 4, :], ACT.Square).then_inc(x_sq, 1)
            act.wait_ge(if_in, 32)
            nc.scalar.copy(ifhi[:], ifraw[:]).then_inc(if_hi, 1)
            act.wait_ge(x_ss, DC)
            act.wait_ge(consts, 3)
            link(nc.scalar.activation(n1rs[:], ps[:, 6, :], ACT.Ln, scale=1.0 / D, bias=small[:, 109:110]))
            nc.scalar.activation(n1rs[:], n1rs[:], ACT.Exp, scale=-0.5).then_inc(x_rs, 1)
            for u in range(RING):
                high(u)
            for d in range(DC):
                act.wait_ge(u_f, d + 1)
                nc.scalar.copy(uhi[:, d, :], n1t[:, d % 2, :]).then_inc(u_hi, 1)
            act.wait_ge(lf_a, 1)
            link(nc.scalar.activation(rows[32:40, 1, :], rows[32:40, 1, :], ACT.Exp, scale=-1.0))
            nc.scalar.activation(rows[32:40, 1, :], rows[32:40, 1, :], ACT.Ln, bias=1.0).then_inc(lf_b, 1)

            def after(u):
                act.wait_ge(unit_done, u + 1)
                if u + RING < N_UNITS:
                    high(u + RING)

            for u in range(U_CONV, U_MO):
                after(u)
                act.wait_ge(cv_acc, u + 1)
                if u >= 1:
                    act.wait_ge(mqk_ok, u)
                nc.scalar.activation(csig[:], cacc[:, u % 2, :], ACT.Sigmoid).then_inc(cv_sig, 1)
            for u in range(U_MO, U_MV):
                after(u)
                if u == U_MO:
                    act.wait_ge(bias_ok, 1)
                nc.scalar.activation(mo[:, u - U_MO, :], G(u), ACT.Sigmoid).then_inc(bank_read[u % 2], 1)

            act.wait_ge(eT_ok, 1)
            nc.scalar.activation(emT, eT[:, 1], ACT.Exp).then_inc(em_ok, 1)

            def m_exp(h):
                if h >= 1:
                    act.wait_ge(wt_ok, 4 * h)
                act.wait_ge(dc_ok, h + 1)
                nc.scalar.activation(diagonal, dcl[:], ACT.Exp).then_inc(ex_dg, 1)
                for j in range(TT - 1):
                    last = nc.scalar.activation(expd[:, j, (j + 1) * P:], ps[:, 5, (j + 1) * P:SEQ], ACT.Exp,
                                                bias=eT[:, 0, j, h:h + 1])
                last.then_inc(ex_ok, 1)

            def m_high(h):
                act.wait_ge(hg_ok, h + 1)
                nc.scalar.copy(hhi[:, h, :], hg[:]).then_inc(h_hi, 1)

            def m_norm(h):
                act.wait_ge(nq_ok, h + 1)
                for i in range(TT):
                    last = nc.scalar.activation(hn[:, i, :], ps[:, 6 + i // 2, (i % 2) * 256:(i % 2) * 256 + DV],
                                                ACT.Square, accum_out=ss[:, i:i + 1])
                last.then_inc(nsq, 1)
                act.wait_ge(nrr, h + 1)
                link(nc.scalar.activation(nv, nv, ACT.Ln, scale=1.0 / DV, bias=small[:, 109:110]))
                nc.scalar.activation(nv, nv, ACT.Exp, scale=-0.5).then_inc(nrs, 1)

            for h in range(MLH):
                u = U_MV + h
                after(u)
                if h >= 1:
                    act.wait_ge(mv_t, h)
                nc.scalar.copy(mvT[:], G(u)).then_inc(bank_read[u % 2], 1)
                m_exp(h)
                if h >= 2:
                    m_high(h - 2)
                if h >= 1:
                    m_norm(h - 1)

            def exps(j):
                g = j % NG
                h = j // NG
                act.wait_ge(mx_ok, j + 1)
                for t in range(TT):
                    lo = P if g == 0 and t == 0 else 0
                    w = 2 * P if g == 0 else P
                    last = nc.scalar.activation(prob[:, t, lo:w], sbias[:, t, lo:w], ACT.Exp,
                                                bias=stats[:, 0, g, t, h:h + 1], accum_out=stats[:, 1, g, t, h:h + 1])
                last.then_inc(pr_ok, 1)

            def o_copy(j):
                g, h = j % NG, j // NG
                dil = GROUPS[g][1]
                act.wait_ge(pv_mm, j + 1)
                nc.scalar.copy(outT[:, j, :].rearrange("p (s r) -> p s r", r=dil),
                               ps[:, 7, :].rearrange("p (r s) -> p s r", r=dil)).then_inc(o_ok, 1)

            def rstd(n):
                act.wait_ge(qk_ss, n + 1)
                if n >= 2:
                    act.wait_ge(qk_n, n - 1)
                link(nc.scalar.activation(rsb[:, n % 2, :], ps[:, 6, :], ACT.Ln, scale=1.0 / DH, bias=small[:, 109:110]))
                nc.scalar.activation(rsb[:, n % 2, :], rsb[:, n % 2, :], ACT.Exp, scale=-0.5).then_inc(qk_rs, 1)

            for s in range(36):
                u = U_ATT + s
                j, part = divmod(s, 3)
                after(u)
                if part < 2:
                    n = 2 * j + part
                    if n >= 2:
                        act.wait_ge(qk_n, n - 1)
                        act.wait_ge(qk_ss, n - 1)
                    nc.scalar.copy(qf[:, part, :], G(u))
                    nc.scalar.activation(sqb[:, part, :], G(u), ACT.Square).then_inc(bank_read[u % 2], 1)
                if part == 0:
                    if s == 0:
                        m_high(6)
                        m_norm(7)
                    if j >= 2:
                        o_copy(j - 2)
                    if j >= 1:
                        exps(j - 1)
                if part == 1:
                    if s == 1:
                        m_high(7)
                    rstd(2 * j)
                if part == 2:
                    rstd(2 * j + 1)

            for t in range(16):
                u = U_YML + t
                n, part = divmod(t, 2)
                after(u)
                if t == 0:
                    o_copy(10)
                    exps(11)
                if t == 3:
                    o_copy(11)
                if t == 6:
                    act.wait_ge(md_ok, 1)
                    nc.scalar.activation(mrow[:], mrow[:], ACT.Exp).then_inc(me_ok, 1)
                if part == 0:
                    if n >= 1:
                        taken(act, u - 1)
                    nc.scalar.activation(gsig[:], G(u), ACT.Sigmoid).then_inc(bank_read[u % 2], 1)
                if t >= 9 and t % 2 == 1:
                    h = (t - 9) // 2
                    act.wait_ge(att_f, h + 1)
                    nc.scalar.copy(ahi[:, h, :], mtmp[:, 0, :]).then_inc(a_hi, 1)
            for t in range(16):
                u = U_YATT + t
                n, part = divmod(t, 2)
                after(u)
                if part == 0:
                    taken(act, u - 1)
                    nc.scalar.activation(gsig[:], G(u), ACT.Sigmoid).then_inc(bank_read[u % 2], 1)
                else:
                    act.wait_ge(y_ok, n + 1)
                    nc.scalar.copy(yhi[:, n, :], ybuf[:, n % 2, :]).then_inc(y_hi, 1)
            for n in range(DC):
                after(U_OUT + n)
                taken(act, U_OUT + n)
                if n >= 2:
                    act.wait_ge(s2_mm, n - 1)
                nc.scalar.activation(sq2[:, n % 2, :], xT[:, n, :], ACT.Square).then_inc(s2_ok, 1)
            act.wait_ge(s2_mm, DC)
            link(nc.scalar.activation(rs2[:], ps[:, 6, :], ACT.Ln, scale=1.0 / D, bias=small[:, 109:110]))
            nc.scalar.activation(rs2[:], rs2[:], ACT.Exp, scale=-0.5).then_inc(r2_ok, 1)
            for d in range(DC):
                act.wait_ge(v_f, d + 1)
                nc.scalar.copy(uhi[:, d, :], n2t[:, d % 2, :]).then_inc(v_hi, 1)
            for q in range(4):
                for j in range(8):
                    u = U_FF + 16 * q + j
                    n = 8 * q + j
                    after(u)
                    if n >= 2:
                        act.wait_ge(f_lo, n - 1)
                    nc.scalar.activation(rbuf[:, j % 2, :], G(u), ACT.Relu).then_inc(bank_read[u % 2], 1)
                    taken(act, u)
                    nc.scalar.activation(hhi[:, j, :], rbuf[:, j % 2, :], ACT.Square).then_inc(f_hi, 1)
                for j in range(8):
                    after(U_FF + 16 * q + 8 + j)
                    if q == 3 and j >= 1:
                        n = j - 1
                        act.wait_ge(xo_mm, n + 1)
                        if n >= 2:
                            act.wait_ge(out_done[n % 2], 16 * (n // 2))
                        nc.scalar.copy(obuf[:, n % 2], ps[:, 4 + n % 2, :].rearrange("p (t d) -> p t d", t=TT)).then_inc(
                            xo_ok, 1)
            act.wait_ge(xo_mm, DC)
            act.wait_ge(out_done[1], 16 * (DC // 2 - 1))
            nc.scalar.copy(obuf[:, 1], ps[:, 5, :].rearrange("p (t d) -> p t d", t=TT)).then_inc(xo_ok, 1)

        @block.vector
        def _(dve):
            count = [0]
            V = nc.vector

            def link(ins):
                count[0] += 1
                ins.then_inc(dve_step, 1)
                dve.wait_ge(dve_step, count[0])

            G = lambda u: ps[:, u % 2, :]

            V.memset(relb[32:33, :], 1.0).then_inc(if_zero, 1)
            V.memset(ifraw[:], 0.0).then_inc(if_zero, 1)
            V.memset(ones[:], 1.0).then_inc(consts, 1)
            V.memset(small[:, 109:110], EPS).then_inc(consts, 1)
            V.memset(bias2[:], NEG).then_inc(consts, 1)
            dve.wait_ge(vec_t, 1)
            V.tensor_copy(cols[:, 0:N_VEC], ps[:, 4, 0:N_VEC]).then_inc(vec_c, 1)
            dve.wait_ge(vec_c, 1)
            V.tensor_scalar(qgs, cols[:, K_QG:K_QG + 1], DH ** -0.5, None, ALU.mult)
            dve.wait_ge(silu_e, 1)
            link(V.tensor_scalar(scE, scE, 1.0, None, ALU.add))
            link(V.reciprocal(scE, scE))
            V.tensor_tensor(sc, cols[:, K_C:K_C + DC], scE, ALU.mult).then_inc(silu_c, 1)
            dve.wait_ge(fr_mm, 1)
            V.tensor_copy(frow[:, 0:512], ps[0:NG * AH, 5, :])
            V.tensor_copy(frow[:, 512:TSUM], ps[0:NG * AH, 7, 0:TSUM - 512]).then_inc(fr_sb, 1)
            dve.wait_ge(silu_c, 1)

            def ada(i):
                dve.wait_ge(ada_in[i % 3], 16 * (i // 3 + 1))
                if i >= 1:
                    dve.wait_ge(ada_acc, i)
                k = i if i < 8 else (i - 8) // 2
                dst = ada1[:] if i < 8 else ada2[:, 2 * D * ((i - 8) % 2):2 * D * ((i - 8) % 2 + 1)]
                if k == 0:
                    V.tensor_scalar(dst, adabuf[:, i % 3, :], sc[:, k:k + 1], None, ALU.mult).then_inc(ada_acc, 1)
                else:
                    V.scalar_tensor_tensor(out=dst, in0=adabuf[:, i % 3, :], scalar=sc[:, k:k + 1], in1=dst,
                                           op0=ALU.mult, op1=ALU.add).then_inc(ada_acc, 1)

            for i in range(8):
                ada(i)
            dve.wait_ge(ada_t, 1)
            link(V.tensor_tensor(adac[:, 0:16], ps[:, 7, 0:16], cols[:, K_BADA:K_BADA + 16], ALU.add))
            V.tensor_copy(sh1, adac[:, 0:8])
            link(V.scalar_tensor_tensor(out=a1, in0=adac[:, 8:16], scalar=1.0, in1=cols[:, K_N1:K_N1 + DC],
                                        op0=ALU.add, op1=ALU.mult))
            dve.wait_ge(x_rs, 1)
            for d in range(DC):
                if d >= 2:
                    dve.wait_ge(u_hi, d - 1)
                    dve.wait_ge(u_lo, d - 1)
                link(V.tensor_tensor(n1t[:, d % 2, :], xT[:, d, :], n1rs[:], ALU.mult))
                V.tensor_scalar(n1t[:, d % 2, :], n1t[:, d % 2, :], a1[:, d:d + 1], sh1[:, d:d + 1], ALU.mult,
                                ALU.add).then_inc(u_f, 1)
                dve.wait_ge(u_f, d + 1)
                dve.wait_ge(u_hi, d + 1)
                V.tensor_tensor(ulo[:, d, :], n1t[:, d % 2, :], uhi[:, d, :].bitcast(F32), ALU.subtract).then_inc(
                    u_lo, 1)
            dve.wait_ge(if_mm, 1)
            dve.wait_ge(bif_in, 32)
            z, az = rows[32:40, 0, :], rows[32:40, 1, :]
            link(V.tensor_scalar(z, ps[32:40, 2, :], bif[32:40, :], None, ALU.add))
            V.scalar_tensor_tensor(out=az, in0=z, scalar=-1.0, in1=z, op0=ALU.mult, op1=ALU.max).then_inc(lf_a, 1)
            link(V.tensor_scalar(rows[0:8, 0, :], ps[0:8, 2, :], bif[0:8, :], None, ALU.add))
            link(V.tensor_scalar(z, z, 0.0, None, ALU.min))
            dve.wait_ge(lf_b, 1)
            link(V.tensor_tensor(rows[0:8, 1, :], z, az, ALU.subtract))
            link(V.memset(rows[0:8, 2, :], 1.0))
            link(V.tensor_tensor_scan(negM[:], rows[0:8, 2, :], rows[0:8, 1, :], 0.0, ALU.mult, ALU.add))
            link(V.tensor_tensor(rows[0:8, 0, :], rows[0:8, 0, :], negM[:], ALU.subtract))
            link(V.tensor_tensor_scan(rows[0:8, 1, :], rows[0:8, 2, :], rows[0:8, 0, :], 0.0, ALU.mult, ALU.max))
            link(V.scalar_tensor_tensor(out=rows[0:8, 2, :], in0=negM[:], scalar=-1.0, in1=rows[0:8, 1, :],
                                        op0=ALU.mult, op1=ALU.subtract))
            V.tensor_scalar(negM[:], rows[0:8, 1, :], -1.0, None, ALU.mult).then_inc(rows_ok, 1)
            link(V.memset(cpad[:, :, 0:TAPS - 1], 0.0))

            def silu_mul(u):
                dve.wait_ge(cv_sig, u + 1)
                V.scalar_tensor_tensor(out=mqk[:, u, :], in0=cacc[:, u % 2, :], scalar=1.0 if u < 4 else DK ** -0.5,
                                       in1=csig[:], op0=ALU.mult, op1=ALU.mult).then_inc(mqk_ok, 1)

            for u in range(U_CONV, U_MO):
                dve.wait_ge(unit_done, u + 1)
                V.tensor_copy(cpad[:, u % 2, TAPS - 1:], G(u)).then_inc(bank_read[u % 2], 1)
                taken(dve, u)
                cw = lambda t: cols[:, K_CW + DC * t + u:K_CW + DC * t + u + 1]
                link(V.tensor_scalar(cacc[:, u % 2, :], cpad[:, u % 2, TAPS - 1:], cw(TAPS - 1),
                                     cols[:, K_CB + u:K_CB + u + 1], ALU.mult, ALU.add))
                for t in range(TAPS - 1):
                    ins = V.scalar_tensor_tensor(out=cacc[:, u % 2, :], in0=cpad[:, u % 2, t:t + SEQ], scalar=cw(t),
                                                 in1=cacc[:, u % 2, :], op0=ALU.mult, op1=ALU.add)
                    if t < TAPS - 2:
                        link(ins)
                ins.then_inc(cv_acc, 1)
                if u >= 1:
                    silu_mul(u - 1)
                ada(8 + u)
                if u == 1:
                    dve.wait_ge(eT_t, 1)
                    V.tensor_copy(eT[:], ps[:, 3, 0:64].rearrange("p (a t h) -> p a t h", a=2, t=TT)).then_inc(eT_ok, 1)
            silu_mul(7)
            for u in range(U_MO, U_MV):
                if u == U_MO:
                    dve.wait_ge(flip_mm, 1)
                    V.tensor_copy(bias0[:, 0:2], ps[:, 3, :].rearrange("p (h w) -> p h w", h=2))
                    V.tensor_copy(bias0[:, 2:4], ps[:, 4, :].rearrange("p (h w) -> p h w", h=2))
                    V.tensor_copy(bias1[:], ps[:, 5, :].rearrange("p (h w) -> p h w", h=AH))
                    for b in range(4):
                        r = slice(32 * b, 32 * b + 32)
                        last = V.tensor_copy(bias2[r, :, r], ps[r, 6, :].rearrange("p (h w) -> p h w", h=AH)[:, :, r])
                    last.then_inc(bias_ok, 1)
                ada(8 + u)
            dve.wait_ge(ada_t, 2)
            link(V.tensor_tensor(adac[:, 16:48], ps[:, 7, 16:48], cols[:, K_BADA + 16:K_BADA + 48], ALU.add))
            V.tensor_copy(gate1, adac[:, 16:24])
            V.tensor_copy(sh2, adac[:, 24:32])
            V.scalar_tensor_tensor(out=a2, in0=adac[:, 32:40], scalar=1.0, in1=cols[:, K_N2:K_N2 + DC],
                                   op0=ALU.add, op1=ALU.mult)
            V.tensor_copy(gate2, adac[:, 40:48])
            V.memset(vext[:, :, :, DV:DV + 1], 1.0).then_inc(ada_ok, 1)

            def m_gate(h):
                dve.wait_ge(ht_mm, h + 1)
                if h >= 1:
                    dve.wait_ge(h_hi, h)
                    dve.wait_ge(h_lo, h)
                V.scalar_tensor_tensor(out=hg[:], in0=ps[:, 4, :], scalar=cols[:, K_MG + h:K_MG + h + 1],
                                       in1=mo[:, h, :], op0=ALU.mult, op1=ALU.mult).then_inc(hg_ok, 1)

            def m_low(h):
                dve.wait_ge(hg_ok, h + 1)
                dve.wait_ge(h_hi, h + 1)
                V.tensor_tensor(hlo[:, h, :], hg[:], hhi[:, h, :].bitcast(F32), ALU.subtract).then_inc(h_lo, 1)

            def m_clamp(h):
                dve.wait_ge(bc_mm, h + 1)
                if h >= 1:
                    dve.wait_ge(ex_dg, h)
                for j in range(TT):
                    last = V.tensor_scalar(dcl[:, j, :], ps[:, 5, j * P:(j + 1) * P], eT[:, 0, j, h:h + 1], 0.0,
                                           ALU.add, ALU.min)
                last.then_inc(dc_ok, 1)

            def m_weights(h, j):
                bank, c0 = ((2, 0), (3, 0), (2, 0), (3, 384))[j]
                w = SEQ - j * P
                dve.wait_ge(ms_mm, 4 * h + (1, 3, 4, 3)[j])
                dve.wait_ge(ex_msk, h + 1)
                dve.wait_ge(ex_ok, h + 1)
                if h >= 2:
                    dve.wait_ge(num_mm, h - 1)
                V.tensor_tensor(wts[:, h % 2, EW[j]:EW[j + 1]], ps[:, bank, c0:c0 + w],
                                expd[:, j, j * P:], ALU.mult).then_inc(wt_ok, 1)

            def m_vext(h):
                dve.wait_ge(mv_t, h + 1)
                if h >= 2:
                    dve.wait_ge(num_mm, h - 1)
                V.tensor_copy(vext[:, h % 2, :, 0:DV], ps[:, 4, :].rearrange("p (t d) -> p t d", t=TT)).then_inc(vx_ok, 1)

            num = ps[:, 6:8, :].rearrange("p b (i w) -> p (b i) w", w=256)

            def m_norm(h):
                dve.wait_ge(num_mm, h + 1)
                V.tensor_copy(nq, num[:, :, DV]).then_inc(nq_ok, 1)
                dve.wait_ge(nq_ok, h + 1)
                link(V.scalar_tensor_tensor(out=nd, in0=nq, scalar=-1.0, in1=nq, op0=ALU.mult, op1=ALU.max))
                dve.wait_ge(em_ok, 1)
                link(V.tensor_tensor(nd, nd, emT[:, :, h], ALU.max))
                link(V.reciprocal(nr, nd))
                link(V.tensor_tensor(nd, nr, nr, ALU.mult))
                dve.wait_ge(nsq, h + 1)
                V.tensor_tensor(nv, ss, nd, ALU.mult).then_inc(nrr, 1)
                dve.wait_ge(nrs, h + 1)
                link(V.tensor_tensor(nf, nr, nv, ALU.mult))
                V.tensor_tensor(hn[:], num[:, :, 0:DV], nf.unsqueeze(2).to_broadcast([P, TT, DV]), ALU.mult).then_inc(
                    hn_ok, 1)

            for h in range(MLH):
                if h >= 2:
                    m_gate(h - 2)
                m_clamp(h)
                m_weights(h, 0)
                m_weights(h, 1)
                m_weights(h, 3)
                m_vext(h)
                m_weights(h, 2)
                if h >= 2:
                    m_low(h - 2)
                if h >= 1:
                    m_norm(h - 1)

            def scores(j):
                g, h = j % NG, j // NG
                dve.wait_ge(sc_mm, j + 1)
                if j >= 1:
                    dve.wait_ge(pr_ok, j)
                if g == 0:
                    S = ps[:, 2:4, :].rearrange("p b (i w) -> p (b i) w", w=2 * P)
                    V.tensor_tensor(sbias[:, 0, P:], S[:, 0, P:], bias0[:, h, P:], ALU.add)
                    link(V.tensor_tensor(sbias[:, 1:], S[:, 1:], bias0[:, h:h + 1, :].to_broadcast([P, 3, 2 * P]),
                                         ALU.add))
                    V.tensor_reduce(mx[:, 0:1], sbias[:, 0, P:], AX.X, ALU.max)
                    link(V.tensor_reduce(mx[:, 1:4], sbias[:, 1:], AX.X, ALU.max))
                else:
                    S = ps[:, 2, :].rearrange("p (i w) -> p i w", w=P)
                    b = (bias1 if g == 1 else bias2)[:, h:h + 1, :]
                    link(V.tensor_tensor(sbias[:, :, 0:P], S, b.to_broadcast([P, TT, P]), ALU.add))
                    link(V.tensor_reduce(mx, sbias[:, :, 0:P], AX.X, ALU.max))
                V.tensor_scalar(stats[:, 0, g, :, h], mx, -1.0, None, ALU.mult).then_inc(mx_ok, 1)

            def normed(n):
                j, part = divmod(n, 2)
                dil = GROUPS[j % NG][1]
                dve.wait_ge(qk_rs, n + 1)
                if j >= 1:
                    dve.wait_ge(sc_mm, j)
                dst, gain = ((qn, qgs), (kn, cols[:, K_KG:K_KG + 1]))[part]
                view = lambda a: a.rearrange("p (s r) -> p s r", r=dil)
                V.scalar_tensor_tensor(out=dst[:].rearrange("p (r s) -> p s r", r=dil), in0=view(qf[:, part, :]),
                                       scalar=gain, in1=view(rsb[:, part, :]), op0=ALU.mult, op1=ALU.mult).then_inc(
                    qk_n, 1)

            def v_copy(j):
                u = U_ATT + 3 * j + 2
                dil = GROUPS[j % NG][1]
                dve.wait_ge(unit_done, u + 1)
                if j >= 1:
                    dve.wait_ge(vt_mm, j)
                V.tensor_copy(vTp[:].rearrange("p (r s) -> p s r", r=dil),
                              G(u).rearrange("p (s r) -> p s r", r=dil)).then_inc(bank_read[u % 2], 1)

            def v_tok(j):
                dve.wait_ge(vt_mm, j + 1)
                if j >= 2:
                    dve.wait_ge(pv_mm, j - 1)
                V.tensor_copy(vtok[:, j % 2], ps[:, 4, :].rearrange("p (t d) -> p t d", t=TT)).then_inc(vt_ok, 1)

            def p_copy(j):
                n = 7 if j % NG == 0 else 4
                dve.wait_ge(pt_mm, j + 1)
                if j >= 1:
                    dve.wait_ge(pv_mm, j)
                V.tensor_copy(probT[:, 0:n, :],
                              ps[:, 4:6, :].rearrange("p b (i w) -> p (b i) w", w=P)[:, 0:n]).then_inc(pt_ok, 1)

            for s in range(36):
                j, part = divmod(s, 3)
                if s == 0:
                    m_gate(6)
                    m_low(6)
                    m_norm(7)
                if s == 1:
                    m_gate(7)
                    m_low(7)
                if part == 0 and j >= 1:
                    v_tok(j - 1)
                    scores(j - 1)
                if part == 1:
                    normed(2 * j)
                if part == 2:
                    v_copy(j)
                    normed(2 * j + 1)
                    if j >= 1:
                        p_copy(j - 1)

            def turn(g):
                dil = GROUPS[g][1]
                dve.wait_ge(st_mm, g + 1)
                for dst, b in ((mrow, 2), (lrow, 3)):
                    last = V.tensor_copy(dst[:, g, :].rearrange("p (s r) -> p s r", r=dil),
                                         ps[0:AH, b, :].rearrange("p (r s) -> p s r", r=dil))
                last.then_inc(st_ok, 1)

            def weigh():
                dve.wait_ge(st_ok, NG)
                link(V.tensor_tensor(mtop[:], mrow[:, 0], mrow[:, 1], ALU.min))
                link(V.tensor_tensor(mtop[:], mtop[:], mrow[:, 2], ALU.min))
                V.tensor_tensor(mrow[:], mtop[:].unsqueeze(1).to_broadcast([AH, NG, SEQ]), mrow[:], ALU.subtract).then_inc(
                    md_ok, 1)
                dve.wait_ge(me_ok, 1)
                link(V.tensor_tensor(lrow[:], lrow[:], mrow[:], ALU.mult))
                link(V.tensor_tensor(mtop[:], lrow[:, 0], lrow[:, 1], ALU.add))
                link(V.tensor_tensor(mtop[:], mtop[:], lrow[:, 2], ALU.add))
                link(V.reciprocal(mrec[:], mtop[:]))
                V.tensor_tensor(mrow[:], mrow[:], mrec[:].unsqueeze(1).to_broadcast([AH, NG, SEQ]), ALU.mult).then_inc(
                    mw_ok, 1)

            def merge(h):
                dve.wait_ge(mw_ok, 1)
                dve.wait_ge(mb_mm, h + 1)
                if h >= 1:
                    dve.wait_ge(a_hi, h)
                    dve.wait_ge(a_lo, h)
                else:
                    dve.wait_ge(o_ok, NG * AH)
                for g in range(NG):
                    last = V.tensor_tensor(mtmp[:, g, :], ps[:, 4 + g, :], outT[:, NG * h + g, :], ALU.mult)
                last.then_inc(mb_rd, 1)
                dve.wait_ge(mb_rd, h + 1)
                link(V.tensor_tensor(mtmp[:, 0, :], mtmp[:, 0, :], mtmp[:, 1, :], ALU.add))
                V.tensor_tensor(mtmp[:, 0, :], mtmp[:, 0, :], mtmp[:, 2, :], ALU.add).then_inc(att_f, 1)

            for t in range(16):
                u = U_YML + t
                n, part = divmod(t, 2)
                if part == 1:
                    dve.wait_ge(unit_done, u + 1)
                    taken(dve, u - 1)
                    V.tensor_tensor(yml[:, n, :], G(u), gsig[:], ALU.mult).then_inc(bank_read[u % 2], 1)
                if t == 0:
                    v_tok(11)
                    scores(11)
                if t == 2:
                    p_copy(11)
                if 4 <= t < 7:
                    turn(t - 4)
                if t == 6:
                    weigh()
                if t >= 8 and t % 2 == 0:
                    merge((t - 8) // 2)
                if t >= 9 and t % 2 == 1:
                    h = (t - 9) // 2
                    dve.wait_ge(a_hi, h + 1)
                    V.tensor_tensor(alo[:, h, :], mtmp[:, 0, :], ahi[:, h, :].bitcast(F32), ALU.subtract).then_inc(a_lo, 1)
            for n in range(DC):
                u = U_YATT + 2 * n + 1
                dve.wait_ge(unit_done, u + 1)
                taken(dve, u - 1)
                yb = ybuf[:, n % 2, :]
                if n >= 2:
                    dve.wait_ge(y_hi, n - 1)
                    dve.wait_ge(y_lo, n - 1)
                V.tensor_tensor(yb, G(u), gsig[:], ALU.mult).then_inc(bank_read[u % 2], 1)
                taken(dve, u)
                V.tensor_tensor(yb, yb, yml[:, n, :], ALU.add).then_inc(y_ok, 1)
                dve.wait_ge(y_ok, n + 1)
                dve.wait_ge(y_hi, n + 1)
                V.tensor_tensor(ylo[:, n, :], yb, yhi[:, n, :].bitcast(F32), ALU.subtract).then_inc(y_lo, 1)
            for n in range(DC):
                u = U_OUT + n
                dve.wait_ge(unit_done, u + 1)
                V.scalar_tensor_tensor(out=xT[:, n, :], in0=G(u), scalar=gate1[:, n:n + 1], in1=xT[:, n, :],
                                       op0=ALU.mult, op1=ALU.add).then_inc(bank_read[u % 2], 1)
            dve.wait_ge(r2_ok, 1)
            for d in range(DC):
                if d >= 2:
                    dve.wait_ge(v_hi, d - 1)
                    dve.wait_ge(v_lo, d - 1)
                link(V.tensor_tensor(n2t[:, d % 2, :], xT[:, d, :], rs2[:], ALU.mult))
                V.tensor_scalar(n2t[:, d % 2, :], n2t[:, d % 2, :], a2[:, d:d + 1], sh2[:, d:d + 1], ALU.mult,
                                ALU.add).then_inc(v_f, 1)
                dve.wait_ge(v_f, d + 1)
                dve.wait_ge(v_hi, d + 1)
                V.tensor_tensor(ulo[:, d, :], n2t[:, d % 2, :], uhi[:, d, :].bitcast(F32), ALU.subtract).then_inc(
                    v_lo, 1)
            for q in range(4):
                for j in range(8):
                    n = 8 * q + j
                    taken(dve, U_FF + 16 * q + j)
                    link(V.tensor_tensor(r2buf[:], rbuf[:, j % 2, :], rbuf[:, j % 2, :], ALU.mult))
                    dve.wait_ge(f_hi, n + 1)
                    V.tensor_tensor(hlo[:, j, :], r2buf[:], hhi[:, j, :].bitcast(F32), ALU.subtract).then_inc(f_lo, 1)
                    dve.wait_ge(f_lo, n + 1)
                for j in range(8):
                    n = 8 * q + j
                    u = U_FF + 16 * q + 8 + j
                    dve.wait_ge(unit_done, u + 1)
                    if q:
                        taken(dve, u - 16)
                    V.scalar_tensor_tensor(out=xT[:, j, :], in0=G(u), scalar=gate2[:, j:j + 1], in1=xT[:, j, :],
                                           op0=ALU.mult, op1=ALU.add).then_inc(bank_read[u % 2], 1)

        @block.tensor
        def _(pe):
            T = nc.tensor
            pe.wait_ge(vec_in, 16 * 9)
            pe.wait_ge(identity_ok, 2)
            T.transpose(ps[:, 4, 0:N_VEC], vrows[0:N_VEC, :], ident[0:N_VEC, 0:N_VEC]).then_inc(vec_t, 1)
            pe.wait_ge(oh_in, 32)
            pe.wait_ge(consts, 1)
            T.matmul(ps[0:NG * AH, 5, :], relb[:], onehot[:, 0:512], start=True, stop=True)
            T.matmul(ps[0:NG * AH, 7, 0:TSUM - 512], relb[:], onehot[:, 512:TSUM], start=True, stop=True).then_inc(
                fr_mm, 1)
            pe.wait_ge(x_in, 16)
            for d in range(DC):
                if d >= 4:
                    pe.wait_ge(x_sq, d - 3)
                for t in range(TT):
                    last = T.transpose(ps[:, d % 4, t * P:(t + 1) * P], xtok[:, t, d * P:(d + 1) * P], ident[:])
                last.then_inc(x_t, 1)
                if d >= 1:
                    pe.wait_ge(x_sq, d)
                    T.matmul(ps[:, 6, :], ones[:], n1sq[:, (d - 1) % 2, :], start=d == 1, stop=False).then_inc(x_ss, 1)
            pe.wait_ge(x_sq, DC)
            T.matmul(ps[:, 6, :], ones[:], n1sq[:, (DC - 1) % 2, :], start=False, stop=True).then_inc(x_ss, 1)
            pe.wait_ge(ada_acc, 8)
            pe.wait_ge(fr_sb, 1)
            for i in range(16):
                last = T.matmul(ps[:, 7, i:i + 1], ada1[:, i * P:(i + 1) * P], ones[:, 0:1], start=True, stop=True)
            last.then_inc(ada_t, 1)
            pe.wait_ge(if_lo, 1)
            pe.wait_ge(x_sq, DC)
            for k in range(DC):
                pe.wait_ge(u_lo, k + 1)
                T.matmul(ps[:, 2, :], ifhi[:, k, :], uhi[:, k, :], start=k == 0, stop=False)
                T.matmul(ps[:, 2, :], ifhi[:, k, :], ulo[:, k, :], start=False, stop=False)
                last = T.matmul(ps[:, 2, :], iflo[:, k, :], uhi[:, k, :], start=False, stop=k == DC - 1)
            last.then_inc(if_mm, 1)

            def unit(u, mhi, mlo, ready=None):
                pe.wait_ge(w_lo, u + 1)
                if u >= 2:
                    taken(pe, u - 2)
                kc, s, b = kchunks(u), u % RING, u % 2
                for k in range(kc):
                    if ready is not None:
                        pe.wait_ge(ready[0], ready[1] + k + 1)
                    T.matmul(ps[:, b, :], whi[:, s, k, :], mhi[:, k, :], start=k == 0, stop=False)
                    T.matmul(ps[:, b, :], whi[:, s, k, :], mlo[:, k, :], start=False, stop=False)
                    last = T.matmul(ps[:, b, :], wlo[:, s, k, :], mhi[:, k, :], start=False, stop=k == kc - 1)
                last.then_inc(unit_done, 1)

            for u in range(U_CONV, U_MV):
                unit(u, uhi, ulo)
                if u == 1:
                    pe.wait_ge(rows_ok, 1)
                    for a, r in ((0, 0), (1, 2)):
                        for t in range(TT):
                            last = T.transpose(ps[:, 3, 32 * a + 8 * t:32 * a + 8 * t + 8],
                                               rows[0:8, r, t * P:(t + 1) * P], ident[0:8, 0:8])
                    last.then_inc(eT_t, 1)
                if u == 7:
                    pe.wait_ge(stage_in, 48)
                    pe.wait_ge(eT_ok, 1)
                    for h in range(AH):
                        T.matmul(ps[:, 3 + h // 2, 256 * (h % 2):256 * (h % 2) + 256], flip[:], stage[:, h, 0:2 * P],
                                 start=True, stop=True)
                    for h in range(AH):
                        T.matmul(ps[:, 5, P * h:P * h + P], flip[:], stage[:, h, 2 * P:3 * P], start=True, stop=True)
                    for h in range(AH):
                        last = T.matmul(ps[:, 6, P * h:P * h + P], flip[:], stage[:, h, 3 * P:], start=True, stop=True)
                    last.then_inc(flip_mm, 1)

            def m_scores(h, j):
                r = slice(DK * (h % 2), DK * (h % 2) + DK)
                bank, c0 = ((2, 0), (3, 0), (2, 0), (3, 384))[j]
                w = SEQ - j * P
                if j == 2:
                    pe.wait_ge(wt_ok, 4 * h + 1)
                T.matmul(ps[:, bank, c0:c0 + w], mqk[r, 4 + h // 2, j * P:(j + 1) * P], mqk[r, h // 2, j * P:],
                         start=True, stop=True).then_inc(ms_mm, 1)

            def m_turn(h):
                pe.wait_ge(hn_ok, h + 1)
                for t in range(TT):
                    last = T.transpose(ps[:, 4, t * P:(t + 1) * P], hn[:, t, :], ident[:])
                last.then_inc(ht_mm, 1)

            def m_num(h):
                pe.wait_ge(wt_ok, 4 * (h + 1))
                pe.wait_ge(vx_ok, h + 1)
                if h >= 1:
                    pe.wait_ge(hn_ok, h)
                for i in range(TT):
                    for j in range(i + 1):
                        c0 = EW[j] + (i - j) * P
                        last = T.matmul(ps[:, 6 + i // 2, (i % 2) * 256:(i % 2) * 256 + DV + 1], wts[:, h % 2, c0:c0 + P],
                                        vext[:, h % 2, j, :], start=j == 0, stop=j == i)
                last.then_inc(num_mm, 1)

            for h in range(MLH):
                unit(U_MV + h, uhi, ulo)
                if h == 0:
                    pe.wait_ge(ada_acc, 24)
                    for i in range(32):
                        last = T.matmul(ps[:, 7, 16 + i:17 + i], ada2[:, i * P:(i + 1) * P], ones[:, 0:1], start=True,
                                        stop=True)
                    last.then_inc(ada_t, 1)
                    pe.wait_ge(mqk_ok, DC)
                    pe.wait_ge(bias_ok, 1)
                    pe.wait_ge(ada_ok, 1)
                else:
                    pe.wait_ge(wt_ok, 4 * h)
                    pe.wait_ge(ex_ok, h)
                if h >= 2:
                    m_turn(h - 2)
                T.matmul(ps[:, 5, :], ident[0:MLH, h:h + 1].to_broadcast([MLH, P]), negM[:], start=True,
                         stop=True).then_inc(bc_mm, 1)
                m_scores(h, 0)
                m_scores(h, 1)
                m_scores(h, 3)
                if h >= 2:
                    pe.wait_ge(hg_ok, h - 1)
                if h >= 1:
                    pe.wait_ge(vx_ok, h)
                taken(pe, U_MV + h)
                for t in range(TT):
                    last = T.transpose(ps[:, 4, t * P:(t + 1) * P], mvT[:, t * P:(t + 1) * P], ident[:])
                last.then_inc(mv_t, 1)
                m_scores(h, 2)
                if h >= 1:
                    m_num(h - 1)

            def v_turn(j):
                taken(pe, U_ATT + 3 * j + 2)
                if j >= 1:
                    pe.wait_ge(pt_ok, j)
                for t in range(TT):
                    last = T.transpose(ps[:, 4, t * P:(t + 1) * P], vTp[:, t * P:(t + 1) * P], ident[:])
                last.then_inc(vt_mm, 1)

            def scores(j):
                pe.wait_ge(qk_n, 2 * (j + 1))
                if j >= 1:
                    pe.wait_ge(mx_ok, j)
                for t in range(TT):
                    q = qn[:, t * P:(t + 1) * P]
                    if j % NG == 0:
                        lo = P if t == 0 else 0
                        o = ps[:, 2 + t // 2, (t % 2) * 256 + lo:(t % 2) * 256 + 256]
                        last = T.matmul(o, q, kn[:, t * P - P + lo:(t + 1) * P], start=True, stop=True)
                    else:
                        last = T.matmul(ps[:, 2, t * P:(t + 1) * P], q, kn[:, t * P:(t + 1) * P], start=True, stop=True)
                last.then_inc(sc_mm, 1)

            def p_turn(j):
                pe.wait_ge(pr_ok, j + 1)
                pe.wait_ge(vt_ok, j + 1)
                slot = 0
                for t in range(TT):
                    for half in ((0, 1) if j % NG == 0 and t else (1,)):
                        c0 = half * P if j % NG == 0 else 0
                        last = T.transpose(ps[:, 4 + slot // 4, (slot % 4) * P:(slot % 4 + 1) * P],
                                           prob[:, t, c0:c0 + P], ident[:])
                        slot += 1
                last.then_inc(pt_mm, 1)

            def p_v(j):
                pe.wait_ge(pt_ok, j + 1)
                if j >= 1:
                    pe.wait_ge(o_ok, j)
                for t in range(TT):
                    o = ps[:, 7, t * P:(t + 1) * P]
                    if j % NG == 0 and t:
                        T.matmul(o, vtok[:, j % 2, t - 1], probT[:, 2 * t - 1], start=True, stop=False)
                        last = T.matmul(o, vtok[:, j % 2, t], probT[:, 2 * t], start=False, stop=True)
                    else:
                        last = T.matmul(o, vtok[:, j % 2, t], probT[:, t if j % NG else 0], start=True, stop=True)
                last.then_inc(pv_mm, 1)

            def sumsq(n):
                taken(pe, U_ATT + 3 * (n // 2) + n % 2)
                if n >= 1:
                    pe.wait_ge(qk_rs, n)
                else:
                    pe.wait_ge(hn_ok, MLH)
                T.matmul(ps[:, 6, :], ones[:], sqb[:, n % 2, :], start=True, stop=True).then_inc(qk_ss, 1)

            for s in range(36):
                j, part = divmod(s, 3)
                unit(U_ATT + s, uhi, ulo)
                if s == 0:
                    m_turn(6)
                    m_num(7)
                if s == 1:
                    pe.wait_ge(hg_ok, 7)
                    m_turn(7)
                if part == 0 and j >= 1:
                    if j == 1:
                        pe.wait_ge(hg_ok, 8)
                    v_turn(j - 1)
                    scores(j - 1)
                if part == 0 and j >= 2:
                    p_v(j - 2)
                if part == 1:
                    sumsq(2 * j)
                if part == 2:
                    sumsq(2 * j + 1)
                    if j >= 1:
                        p_turn(j - 1)

            for t in range(16):
                n, part = divmod(t, 2)
                if part == 0:
                    unit(U_YML + t, uhi, ulo)
                else:
                    unit(U_YML + t, hhi, hlo, (h_lo, 0) if t == 1 else None)
                if t == 0:
                    v_turn(11)
                    scores(11)
                    p_v(10)
                if t == 2:
                    p_turn(11)
                if t == 3:
                    p_v(11)
                if 4 <= t < 7:
                    g = t - 4
                    if g:
                        pe.wait_ge(st_ok, g)
                    for a in range(2):
                        for i in range(TT):
                            last = T.matmul(ps[0:AH, 2 + a, i * P:(i + 1) * P], stats[:, a, g, i, :], ident[:],
                                            start=True, stop=True)
                    last.then_inc(st_mm, 1)
                if t >= 8 and t % 2 == 0:
                    h = (t - 8) // 2
                    pe.wait_ge(mw_ok, 1)
                    if h:
                        pe.wait_ge(mb_rd, h)
                    for g in range(NG):
                        last = T.matmul(ps[:, 4 + g, :], ident[0:AH, h:h + 1].to_broadcast([AH, P]), mrow[:, g, :],
                                        start=True, stop=True)
                    last.then_inc(mb_mm, 1)
            for t in range(16):
                if t % 2 == 0:
                    unit(U_YATT + t, uhi, ulo)
                else:
                    unit(U_YATT + t, ahi, alo, (a_lo, 0) if t == 1 else None)
            for n in range(DC):
                unit(U_OUT + n, yhi, ylo, (y_lo, 0) if n == 0 else None)
                if n >= 1:
                    pe.wait_ge(s2_ok, n)
                    T.matmul(ps[:, 6, :], ones[:], sq2[:, (n - 1) % 2, :], start=n == 1, stop=False).then_inc(s2_mm, 1)
            pe.wait_ge(s2_ok, DC)
            T.matmul(ps[:, 6, :], ones[:], sq2[:, (DC - 1) % 2, :], start=False, stop=True).then_inc(s2_mm, 1)

            def x_turn(n):
                taken(pe, U_FF + 56 + n)
                if n >= 2:
                    pe.wait_ge(xo_ok, n - 1)
                for t in range(TT):
                    last = T.transpose(ps[:, 4 + n % 2, t * P:(t + 1) * P], xT[:, n, t * P:(t + 1) * P], ident[:])
                last.then_inc(xo_mm, 1)

            for q in range(4):
                for j in range(8):
                    unit(U_FF + 16 * q + j, uhi, ulo, (v_lo, 0) if q == 0 and j == 0 else None)
                for j in range(8):
                    unit(U_FF + 16 * q + 8 + j, hhi, hlo, (f_lo, 8 * q) if j == 0 else None)
                    if q == 3 and j >= 1:
                        x_turn(j - 1)
            x_turn(DC - 1)


_INS = ['x', 'c', 'w_ada', 'b_ada', 'norm1_g', 'norm2_g', 'w_in', 'b_if', 'conv_w', 'conv_b', 'q_norm_g', 'k_norm_g',
        'rel_bias', 'mlstm_norm_g', 'w_att_out', 'w_ml_out', 'w_out', 'w_ff1', 'w_ff2']
_OUTS = [((1, SEQ, D), 'float32')]


def kernel(**inputs):
    import numpy as _np
    import concourse.bacc as _bacc
    from concourse import mybir as _mybir
    from concourse.bass_utils import run_bass_kernel_spmd as _run

    nc = _bacc.Bacc("TRN2", target_bir_lowering=False, num_devices=1)
    arrays, args = {}, []
    data = [(name, _np.ascontiguousarray(inputs[name])) for name in _INS] + [("one_hot", bucket_one_hot())]
    for name, a in data:
        arrays[f"in_{name}_dram"] = a
        args.append(nc.dram_tensor(f"in_{name}_dram", a.shape, _mybir.dt.from_np(a.dtype), kind="ExternalInput").ap())
    for i, (shape, dtype) in enumerate(_OUTS):
        dt = _mybir.dt.from_np(_np.dtype(dtype))
        args.append(nc.dram_tensor(f"out_{i}_dram", shape, dt, kind="ExternalOutput").ap())
    block_kernel(nc, *args)
    r = _run(nc, [arrays], core_ids=[0])
    got = tuple(r.results[0][f"out_{i}_dram"] for i in range(len(_OUTS)))
    return got[0]
```

```python
from contextlib import ExitStack
import math

import numpy as np

import concourse.bass as bass
from concourse import mybir

ALU = mybir.AluOpType
ACT = mybir.ActivationFunctionType
AX = mybir.AxisListType
F32 = mybir.dt.float32
F32R = mybir.dt.float32r

P = 128
KB = 1024
SEQ = 512
D = 1024
DC = D // P
TT = SEQ // P
D_FF = 4 * D
NBUCK = 32
MAXDIST = 2048
GROUPS = ((128, 1), (512, 4), (2048, 16))
NG = 3
AH = 4
DH = 128
MLH = 8
DK = 64
DV = 128
TAPS = 4
EPS = 1e-6
NEG = -1e30
C_AQ, C_AK, C_AV = 0, NG * AH * DH, 2 * NG * AH * DH
C_MQ = 3 * NG * AH * DH
C_MV = C_MQ + 2 * MLH * DK
C_MO = C_MV + MLH * DV
C_MI = C_MO + MLH * DV
C_MF = C_MI + MLH
C_GA = C_MF + MLH
C_GB = C_GA + D
TW = (3 * P - 1, 2 * P - 1, 2 * P - 1)
TO = (0, TW[0], TW[0] + TW[1])
TSUM = sum(TW)

U_CONV = 0
U_MO = 8
U_MV = 16
U_ATT = 24
U_YML = 60
U_YATT = 76
U_OUT = 92
U_FF = 100
N_UNITS = 164
RING = 4
WARM = 6
WARM2 = 2


def bucket_of(dist):
    exact = NBUCK // 2
    d = np.maximum(dist, exact).astype(np.float32)
    large = exact + (np.log(d / np.float32(exact)) / np.float32(math.log(MAXDIST / exact))
                     * np.float32(NBUCK - exact)).astype(np.int32)
    return np.where(dist < exact, dist, np.minimum(large, NBUCK - 1))


def bucket_one_hot():
    m = np.zeros((NBUCK + 1, TSUM), np.float32)
    for g, (window, dil) in enumerate(GROUPS):
        for x in range(TW[g]):
            delta = (2 * P - 1 if g == 0 else P - 1) - x
            if 0 <= delta <= window // dil:
                m[int(bucket_of(np.array(delta * dil))), TO[g] + x] = 1.0
            else:
                m[NBUCK, TO[g] + x] = NEG
    return m


def block_kernel(nc, x, c, w_ada, b_ada, norm1_g, norm2_g, w_in, b_if, conv_w, conv_b, q_norm_g, k_norm_g,
                 rel_bias, mlstm_norm_g, w_att_out, w_ml_out, w_out, w_ff1, w_ff2, one_hot, out):
    base = nc.sbuf_base + (-nc.sbuf_base) % 64
    limit = nc.sbuf_usable_end

    def at(name, kb, shape, dt=F32):
        off = base + int(kb * KB)
        assert off + 4 * int(np.prod(shape[1:])) <= limit, name
        return nc.alloc_sbuf_tensor_at(name, shape, dt, offset=off)

    xT = at("xT", 0, [P, DC, SEQ])
    wraw = at("wraw", 16, [P, RING, DC, P])
    whi = at("whi", 32, [P, RING, DC, P], F32R)
    wlo = at("wlo", 48, [P, RING, DC, P], F32R)
    uhi = at("uhi", 64, [P, DC, SEQ], F32R)
    ulo = at("ulo", 80, [P, DC, SEQ], F32R)
    hhi = at("hhi", 96, [P, DC, SEQ], F32R)
    hlo = at("hlo", 112, [P, DC, SEQ], F32R)
    ada1 = at("ada1", 96, [P, 2 * D])
    ada2 = at("ada2", 96, [P, 2 * D])
    vrows = at("vrows", 120, [P, P])
    crow = at("crow", 194.25, [DC, P])
    flip = at("flip", 120, [P, P])
    rows = at("rows", 120.5, [P, 3, SEQ])
    onehot = at("onehot", 124, [NBUCK + 1, TSUM])
    relb = at("relb", 127.75, [NBUCK + 1, NG * AH])
    xtok = at("xtok", 128, [P, TT, D])
    xn = at("xn", 128, [P, DC, SEQ])
    ifraw = at("ifraw", 144, [P, DC, P])
    ifhi = at("ifhi", 148, [P, DC, P], F32R)
    iflo = at("iflo", 152, [P, DC, P], F32R)
    stage = at("stage", 144, [P, AH, 4 * P])
    n1sq = at("n1sq", 184, [P, 2, SEQ])
    n1t = at("n1t", 188, [P, 2, SEQ])
    n1rs = at("n1rs", 192, [P, SEQ])
    adabuf = at("adabuf", 160, [P, 3, 2 * D])
    adabuf3 = at("adabuf3", 104, [P, 3, 2 * D])
    ada3 = at("ada3", 96, [P, 2 * D])
    mqk = at("mqk", 128, [P, DC, SEQ])
    mo = at("mo", 144, [P, DC, SEQ])
    cpad = at("cpad", 184, [P, 2, SEQ + TAPS - 1])
    cacc = at("cacc", 188.0625, [P, 2, SEQ])
    csig = at("csig", 192.0625, [P, SEQ])
    csum = at("csum", 116, [MLH, SEQ])
    frow = at("frow", 156, [NG * AH, TSUM])
    negM = at("negM", 194.125, [32 + MLH, SEQ], F32R)
    EW = (0, 512, 896, 1152, 1280)
    expd = at("expd", 160, [P, TT, SEQ])
    dcl = at("dcl", 168, [P, TT, P])
    wts = at("wts", 170, [P, 2, EW[4]])
    vext = at("vext", 180, [P, 2, TT, DV + 1])
    mvT = at("mvT", 184.125, [P, SEQ])
    hn = at("hn", 186.125, [P, TT, DV])
    hg = at("hg", 188.125, [P, SEQ])
    kst = [at(f"kst{i}", o, [P, SEQ], F32R) for i, o in enumerate((108, 124))]
    qst = [at(f"qst{i}", o, [P, SEQ], F32R) for i, o in enumerate((110, 126))]
    qsw = [at(f"qsw{i}", o, [P, SEQ], F32R) for i, o in enumerate((190.125, 192.125))]
    qf = at("qf", 128, [P, 2, SEQ])
    sqhi = at("sqhi", 132, [P, 2, SEQ], F32R)
    sqf = at("sqf", 190.125, [P, SEQ])
    sqlo = at("sqlo", 192.125, [P, SEQ], F32R)
    rsb = at("rsb", 136, [P, 2, SEQ])
    qn = at("qn", 140, [P, SEQ])
    kn = at("kn", 142, [P, SEQ])
    outT = at("outT", 144, [P, NG * AH, SEQ])
    vTp = at("vTp", 168, [P, SEQ])
    vtok = at("vtok", 170, [P, 2, TT, DH])
    sbias = at("sbias", 174, [P, TT, 2 * P])
    prob = at("prob", 178, [P, TT, 2 * P])
    probT = at("probT", 182, [P, 7, P])
    bias0 = at("bias0", 196.125, [P, AH, 2 * P])
    bias1 = at("bias1", 200.125, [P, AH, P])
    bias2 = at("bias2", 202.125, [P, AH, P])
    ahi = at("ahi", 128, [P, AH, SEQ], F32R)
    alo = at("alo", 136, [P, AH, SEQ], F32R)
    mrow = at("mrow", 168, [AH, NG, SEQ])
    lrow = at("lrow", 174, [AH, NG, SEQ])
    mtop = at("mtop", 180, [AH, SEQ])
    mrec = at("mrec", 182, [AH, SEQ])
    mtmp = at("mtmp", 168, [P, 3, SEQ])
    mrr = at("mrr", 174, [32 + AH, NG, SEQ], F32R)
    gsig = at("gsig", 186, [P, SEQ])
    yml = at("yml", 188, [P, DC, SEQ])
    yhi = at("yhi", 144, [P, DC, SEQ], F32R)
    ylo = at("ylo", 160, [P, DC, SEQ], F32R)
    ybuf = at("ybuf", 176, [P, 2, SEQ])
    sq2 = at("sq2", 128, [P, 2, SEQ])
    rs2 = at("rs2", 132, [P, SEQ])
    sqacc = at("sqacc", 134, [P, SEQ])
    xa = at("xa", 96, [P, DC, SEQ])
    rbuf = at("rbuf", 138, [P, 2, SEQ])
    r2buf = at("r2buf", 142, [P, SEQ])
    obuf = at("obuf", 144, [P, 2, TT, P])
    CO = 204.25
    ident = at("ident", CO, [P, P])
    ones = at("ones", CO + 0.5, [P, P])
    cols = at("cols", CO + 1, [P, P])
    adac = at("adac", CO + 1.5, [P, 48])
    small = at("small", CO + 1.75, [P, 112])
    eT = at("eT", CO + 2.25, [P, 2, TT, MLH])
    stats = at("stats", CO + 2.5, [P, 2, NG, TT, AH])
    colb = at("colb", CO + 2.875, [P, 32])
    onesr = at("onesr", CO + 3, [P, P], F32R)
    selr = at("selr", CO + 3.5, [32 + MLH, MLH], F32R)

    sc = small[:, 0:8]
    scE = small[:, 8:16]
    a1, sh1 = small[:, 16:24], small[:, 24:32]
    a2, sh2 = small[:, 32:40], small[:, 40:48]
    gate1, gate2 = small[:, 48:56], small[:, 56:64]
    qgs = small[:, 64:65]
    emT = small[:, 72:104].rearrange("p (t h) -> p t h", t=TT)
    bif = small[:, 104:105]
    mx = small[:, 105:109]
    nq, nd, nr, ss, nv = (colb[:, 4 * i:4 * i + 4] for i in range(5))
    nf = colb[:, 20:24]

    K_BADA, K_N1, K_N2, K_CW, K_CB, K_QG, K_KG, K_MG = 0, 48, 56, 64, 96, 104, 105, 106
    N_VEC = 114

    ps = nc.alloc_psum_tensor("ps", [P, 8, 512], F32)
    f_dram = nc.dram_tensor("toeplitz_rows", (NG * AH, TSUM), F32)

    with ExitStack() as ctx:
        def sem(name):
            return ctx.enter_context(nc.semaphore(name))

        c_in, c_t = sem("c_in"), sem("c_transposed")
        vec_in, x_in, oh_in, if_in, bif_in = sem("vec_in"), sem("x_in"), sem("oh_in"), sem("if_in"), sem("bif_in")
        ada_in = [sem(f"ada_in{i}") for i in range(3)]
        w_in_sem = [sem(f"w_landed{i}") for i in range(RING)]
        frow_out, stage_in = sem("frow_out"), sem("stage_in")
        out_done = [sem(f"out{i}_stored") for i in range(2)]
        consts, identity_ok, if_zero = sem("consts_set"), sem("identity_made"), sem("if_zeroed")
        w_hi, w_lo, unit_done = sem("w_hi_ready"), sem("w_lo_ready"), sem("unit_done")
        bank_read = [sem(f"bank{i}_read") for i in range(2)]
        vec_t, vec_c = sem("vec_transposed"), sem("vec_columns")
        silu_e, silu_c = sem("silu_exp"), sem("silu_ready")
        ada_acc, ada_t, ada_ok = sem("ada_accumulated"), sem("ada_transposed"), sem("ada_columns")
        x_t, x_sq, x_ss, x_rs = sem("x_transposed"), sem("x_squared"), sem("x_sumsq"), sem("x_rstd")
        u_hi, u_lo = sem("u_hi"), sem("u_lo")
        if_hi, if_lo, if_mm = sem("if_hi"), sem("if_lo"), sem("if_product")
        lf_a, lf_b, rows_ok, eT_t, eT_ok = (sem("lf_abs"), sem("lf_log"), sem("rows_ready"), sem("e_transposed"),
                                            sem("e_columns"))
        em_ok = sem("exp_neg_m")
        fr_mm, fr_sb, flip_mm, bias_ok = sem("frow_product"), sem("frow_sbuf"), sem("bias_flipped"), sem("bias_ready")
        cv_acc, cv_sig, mqk_ok, mo_ok = sem("conv_sum"), sem("conv_sigmoid"), sem("mqk_ready"), sem("mo_ready")
        mv_t, vx_ok = sem("mv_transposed"), sem("v_ready")
        st_hi, st_lo, pad_ok = sem("stack_hi"), sem("stack_lo"), sem("pad_zeroed")
        bc_mm, dc_ok, ex_dg, ex_ok, ex_msk = (sem("negM_broadcast"), sem("decay_clamped"), sem("decay_diagonal"),
                                               sem("decay_exp"), sem("decay_masked"))
        ms_mm, wt_ok, num_mm = sem("mscores"), sem("mweights"), sem("mnumerator")
        nq_ok, nsq, nrr, nrs, hn_ok = sem("nq_copied"), sem("num_squares"), sem("num_var"), sem("num_rstd"), sem("hn_ready")
        ht_mm, hg_ok, h_hi, h_lo = sem("h_transposed"), sem("h_gated"), sem("h_hi"), sem("h_lo")
        qk_ss, qk_rs, qk_n = sem("qk_sumsq"), sem("qk_rstd"), sem("qk_normed")
        vt_mm, vt_ok = sem("v_transposed"), sem("v_tokens")
        sc_mm, mx_ok, pr_ok = sem("scores"), sem("row_max"), sem("probs")
        pt_mm, pt_ok, pv_mm, o_ok = sem("probs_transposed"), sem("probsT_ready"), sem("pv"), sem("o_copied")
        st_mm, st_ok, md_ok, me_ok, mw_ok = (sem("stats_turned"), sem("stats_rows"), sem("merge_diff"),
                                             sem("merge_exp"), sem("merge_weights"))
        mb_mm, mb_rd, att_f, a_hi, a_lo = (sem("weights_broadcast"), sem("broadcast_read"), sem("att_ready"),
                                           sem("att_hi"), sem("att_lo"))
        y_ok, y_hi, y_lo = sem("y_ready"), sem("y_hi"), sem("y_lo")
        s2_ok, s2_mm, r2_ok = sem("x1_squared"), sem("x1_sumsq"), sem("x1_rstd")
        v_f, v_g, v_hi, v_lo = sem("u2_even"), sem("u2_odd"), sem("u2_hi"), sem("u2_lo")
        xn_ok, sq_lo, s2_add, xa_ok = sem("xn_ready"), sem("squares_lo"), sem("squares_added"), sem("x1_scaled")
        f_hi, f_lo = sem("hdn_hi"), sem("hdn_lo")
        xo_mm, xo_ok = sem("x2_transposed"), sem("out_tile")
        dve_step, act_step, pool_step = sem("dve_step"), sem("act_step"), sem("pool_step")

        w_in2 = w_in[0]

        def slab(u):
            def cols_of(w, c0, kc=DC, r0=0):
                return w[r0:r0 + kc * P, c0:c0 + P].rearrange("(k p) n -> p k n", p=P), kc
            if u < U_MO:
                return cols_of(w_in2, C_MQ + u * P)
            if u < U_MV:
                return cols_of(w_in2, C_MO + (u - U_MO) * P)
            if u < U_ATT:
                return cols_of(w_in2, C_MV + (u - U_MV) * P)
            if u < U_YML:
                j, part = divmod(u - U_ATT, 3)
                h, g = divmod(j, NG)
                return cols_of(w_in2, (C_AQ, C_AK, C_AV)[part] + (g * AH + h) * DH)
            if u < U_YATT:
                n, part = divmod(u - U_YML, 2)
                return cols_of(w_ml_out[0], n * P) if part else cols_of(w_in2, C_GB + n * P)
            if u < U_OUT:
                n, part = divmod(u - U_YATT, 2)
                return cols_of(w_att_out[0], n * P, AH) if part else cols_of(w_in2, C_GA + n * P)
            if u < U_FF:
                return cols_of(w_out[0], (u - U_OUT) * P)
            q, j = divmod(u - U_FF, 16)
            if j < 8:
                return cols_of(w_ff1[0], (q * 8 + j) * P)
            return cols_of(w_ff2[0], (j - 8) * P, DC, q * D)

        def kchunks(u):
            return AH if U_YATT <= u < U_OUT and (u - U_YATT) % 2 else DC

        def taken(eng, u):
            eng.wait_ge(bank_read[u % 2], u // 2 + 1)

        diagonal = bass.AP(tensor=expd[:].tensor, offset=expd[:].offset, ap=[expd[:].ap[0], [SEQ + P, TT], [1, P]])

        block = ctx.enter_context(nc.Block())

        @block.sync
        def _(sp):
            sp.dma_start(crow[0:DC, :], c.rearrange("b (a p) -> (b a) p", p=P)).then_inc(c_in, 16)
            sp.dma_start(xtok[:], x[0].rearrange("(t p) d -> p t d", p=P)).then_inc(x_in, 16)

            def ada(i):
                if i >= 3:
                    sp.wait_ge(ada_acc, i - 2)
                g, k = divmod(i, 8)
                dst = adabuf if i < 16 else adabuf3
                sp.dma_start(dst[:, i % 3, :], w_ada[0, k * P:(k + 1) * P, 2 * D * g:2 * D * (g + 1)]).then_inc(
                    ada_in[i % 3], 16)

            def weights(u):
                if u >= RING:
                    sp.wait_ge(w_lo, u - RING + 1)
                src, kc = slab(u)
                sp.dma_start(wraw[:, u % RING, 0:kc, :], src).then_inc(w_in_sem[u % RING], 16)

            for i in range(8):
                ada(i)
                if i == 2:
                    sp.wait_ge(if_zero, 2)
                    sp.dma_start(ifraw[:, :, 0:MLH],
                                 w_in2[:, C_MI:C_MI + MLH].rearrange("(k p) n -> p k n", p=P)).then_inc(if_in, 16)
                    sp.dma_start(ifraw[:, :, 32:32 + MLH],
                                 w_in2[:, C_MF:C_MF + MLH].rearrange("(k p) n -> p k n", p=P)).then_inc(if_in, 16)
            for u in range(RING):
                weights(u)
            for u in range(RING, N_UNITS):
                weights(u)
                if RING + 6 <= u < RING + 14:
                    ada(8 + u - RING - 6)
                if U_YATT + 8 <= u < U_YATT + 16:
                    sp.wait_ge(unit_done, U_YATT)
                    ada(16 + u - U_YATT - 8)
                if u == RING + 4:
                    sp.wait_ge(fr_sb, 1)
                    sp.dma_start(f_dram.ap(), frow[:]).then_inc(frow_out, 16)
                    sp.wait_ge(frow_out, 16)
                    sp.wait_ge(if_mm, 1)
                    for g, (w, c0) in enumerate(((2 * P, 0), (P, 2 * P), (P, 3 * P))):
                        src = bass.AP(tensor=f_dram.ap().tensor, offset=g * AH * TSUM + TO[g],
                                      ap=[[1, P], [TSUM, AH], [1, w]])
                        sp.dma_start(stage[:, :, c0:c0 + w], src).then_inc(stage_in, 16)
            out_tok = out[0].rearrange("(t p) d -> p t d", p=P)
            for n in range(DC):
                sp.wait_ge(xo_ok, n + 1)
                sp.dma_start(out_tok[:, :, n * P:(n + 1) * P], obuf[:, n % 2]).then_inc(out_done[n % 2], 16)
            for b in range(2):
                sp.wait_ge(out_done[b], 16 * DC // 2)

        @block.gpsimd
        def _(pool):
            nc.gpsimd.memset(ident[:], 0.0).then_inc(pool_step, 1)
            pool.wait_ge(pool_step, 1)
            nc.gpsimd.affine_select(out=ident[:], in_=ident[:], compare_op=ALU.not_equal, fill=1.0, base=0,
                                    pattern=[[1, P]], channel_multiplier=-1).then_inc(identity_ok, 1)
            pool.wait_ge(vec_t, 1)
            nc.gpsimd.memset(flip[:], 0.0).then_inc(pool_step, 1)
            pool.wait_ge(pool_step, 2)
            nc.gpsimd.affine_select(out=flip[:], in_=flip[:], compare_op=ALU.not_equal, fill=1.0, base=1 - P,
                                    pattern=[[1, P]], channel_multiplier=1).then_inc(identity_ok, 1)
            pool.wait_ge(if_hi, 1)
            nc.gpsimd.tensor_tensor(iflo[:], ifraw[:], ifhi[:].bitcast(F32), ALU.subtract).then_inc(if_lo, 1)

            def low(u):
                pool.wait_ge(w_hi, u + 1)
                kc, s = kchunks(u), u % RING
                nc.gpsimd.tensor_tensor(wlo[:, s, 0:kc, :], wraw[:, s, 0:kc, :], whi[:, s, 0:kc, :].bitcast(F32),
                                        ALU.subtract).then_inc(w_lo, 1)

            pool.wait_ge(x_rs, 1)
            for d in range(DC):
                nc.gpsimd.tensor_tensor(xn[:, d, :], xT[:, d, :], n1rs[:], ALU.mult).then_inc(xn_ok, 1)
                if d == 5:
                    low(0)

            def mask(h):
                pool.wait_ge(ex_dg, h + 1)
                nc.gpsimd.affine_select(out=diagonal, in_=diagonal, compare_op=ALU.is_ge, fill=0.0, base=0,
                                        pattern=[[0, TT], [1, P]], channel_multiplier=-1).then_inc(ex_msk, 1)

            def m_stack(h):
                own, other = (slice(DK * b, DK * b + DK) for b in (h % 2, 1 - h % 2))
                pool.wait_ge(st_hi, h + 1)
                pool.wait_ge(w_lo, U_MV + 4 + h)
                if h >= 1:
                    pool.wait_ge(ex_msk, h)
                k, q = mqk[own, 4 + h // 2, :], mqk[own, h // 2, :]
                khi, qhi = kst[h % 2][own, :].bitcast(F32), qst[h % 2][own, :].bitcast(F32)
                for n, (dst, src, hi) in enumerate(((kst[h % 2][other, :], k, khi), (qst[h % 2][other, :], q, qhi),
                                                    (qsw[h % 2][own, :], q, qhi))):
                    nc.gpsimd.tensor_tensor(dst, src, hi, ALU.subtract).then_inc(st_lo, 1)
                    pool.wait_ge(st_lo, 3 * h + n + 1)

            for u in range(1, N_UNITS):
                low(u)
                if u == U_MV + 3:
                    m_stack(0)
                if U_MV + 4 <= u < U_MV + 4 + MLH:
                    mask(u - U_MV - 4)
                    if u < U_MV + 3 + MLH:
                        m_stack(u - U_MV - 3)
                if u == U_FF + RING - 1:
                    pool.wait_ge(r2_ok, 1)
                    for d in range(1, DC, 2):
                        pool.wait_ge(xa_ok, d + 1)
                        nc.gpsimd.tensor_tensor(xa[:, d, :], xa[:, d, :], rs2[:], ALU.mult).then_inc(v_g, 1)

        @block.scalar
        def _(act):
            count = [0]

            def link(ins):
                count[0] += 1
                ins.then_inc(act_step, 1)
                act.wait_ge(act_step, count[0])

            def high(u):
                act.wait_ge(w_in_sem[u % RING], 16 * (u // RING + 1))
                if u >= RING:
                    act.wait_ge(unit_done, u - RING + 1)
                kc, s = kchunks(u), u % RING
                nc.scalar.copy(whi[:, s, 0:kc, :], wraw[:, s, 0:kc, :]).then_inc(w_hi, 1)

            G = lambda u: ps[:, u % 2, :]

            def rows_of(a, r0, n):
                act.dma_start(vrows[r0:r0 + n, :], a).then_inc(vec_in, 16)
            rows_of(b_ada.rearrange("b (a p) -> (b a) p", p=P), K_BADA, 48)
            rows_of(norm1_g.rearrange("b (a p) -> (b a) p", p=P), K_N1, DC)
            rows_of(norm2_g.rearrange("b (a p) -> (b a) p", p=P), K_N2, DC)
            rows_of(conv_w[0].rearrange("t (a p) -> (t a) p", p=P), K_CW, TAPS * DC)
            rows_of(conv_b.rearrange("b (a p) -> (b a) p", p=P), K_CB, DC)
            rows_of(q_norm_g, K_QG, 1)
            rows_of(k_norm_g, K_KG, 1)
            rows_of(mlstm_norm_g.rearrange("b (a p) -> (b a) p", p=P), K_MG, DC)
            act.dma_start(onehot[:], one_hot).then_inc(oh_in, 16)
            act.wait_ge(if_zero, 1)
            act.dma_start(relb[0:NBUCK, :], rel_bias).then_inc(oh_in, 16)
            act.dma_start(bif[0:MLH, :], b_if[0, 0:1, :].rearrange("a h -> h a")).then_inc(bif_in, 16)
            act.dma_start(bif[32:32 + MLH, :], b_if[0, 1:2, :].rearrange("a h -> h a")).then_inc(bif_in, 16)
            nc.scalar.preload_act_table_set("natural_log_exp_and_others")
            act.wait_ge(c_t, 1)
            nc.scalar.activation(scE, ps[:, 7, 0:DC], ACT.Exp, scale=-1.0).then_inc(silu_e, 1)
            for d in range(DC):
                act.wait_ge(x_t, d + 1)
                nc.scalar.copy(xT[:, d, :], ps[:, d % 4, :])
                if d >= 2:
                    act.wait_ge(x_ss, d - 1)
                nc.scalar.activation(n1sq[:, d % 2, :], ps[:, d % 4, :], ACT.Square).then_inc(x_sq, 1)
            act.wait_ge(if_in, 32)
            nc.scalar.copy(ifhi[:], ifraw[:]).then_inc(if_hi, 1)
            act.wait_ge(x_ss, DC)
            act.wait_ge(consts, 3)
            link(nc.scalar.activation(n1rs[:], ps[:, 6, :], ACT.Ln, scale=1.0 / D, bias=small[:, 109:110]))
            nc.scalar.activation(n1rs[:], n1rs[:], ACT.Exp, scale=-0.5).then_inc(x_rs, 1)
            act.wait_ge(vec_t, 1)
            nc.scalar.copy(cols[:, 0:N_VEC], ps[:, 4, 0:N_VEC]).then_inc(vec_c, 1)
            act.wait_ge(fr_mm, 1)
            nc.scalar.copy(frow[:, 0:512], ps[0:NG * AH, 5, :])
            nc.scalar.copy(frow[:, 512:TSUM], ps[0:NG * AH, 4, 0:TSUM - 512]).then_inc(fr_sb, 1)
            for u in range(RING - 1):
                high(u)
            act.wait_ge(ada_ok, 1)
            for d in range(DC):
                act.wait_ge(xn_ok, d + 1)
                nc.scalar.activation(uhi[:, d, :], xn[:, d, :], ACT.Identity, scale=a1[:, d:d + 1],
                                     bias=sh1[:, d:d + 1]).then_inc(u_hi, 1)
                if d == 1:
                    high(RING - 1)

            def after(u):
                act.wait_ge(unit_done, u + 1)
                if u + RING < N_UNITS:
                    high(u + RING)

            def conv_sigmoid(u):
                act.wait_ge(cv_acc, u + 1)
                if u >= 1:
                    act.wait_ge(mqk_ok, u)
                nc.scalar.activation(csig[:], cacc[:, u % 2, :], ACT.Sigmoid).then_inc(cv_sig, 1)

            for u in range(U_CONV, U_MO):
                after(u)
                if u >= 2:
                    act.wait_ge(cv_acc, u - 1)
                else:
                    act.wait_ge(pad_ok, 1)
                nc.scalar.copy(cpad[:, u % 2, TAPS - 1:], G(u)).then_inc(bank_read[u % 2], 1)
                if u == 0:
                    act.wait_ge(lf_a, 1)
                    link(nc.scalar.activation(rows[32:40, 1, :], rows[32:40, 1, :], ACT.Exp, scale=-1.0))
                    nc.scalar.activation(rows[32:40, 1, :], rows[32:40, 1, :], ACT.Ln, bias=1.0).then_inc(lf_b, 1)
                if u >= 1:
                    conv_sigmoid(u - 1)
            conv_sigmoid(U_MO - 1)

            def m_stack(h):
                own, other = (slice(DK * b, DK * b + DK) for b in (h % 2, 1 - h % 2))
                act.wait_ge(mqk_ok, 5 + h // 2)
                if h >= 2:
                    act.wait_ge(ms_mm, 4 * (h - 1))
                nc.scalar.copy(kst[h % 2][own, :], mqk[own, 4 + h // 2, :])
                nc.scalar.copy(qst[h % 2][own, :], mqk[own, h // 2, :])
                nc.scalar.copy(qsw[h % 2][other, :], mqk[own, h // 2, :]).then_inc(st_hi, 1)

            for u in range(U_MO, U_MV):
                after(u)
                if u == U_MV - 1:
                    m_stack(0)
                if u == U_MO:
                    act.wait_ge(bias_ok, 1)
                nc.scalar.activation(mo[:, u - U_MO, :], G(u), ACT.Sigmoid).then_inc(bank_read[u % 2], 1)

            nc.scalar.preload_act_table_set("natural_log_exp_and_others")
            act.wait_ge(eT_ok, 1)
            nc.scalar.activation(emT, eT[:, 1], ACT.Exp).then_inc(em_ok, 1)

            def m_exp(h):
                if h >= 1:
                    act.wait_ge(wt_ok, 4 * h)
                act.wait_ge(dc_ok, h + 1)
                nc.scalar.activation(diagonal, dcl[:], ACT.Exp).then_inc(ex_dg, 1)
                for j in range(TT - 1):
                    last = nc.scalar.activation(expd[:, j, (j + 1) * P:], ps[:, 5, (j + 1) * P:SEQ], ACT.Exp,
                                                bias=eT[:, 0, j, h:h + 1])
                last.then_inc(ex_ok, 1)

            def m_high(h):
                act.wait_ge(hg_ok, h + 1)
                nc.scalar.copy(hhi[:, h, :], hg[:]).then_inc(h_hi, 1)

            def m_norm(h):
                act.wait_ge(nq_ok, h + 1)
                for i in range(TT):
                    last = nc.scalar.activation(hn[:, i, :], ps[:, 6 + i // 2, (i % 2) * 256:(i % 2) * 256 + DV],
                                                ACT.Square, accum_out=ss[:, i:i + 1])
                last.then_inc(nsq, 1)
                act.wait_ge(nrr, h + 1)
                link(nc.scalar.activation(nv, nv, ACT.Ln, scale=1.0 / DV, bias=small[:, 109:110]))
                nc.scalar.activation(nv, nv, ACT.Exp, scale=-0.5).then_inc(nrs, 1)

            for h in range(MLH):
                u = U_MV + h
                after(u)
                if h >= 1:
                    act.wait_ge(mv_t, h)
                nc.scalar.copy(mvT[:], G(u)).then_inc(bank_read[u % 2], 1)
                m_exp(h)
                if h < MLH - 1:
                    m_stack(h + 1)
                if h >= 2:
                    m_high(h - 2)
                if h >= 1:
                    m_norm(h - 1)

            def exps(j):
                g = j % NG
                h = j // NG
                act.wait_ge(mx_ok, j + 1)
                for t in range(TT):
                    lo = P if g == 0 and t == 0 else 0
                    w = 2 * P if g == 0 else P
                    last = nc.scalar.activation(prob[:, t, lo:w], sbias[:, t, lo:w], ACT.Exp,
                                                bias=stats[:, 0, g, t, h:h + 1], accum_out=stats[:, 1, g, t, h:h + 1])
                last.then_inc(pr_ok, 1)

            def o_copy(j):
                g, h = j % NG, j // NG
                dil = GROUPS[g][1]
                act.wait_ge(pv_mm, j + 1)
                nc.scalar.copy(outT[:, j, :].rearrange("p (s r) -> p s r", r=dil),
                               ps[:, 7, :].rearrange("p (r s) -> p s r", r=dil)).then_inc(o_ok, 1)

            def rstd(n):
                act.wait_ge(qk_ss, n + 1)
                if n >= 2:
                    act.wait_ge(qk_n, n - 1)
                link(nc.scalar.activation(rsb[:, n % 2, :], ps[:, 6, :], ACT.Ln, scale=1.0 / DH, bias=small[:, 109:110]))
                nc.scalar.activation(rsb[:, n % 2, :], rsb[:, n % 2, :], ACT.Exp, scale=-0.5).then_inc(qk_rs, 1)

            for s in range(36):
                u = U_ATT + s
                j, part = divmod(s, 3)
                after(u)
                if part < 2:
                    n = 2 * j + part
                    if n >= 2:
                        act.wait_ge(qk_n, n - 1)
                        act.wait_ge(qk_ss, n - 1)
                    nc.scalar.copy(qf[:, part, :], G(u))
                    nc.scalar.activation(sqhi[:, part, :], G(u), ACT.Square).then_inc(bank_read[u % 2], 1)
                if part == 0:
                    if s == 0:
                        m_high(6)
                        m_norm(7)
                    if j >= 2:
                        o_copy(j - 2)
                    if j >= 1:
                        exps(j - 1)
                if part == 1:
                    if s == 1:
                        m_high(7)
                    rstd(2 * j)
                if part == 2:
                    rstd(2 * j + 1)

            for t in range(16):
                u = U_YML + t
                n, part = divmod(t, 2)
                if t == 5:
                    act.wait_ge(md_ok, 1)
                    nc.scalar.activation(mrow[:], mrow[:], ACT.Exp).then_inc(me_ok, 1)
                after(u)
                if t == 0:
                    o_copy(10)
                    exps(11)
                if t == 3:
                    o_copy(11)
                if part == 0:
                    if n >= 1:
                        taken(act, u - 1)
                    nc.scalar.activation(gsig[:], G(u), ACT.Sigmoid).then_inc(bank_read[u % 2], 1)
                if t == 4:
                    nc.scalar.preload_act_table_set("natural_log_exp_and_others")
                if t >= 9 and t % 2 == 1:
                    h = (t - 9) // 2
                    act.wait_ge(att_f, h + 1)
                    nc.scalar.copy(ahi[:, h, :], mtmp[:, 0, :]).then_inc(a_hi, 1)
            for t in range(16):
                u = U_YATT + t
                n, part = divmod(t, 2)
                after(u)
                if part == 0:
                    taken(act, u - 1)
                    nc.scalar.activation(gsig[:], G(u), ACT.Sigmoid).then_inc(bank_read[u % 2], 1)
                else:
                    act.wait_ge(y_ok, n + 1)
                    nc.scalar.copy(yhi[:, n, :], ybuf[:, n % 2, :]).then_inc(y_hi, 1)
            nc.scalar.preload_act_table_set("natural_log_exp_and_others")
            for n in range(DC):
                if n < DC - 1:
                    after(U_OUT + n)
                taken(act, U_OUT + n)
                if n >= 3:
                    act.wait_ge(s2_add, n - 2)
                dst = sq2[:, n % 2, :] if n else sqacc[:]
                nc.scalar.activation(dst, xT[:, n, :], ACT.Square).then_inc(s2_ok, 1)
            after(U_OUT + DC - 1)
            act.wait_ge(s2_mm, 1)
            link(nc.scalar.activation(rs2[:], ps[:, 6, :], ACT.Ln, scale=1.0 / D, bias=small[:, 109:110]))
            nc.scalar.activation(rs2[:], rs2[:], ACT.Exp, scale=-0.5).then_inc(r2_ok, 1)
            for d in range(DC):
                act.wait_ge((v_f, v_g)[d % 2], d // 2 + 1)
                nc.scalar.activation(uhi[:, d, :], xa[:, d, :], ACT.Identity, bias=sh2[:, d:d + 1]).then_inc(v_hi, 1)
            for q in range(4):
                for j in range(8):
                    u = U_FF + 16 * q + j
                    n = 8 * q + j
                    after(u)
                    if n >= 2:
                        act.wait_ge(f_lo, n - 1)
                    nc.scalar.activation(rbuf[:, j % 2, :], G(u), ACT.Relu).then_inc(bank_read[u % 2], 1)
                    taken(act, u)
                    nc.scalar.activation(hhi[:, j, :], rbuf[:, j % 2, :], ACT.Square).then_inc(f_hi, 1)
                for j in range(8):
                    after(U_FF + 16 * q + 8 + j)
                    if q == 3 and j >= 1:
                        n = j - 1
                        act.wait_ge(xo_mm, n + 1)
                        if n >= 2:
                            act.wait_ge(out_done[n % 2], 16 * (n // 2))
                        nc.scalar.copy(obuf[:, n % 2], ps[:, 4 + n % 2, :].rearrange("p (t d) -> p t d", t=TT)).then_inc(
                            xo_ok, 1)
            act.wait_ge(xo_mm, DC)
            act.wait_ge(out_done[1], 16 * (DC // 2 - 1))
            nc.scalar.copy(obuf[:, 1], ps[:, 5, :].rearrange("p (t d) -> p t d", t=TT)).then_inc(xo_ok, 1)

        @block.vector
        def _(dve):
            count = [0]
            V = nc.vector

            def link(ins):
                count[0] += 1
                ins.then_inc(dve_step, 1)
                dve.wait_ge(dve_step, count[0])

            G = lambda u: ps[:, u % 2, :]

            V.memset(relb[32:33, :], 1.0).then_inc(if_zero, 1)
            V.memset(ifraw[:], 0.0).then_inc(if_zero, 1)
            V.memset(ones[:], 1.0).then_inc(consts, 1)
            V.memset(selr[:].bitcast(F32), 0.0)
            dve.wait_ge(consts, 1)
            link(V.tensor_copy(onesr[:], ones[:]))
            dve.wait_ge(identity_ok, 1)
            V.tensor_copy(selr[0:MLH, :], ident[0:MLH, 0:MLH])
            link(V.tensor_copy(selr[32:32 + MLH, :], ident[32:32 + MLH, 32:32 + MLH]))
            V.memset(small[:, 109:110], EPS).then_inc(consts, 1)
            V.memset(bias2[:], NEG).then_inc(consts, 1)
            dve.wait_ge(silu_e, 1)
            link(V.tensor_scalar(scE, scE, 1.0, None, ALU.add))
            link(V.reciprocal(scE, scE))
            V.tensor_tensor(sc, ps[:, 7, 0:DC], scE, ALU.mult).then_inc(silu_c, 1)
            dve.wait_ge(silu_c, 1)

            def ada(i):
                dve.wait_ge(ada_in[i % 3], 16 * (i // 3 + 1))
                if i >= 1:
                    dve.wait_ge(ada_acc, i)
                g, k = divmod(i, 8)
                dst = (ada1, ada2, ada3)[g][:]
                src = (adabuf, adabuf, adabuf3)[g][:, i % 3, :]
                if k == 0:
                    V.tensor_scalar(dst, src, sc[:, k:k + 1], None, ALU.mult).then_inc(ada_acc, 1)
                else:
                    V.scalar_tensor_tensor(out=dst, in0=src, scalar=sc[:, k:k + 1], in1=dst,
                                           op0=ALU.mult, op1=ALU.add).then_inc(ada_acc, 1)

            for i in range(8):
                ada(i)
            dve.wait_ge(vec_c, 1)
            V.tensor_scalar(qgs, cols[:, K_QG:K_QG + 1], DH ** -0.5, None, ALU.mult)
            dve.wait_ge(ada_t, 1)
            link(V.tensor_tensor(adac[:, 0:16], ps[:, 7, 0:16], cols[:, K_BADA:K_BADA + 16], ALU.add))
            V.tensor_copy(sh1, adac[:, 0:8])
            V.scalar_tensor_tensor(out=a1, in0=adac[:, 8:16], scalar=1.0, in1=cols[:, K_N1:K_N1 + DC],
                                   op0=ALU.add, op1=ALU.mult).then_inc(ada_ok, 1)
            dve.wait_ge(ada_ok, 1)
            for d in range(DC):
                dve.wait_ge(xn_ok, d + 1)
                if d >= 2:
                    dve.wait_ge(u_lo, d - 1)
                link(V.tensor_scalar(n1t[:, d % 2, :], xn[:, d, :], a1[:, d:d + 1], sh1[:, d:d + 1], ALU.mult,
                                     ALU.add))
                dve.wait_ge(u_hi, d + 1)
                V.tensor_tensor(ulo[:, d, :], n1t[:, d % 2, :], uhi[:, d, :].bitcast(F32), ALU.subtract).then_inc(
                    u_lo, 1)
            V.memset(rows[0:8, 2, :], 1.0)
            V.memset(negM[:].bitcast(F32), 0.0)
            V.memset(cpad[:, :, 0:TAPS - 1], 0.0).then_inc(pad_ok, 1)
            dve.wait_ge(pad_ok, 1)
            dve.wait_ge(if_mm, 1)
            dve.wait_ge(bif_in, 32)
            z, az = rows[32:40, 0, :], rows[32:40, 1, :]
            link(V.tensor_scalar(z, ps[32:40, 2, :], bif[32:40, :], None, ALU.add))
            V.scalar_tensor_tensor(out=az, in0=z, scalar=-1.0, in1=z, op0=ALU.mult, op1=ALU.max).then_inc(lf_a, 1)
            link(V.tensor_scalar(rows[0:8, 0, :], ps[0:8, 2, :], bif[0:8, :], None, ALU.add))
            link(V.tensor_scalar(z, z, 0.0, None, ALU.min))
            dve.wait_ge(lf_b, 1)
            link(V.tensor_tensor(rows[0:8, 1, :], z, az, ALU.subtract))
            link(V.tensor_tensor_scan(csum[:], rows[0:8, 2, :], rows[0:8, 1, :], 0.0, ALU.mult, ALU.add))
            link(V.tensor_tensor(rows[0:8, 0, :], rows[0:8, 0, :], csum[:], ALU.subtract))
            link(V.tensor_tensor_scan(rows[0:8, 1, :], rows[0:8, 2, :], rows[0:8, 0, :], 0.0, ALU.mult, ALU.max))
            link(V.scalar_tensor_tensor(out=rows[0:8, 2, :], in0=csum[:], scalar=-1.0, in1=rows[0:8, 1, :],
                                        op0=ALU.mult, op1=ALU.subtract))
            link(V.tensor_scalar(negM[0:MLH, :], rows[0:8, 1, :], -1.0, None, ALU.mult))
            V.scalar_tensor_tensor(out=negM[32:32 + MLH, :], in0=rows[0:8, 1, :], scalar=-1.0,
                                   in1=negM[0:MLH, :].bitcast(F32), op0=ALU.mult, op1=ALU.subtract).then_inc(rows_ok, 1)

            def silu_mul(u):
                dve.wait_ge(cv_sig, u + 1)
                V.scalar_tensor_tensor(out=mqk[:, u, :], in0=cacc[:, u % 2, :], scalar=1.0 if u < 4 else DK ** -0.5,
                                       in1=csig[:], op0=ALU.mult, op1=ALU.mult).then_inc(mqk_ok, 1)

            for u in range(U_CONV, U_MO):
                taken(dve, u)
                if u >= 2:
                    dve.wait_ge(mqk_ok, u - 1)
                cw = lambda t: cols[:, K_CW + DC * t + u:K_CW + DC * t + u + 1]
                link(V.tensor_scalar(cacc[:, u % 2, :], cpad[:, u % 2, TAPS - 1:], cw(TAPS - 1),
                                     cols[:, K_CB + u:K_CB + u + 1], ALU.mult, ALU.add))
                for t in range(TAPS - 1):
                    ins = V.scalar_tensor_tensor(out=cacc[:, u % 2, :], in0=cpad[:, u % 2, t:t + SEQ], scalar=cw(t),
                                                 in1=cacc[:, u % 2, :], op0=ALU.mult, op1=ALU.add)
                    if t < TAPS - 2:
                        link(ins)
                ins.then_inc(cv_acc, 1)
                if u >= 1:
                    silu_mul(u - 1)
                if u == 4:
                    dve.wait_ge(eT_t, 1)
                    V.tensor_copy(eT[:], ps[:, 3, 0:64].rearrange("p (a t h) -> p a t h", a=2, t=TT)).then_inc(eT_ok, 1)
            silu_mul(7)
            for u in range(U_MO, U_MV):
                if u == U_MO:
                    dve.wait_ge(flip_mm, 1)
                    V.tensor_copy(bias0[:, 0:2], ps[:, 3, :].rearrange("p (h w) -> p h w", h=2))
                    V.tensor_copy(bias0[:, 2:4], ps[:, 4, :].rearrange("p (h w) -> p h w", h=2))
                    V.tensor_copy(bias1[:], ps[:, 5, :].rearrange("p (h w) -> p h w", h=AH))
                    for b in range(4):
                        r = slice(32 * b, 32 * b + 32)
                        last = V.tensor_copy(bias2[r, :, r], ps[r, 6, :].rearrange("p (h w) -> p h w", h=AH)[:, :, r])
                    last.then_inc(bias_ok, 1)
                ada(8 + u - U_MO)
            dve.wait_ge(ada_t, 2)
            link(V.tensor_tensor(adac[:, 16:32], ps[:, 7, 16:32], cols[:, K_BADA + 16:K_BADA + 32], ALU.add))
            V.tensor_copy(gate1, adac[:, 16:24])
            V.tensor_copy(sh2, adac[:, 24:32])
            V.memset(vext[:, :, :, DV:DV + 1], 1.0).then_inc(ada_ok, 1)

            def m_gate(h):
                dve.wait_ge(ht_mm, h + 1)
                if h >= 1:
                    dve.wait_ge(h_hi, h)
                    dve.wait_ge(h_lo, h)
                V.scalar_tensor_tensor(out=hg[:], in0=ps[:, 4, :], scalar=cols[:, K_MG + h:K_MG + h + 1],
                                       in1=mo[:, h, :], op0=ALU.mult, op1=ALU.mult).then_inc(hg_ok, 1)

            def m_low(h):
                dve.wait_ge(hg_ok, h + 1)
                dve.wait_ge(h_hi, h + 1)
                V.tensor_tensor(hlo[:, h, :], hg[:], hhi[:, h, :].bitcast(F32), ALU.subtract).then_inc(h_lo, 1)

            def m_clamp(h):
                dve.wait_ge(bc_mm, h + 1)
                if h >= 1:
                    dve.wait_ge(ex_dg, h)
                for j in range(TT):
                    last = V.tensor_scalar(dcl[:, j, :], ps[:, 5, j * P:(j + 1) * P], eT[:, 0, j, h:h + 1], 0.0,
                                           ALU.add, ALU.min)
                last.then_inc(dc_ok, 1)

            def m_weights(h, j):
                bank, c0 = ((2, 0), (3, 0), (2, 0), (3, 384))[j]
                w = SEQ - j * P
                dve.wait_ge(ms_mm, 4 * h + (1, 3, 4, 3)[j])
                dve.wait_ge(ex_msk, h + 1)
                dve.wait_ge(ex_ok, h + 1)
                if h >= 2:
                    dve.wait_ge(num_mm, h - 1)
                V.tensor_tensor(wts[:, h % 2, EW[j]:EW[j + 1]], ps[:, bank, c0:c0 + w],
                                expd[:, j, j * P:], ALU.mult).then_inc(wt_ok, 1)

            def m_vext(h):
                dve.wait_ge(mv_t, h + 1)
                if h >= 2:
                    dve.wait_ge(num_mm, h - 1)
                V.tensor_copy(vext[:, h % 2, :, 0:DV], ps[:, 4, :].rearrange("p (t d) -> p t d", t=TT)).then_inc(vx_ok, 1)

            num = ps[:, 6:8, :].rearrange("p b (i w) -> p (b i) w", w=256)

            def m_norm(h):
                dve.wait_ge(num_mm, h + 1)
                V.tensor_copy(nq, num[:, :, DV]).then_inc(nq_ok, 1)
                dve.wait_ge(nq_ok, h + 1)
                link(V.scalar_tensor_tensor(out=nd, in0=nq, scalar=-1.0, in1=nq, op0=ALU.mult, op1=ALU.max))
                dve.wait_ge(em_ok, 1)
                link(V.tensor_tensor(nd, nd, emT[:, :, h], ALU.max))
                link(V.reciprocal(nr, nd))
                link(V.tensor_tensor(nd, nr, nr, ALU.mult))
                dve.wait_ge(nsq, h + 1)
                V.tensor_tensor(nv, ss, nd, ALU.mult).then_inc(nrr, 1)
                dve.wait_ge(nrs, h + 1)
                link(V.tensor_tensor(nf, nr, nv, ALU.mult))
                V.tensor_tensor(hn[:], num[:, :, 0:DV], nf.unsqueeze(2).to_broadcast([P, TT, DV]), ALU.mult).then_inc(
                    hn_ok, 1)

            for h in range(MLH):
                if h >= 2:
                    m_gate(h - 2)
                m_clamp(h)
                m_weights(h, 0)
                m_weights(h, 1)
                m_weights(h, 3)
                m_vext(h)
                if h >= 1:
                    m_norm(h - 1)
                m_weights(h, 2)
                if h >= 2:
                    m_low(h - 2)

            def scores(j):
                g, h = j % NG, j // NG
                dve.wait_ge(sc_mm, j + 1)
                if j >= 1:
                    dve.wait_ge(pr_ok, j)
                if g == 0:
                    S = ps[:, 2:4, :].rearrange("p b (i w) -> p (b i) w", w=2 * P)
                    V.tensor_tensor(sbias[:, 0, P:], S[:, 0, P:], bias0[:, h, P:], ALU.add)
                    link(V.tensor_tensor(sbias[:, 1:], S[:, 1:], bias0[:, h:h + 1, :].to_broadcast([P, 3, 2 * P]),
                                         ALU.add))
                    V.tensor_reduce(mx[:, 0:1], sbias[:, 0, P:], AX.X, ALU.max)
                    link(V.tensor_reduce(mx[:, 1:4], sbias[:, 1:], AX.X, ALU.max))
                else:
                    S = ps[:, 2, :].rearrange("p (i w) -> p i w", w=P)
                    b = (bias1 if g == 1 else bias2)[:, h:h + 1, :]
                    link(V.tensor_tensor(sbias[:, :, 0:P], S, b.to_broadcast([P, TT, P]), ALU.add))
                    link(V.tensor_reduce(mx, sbias[:, :, 0:P], AX.X, ALU.max))
                V.tensor_scalar(stats[:, 0, g, :, h], mx, -1.0, None, ALU.mult).then_inc(mx_ok, 1)

            def normed(n):
                j, part = divmod(n, 2)
                dil = GROUPS[j % NG][1]
                dve.wait_ge(qk_rs, n + 1)
                if j >= 1:
                    dve.wait_ge(sc_mm, j)
                dst, gain = ((qn, qgs), (kn, cols[:, K_KG:K_KG + 1]))[part]
                view = lambda a: a.rearrange("p (s r) -> p s r", r=dil)
                V.scalar_tensor_tensor(out=dst[:].rearrange("p (r s) -> p s r", r=dil), in0=view(qf[:, part, :]),
                                       scalar=gain, in1=view(rsb[:, part, :]), op0=ALU.mult, op1=ALU.mult).then_inc(
                    qk_n, 1)

            def sq_low(n):
                u = U_ATT + 3 * (n // 2) + n % 2
                taken(dve, u)
                if n >= 1:
                    dve.wait_ge(qk_ss, n)
                link(V.tensor_tensor(sqf[:], qf[:, n % 2, :], qf[:, n % 2, :], ALU.mult))
                V.tensor_tensor(sqlo[:], sqf[:], sqhi[:, n % 2, :].bitcast(F32), ALU.subtract).then_inc(sq_lo, 1)
                dve.wait_ge(sq_lo, n + 1)

            def v_copy(j):
                u = U_ATT + 3 * j + 2
                dil = GROUPS[j % NG][1]
                dve.wait_ge(unit_done, u + 1)
                if j >= 1:
                    dve.wait_ge(vt_mm, j)
                V.tensor_copy(vTp[:].rearrange("p (r s) -> p s r", r=dil),
                              G(u).rearrange("p (s r) -> p s r", r=dil)).then_inc(bank_read[u % 2], 1)

            def v_tok(j):
                dve.wait_ge(vt_mm, j + 1)
                if j >= 2:
                    dve.wait_ge(pv_mm, j - 1)
                V.tensor_copy(vtok[:, j % 2], ps[:, 4, :].rearrange("p (t d) -> p t d", t=TT)).then_inc(vt_ok, 1)

            def p_copy(j):
                n = 7 if j % NG == 0 else 4
                dve.wait_ge(pt_mm, j + 1)
                if j >= 1:
                    dve.wait_ge(pv_mm, j)
                V.tensor_copy(probT[:, 0:n, :],
                              ps[:, 4:6, :].rearrange("p b (i w) -> p (b i) w", w=P)[:, 0:n]).then_inc(pt_ok, 1)

            for s in range(36):
                j, part = divmod(s, 3)
                if s == 0:
                    m_gate(6)
                    m_low(6)
                    m_norm(7)
                if s == 1:
                    m_gate(7)
                    m_low(7)
                if part == 0:
                    sq_low(2 * j)
                if part == 0 and j >= 1:
                    v_tok(j - 1)
                    scores(j - 1)
                if part == 1:
                    sq_low(2 * j + 1)
                    normed(2 * j)
                if part == 2:
                    v_copy(j)
                    normed(2 * j + 1)
                    if j >= 1:
                        p_copy(j - 1)

            def turn(g):
                dil = GROUPS[g][1]
                dve.wait_ge(st_mm, g + 1)
                for dst, b in ((mrow, 2 + 2 * g), (lrow, 3 + 2 * g)):
                    last = V.tensor_copy(dst[:, g, :].rearrange("p (s r) -> p s r", r=dil),
                                         ps[0:AH, b, :].rearrange("p (r s) -> p s r", r=dil))
                last.then_inc(st_ok, 1)

            def weigh_exponents():
                dve.wait_ge(st_ok, NG)
                link(V.tensor_tensor(mtop[:], mrow[:, 0], mrow[:, 1], ALU.min))
                link(V.tensor_tensor(mtop[:], mtop[:], mrow[:, 2], ALU.min))
                V.tensor_tensor(mrow[:], mtop[:].unsqueeze(1).to_broadcast([AH, NG, SEQ]), mrow[:], ALU.subtract).then_inc(
                    md_ok, 1)

            def weigh_sum():
                dve.wait_ge(me_ok, 1)
                link(V.tensor_tensor(lrow[:], lrow[:], mrow[:], ALU.mult))
                link(V.tensor_tensor(mtop[:], lrow[:, 0], lrow[:, 1], ALU.add))
                link(V.tensor_tensor(mtop[:], mtop[:], lrow[:, 2], ALU.add))
                link(V.reciprocal(mrec[:], mtop[:]))
                link(V.tensor_tensor(mrow[:], mrow[:], mrec[:].unsqueeze(1).to_broadcast([AH, NG, SEQ]), ALU.mult))
                link(V.memset(mrr[:].bitcast(F32), 0.0))

            def weigh_split():
                link(V.tensor_copy(mrr[0:AH], mrow[:]))
                V.tensor_tensor(mrr[32:32 + AH], mrow[:], mrr[0:AH].bitcast(F32), ALU.subtract).then_inc(mw_ok, 1)

            def merge(h):
                dve.wait_ge(mw_ok, 1)
                dve.wait_ge(mb_mm, h + 1)
                if h >= 1:
                    dve.wait_ge(a_hi, h)
                    dve.wait_ge(a_lo, h)
                else:
                    dve.wait_ge(o_ok, NG * AH)
                for g in range(NG):
                    last = V.tensor_tensor(mtmp[:, g, :], ps[:, 4 + g, :], outT[:, NG * h + g, :], ALU.mult)
                last.then_inc(mb_rd, 1)
                dve.wait_ge(mb_rd, h + 1)
                link(V.tensor_tensor(mtmp[:, 0, :], mtmp[:, 0, :], mtmp[:, 1, :], ALU.add))
                V.tensor_tensor(mtmp[:, 0, :], mtmp[:, 0, :], mtmp[:, 2, :], ALU.add).then_inc(att_f, 1)

            for t in range(16):
                u = U_YML + t
                n, part = divmod(t, 2)
                if part == 1:
                    dve.wait_ge(unit_done, u + 1)
                    taken(dve, u - 1)
                    V.tensor_tensor(yml[:, n, :], G(u), gsig[:], ALU.mult).then_inc(bank_read[u % 2], 1)
                if t == 5:
                    weigh_sum()
                if t == 7:
                    weigh_split()
                if t == 0:
                    v_tok(11)
                    scores(11)
                if t == 2:
                    p_copy(11)
                if t == 4:
                    for g in range(NG):
                        turn(g)
                    weigh_exponents()
                if t >= 8 and t % 2 == 0:
                    merge((t - 8) // 2)
                if t >= 9 and t % 2 == 1:
                    h = (t - 9) // 2
                    dve.wait_ge(a_hi, h + 1)
                    V.tensor_tensor(alo[:, h, :], mtmp[:, 0, :], ahi[:, h, :].bitcast(F32), ALU.subtract).then_inc(a_lo, 1)
            for n in range(DC):
                u = U_YATT + 2 * n + 1
                dve.wait_ge(unit_done, u + 1)
                taken(dve, u - 1)
                yb = ybuf[:, n % 2, :]
                if n >= 2:
                    dve.wait_ge(y_hi, n - 1)
                    dve.wait_ge(y_lo, n - 1)
                V.tensor_tensor(yb, G(u), gsig[:], ALU.mult).then_inc(bank_read[u % 2], 1)
                taken(dve, u)
                V.tensor_tensor(yb, yb, yml[:, n, :], ALU.add).then_inc(y_ok, 1)
                dve.wait_ge(y_ok, n + 1)
                dve.wait_ge(y_hi, n + 1)
                V.tensor_tensor(ylo[:, n, :], yb, yhi[:, n, :].bitcast(F32), ALU.subtract).then_inc(y_lo, 1)
                ada(16 + n)
            dve.wait_ge(ada_t, 3)
            link(V.tensor_tensor(adac[:, 32:48], ps[:, 7, 32:48], cols[:, K_BADA + 32:K_BADA + 48], ALU.add))
            link(V.scalar_tensor_tensor(out=a2, in0=adac[:, 32:40], scalar=1.0, in1=cols[:, K_N2:K_N2 + DC],
                                        op0=ALU.add, op1=ALU.mult))
            link(V.tensor_copy(gate2, adac[:, 40:48]))
            for n in range(DC):
                u = U_OUT + n
                dve.wait_ge(unit_done, u + 1)
                V.scalar_tensor_tensor(out=xT[:, n, :], in0=G(u), scalar=gate1[:, n:n + 1], in1=xT[:, n, :],
                                       op0=ALU.mult, op1=ALU.add).then_inc(bank_read[u % 2], 1)
                taken(dve, u)
                V.tensor_scalar(xa[:, n, :], xT[:, n, :], a2[:, n:n + 1], None, ALU.mult).then_inc(xa_ok, 1)
                if 1 <= n < DC - 1:
                    dve.wait_ge(s2_ok, n + 1)
                    V.tensor_tensor(sqacc[:], sqacc[:], sq2[:, n % 2, :], ALU.add).then_inc(s2_add, 1)
                    dve.wait_ge(s2_add, n)
            dve.wait_ge(r2_ok, 1)
            for d in range(DC + 2):
                if d < DC and d % 2 == 0:
                    V.tensor_tensor(xa[:, d, :], xa[:, d, :], rs2[:], ALU.mult).then_inc(v_f, 1)
                if d >= 2:
                    k = d - 2
                    dve.wait_ge(v_hi, k + 1)
                    V.scalar_tensor_tensor(out=ulo[:, k, :], in0=xa[:, k, :], scalar=sh2[:, k:k + 1],
                                           in1=uhi[:, k, :].bitcast(F32), op0=ALU.add, op1=ALU.subtract).then_inc(
                        v_lo, 1)
            for q in range(4):
                for j in range(8):
                    n = 8 * q + j
                    taken(dve, U_FF + 16 * q + j)
                    link(V.tensor_tensor(r2buf[:], rbuf[:, j % 2, :], rbuf[:, j % 2, :], ALU.mult))
                    dve.wait_ge(f_hi, n + 1)
                    V.tensor_tensor(hlo[:, j, :], r2buf[:], hhi[:, j, :].bitcast(F32), ALU.subtract).then_inc(f_lo, 1)
                    dve.wait_ge(f_lo, n + 1)
                for j in range(8):
                    n = 8 * q + j
                    u = U_FF + 16 * q + 8 + j
                    dve.wait_ge(unit_done, u + 1)
                    if q:
                        taken(dve, u - 16)
                    V.scalar_tensor_tensor(out=xT[:, j, :], in0=G(u), scalar=gate2[:, j:j + 1], in1=xT[:, j, :],
                                           op0=ALU.mult, op1=ALU.add).then_inc(bank_read[u % 2], 1)

        @block.tensor
        def _(pe):
            T = nc.tensor
            pe.wait_ge(c_in, 16)
            pe.wait_ge(identity_ok, 1)
            T.transpose(ps[:, 7, 0:DC], crow[:], ident[0:DC, 0:DC]).then_inc(c_t, 1)
            pe.wait_ge(x_in, 16)
            pe.wait_ge(consts, 1)
            for d in range(DC):
                if d >= 4:
                    pe.wait_ge(x_sq, d - 3)
                for t in range(TT):
                    last = T.transpose(ps[:, d % 4, t * P:(t + 1) * P], xtok[:, t, d * P:(d + 1) * P], ident[:])
                last.then_inc(x_t, 1)
                if d >= 1:
                    pe.wait_ge(x_sq, d)
                    T.matmul(ps[:, 6, :], ones[:], n1sq[:, (d - 1) % 2, :], start=d == 1, stop=False).then_inc(x_ss, 1)
            pe.wait_ge(x_sq, DC)
            T.matmul(ps[:, 6, :], ones[:], n1sq[:, (DC - 1) % 2, :], start=False, stop=True).then_inc(x_ss, 1)
            pe.wait_ge(vec_in, 16 * 8)
            T.transpose(ps[:, 4, 0:N_VEC], vrows[0:N_VEC, :], ident[0:N_VEC, 0:N_VEC]).then_inc(vec_t, 1)
            pe.wait_ge(oh_in, 32)
            pe.wait_ge(vec_c, 1)
            T.matmul(ps[0:NG * AH, 5, :], relb[:], onehot[:, 0:512], start=True, stop=True)
            T.matmul(ps[0:NG * AH, 4, 0:TSUM - 512], relb[:], onehot[:, 512:TSUM], start=True, stop=True).then_inc(
                fr_mm, 1)
            def keep_warm(n):
                for _ in range(n):
                    T.matmul(ps[:, 3, :], ones[:], xT[:, 0, :], start=True, stop=True)

            keep_warm(WARM)
            pe.wait_ge(ada_acc, 8)
            for i in range(16):
                last = T.matmul(ps[:, 7, i:i + 1], ada1[:, i * P:(i + 1) * P], ones[:, 0:1], start=True, stop=True)
            last.then_inc(ada_t, 1)
            keep_warm(WARM2)
            pe.wait_ge(if_lo, 1)
            for k in range(DC):
                pe.wait_ge(u_lo, k + 1)
                for bank, hi, lo, done in ((2, ifhi[:, k, :], iflo[:, k, :], if_mm),
                                           (0, whi[:, 0, k, :], wlo[:, 0, k, :], unit_done)):
                    if k == 0 and bank == 0:
                        pe.wait_ge(w_lo, 1)
                    T.matmul(ps[:, bank, :], hi, uhi[:, k, :], start=k == 0, stop=False)
                    T.matmul(ps[:, bank, :], hi, ulo[:, k, :], start=False, stop=False)
                    last = T.matmul(ps[:, bank, :], lo, uhi[:, k, :], start=False, stop=k == DC - 1)
                    if k == DC - 1:
                        last.then_inc(done, 1)

            def unit(u, mhi, mlo, ready=None, amid=None):
                pe.wait_ge(w_lo, u + 1)
                if u >= 2:
                    taken(pe, u - 2)
                kc, s, b = kchunks(u), u % RING, u % 2
                for k in range(kc):
                    if ready is not None:
                        pe.wait_ge(ready[0], ready[1] + k + 1)
                    T.matmul(ps[:, b, :], whi[:, s, k, :], mhi[:, k, :], start=k == 0, stop=False)
                    T.matmul(ps[:, b, :], whi[:, s, k, :], mlo[:, k, :], start=False, stop=False)
                    last = T.matmul(ps[:, b, :], wlo[:, s, k, :], mhi[:, k, :], start=False, stop=k == kc - 1)
                    if amid and k == 2:
                        amid()
                last.then_inc(unit_done, 1)

            for u in range(U_CONV + 1, U_MV):
                unit(u, uhi, ulo)
                if u == 4:
                    pe.wait_ge(rows_ok, 1)
                    for a, r in ((0, 0), (1, 2)):
                        for t in range(TT):
                            last = T.transpose(ps[:, 3, 32 * a + 8 * t:32 * a + 8 * t + 8],
                                               rows[0:8, r, t * P:(t + 1) * P], ident[0:8, 0:8])
                    last.then_inc(eT_t, 1)
                if u == 7:
                    pe.wait_ge(stage_in, 48)
                    pe.wait_ge(identity_ok, 2)
                    pe.wait_ge(eT_ok, 1)
                    for h in range(AH):
                        T.matmul(ps[:, 3 + h // 2, 256 * (h % 2):256 * (h % 2) + 256], flip[:], stage[:, h, 0:2 * P],
                                 start=True, stop=True)
                    for h in range(AH):
                        T.matmul(ps[:, 5, P * h:P * h + P], flip[:], stage[:, h, 2 * P:3 * P], start=True, stop=True)
                    for h in range(AH):
                        last = T.matmul(ps[:, 6, P * h:P * h + P], flip[:], stage[:, h, 3 * P:], start=True, stop=True)
                    last.then_inc(flip_mm, 1)

            def m_scores(h, j):
                bank, c0 = ((2, 0), (3, 0), (2, 0), (3, 384))[j]
                w = SEQ - j * P
                if j == 2:
                    pe.wait_ge(wt_ok, 4 * h + 1)
                k = kst[h % 2][:, j * P:(j + 1) * P]
                T.matmul(ps[:, bank, c0:c0 + w], k, qst[h % 2][:, j * P:], start=True, stop=False)
                T.matmul(ps[:, bank, c0:c0 + w], k, qsw[h % 2][:, j * P:], start=False, stop=True).then_inc(ms_mm, 1)

            def m_turn(h):
                pe.wait_ge(hn_ok, h + 1)
                for t in range(TT):
                    last = T.transpose(ps[:, 4, t * P:(t + 1) * P], hn[:, t, :], ident[:])
                last.then_inc(ht_mm, 1)

            def m_num(h):
                pe.wait_ge(wt_ok, 4 * (h + 1))
                pe.wait_ge(vx_ok, h + 1)
                if h >= 1:
                    pe.wait_ge(hn_ok, h)
                for i in range(TT):
                    for j in range(i + 1):
                        c0 = EW[j] + (i - j) * P
                        last = T.matmul(ps[:, 6 + i // 2, (i % 2) * 256:(i % 2) * 256 + DV + 1], wts[:, h % 2, c0:c0 + P],
                                        vext[:, h % 2, j, :], start=j == 0, stop=j == i)
                last.then_inc(num_mm, 1)

            for h in range(MLH):
                unit(U_MV + h, uhi, ulo, amid=(lambda: m_scores(h - 1, 2)) if h else None)
                if h == 0:
                    pe.wait_ge(ada_acc, 16)
                    for i in range(16):
                        last = T.matmul(ps[:, 7, 16 + i:17 + i], ada2[:, i * P:(i + 1) * P], ones[:, 0:1], start=True,
                                        stop=True)
                    last.then_inc(ada_t, 1)
                    pe.wait_ge(bias_ok, 1)
                    pe.wait_ge(ada_ok, 2)
                else:
                    pe.wait_ge(ex_ok, h)
                if h >= 2:
                    m_turn(h - 2)
                T.matmul(ps[:, 5, :], selr[:, h:h + 1].to_broadcast([32 + MLH, P]), negM[:], start=True,
                         stop=True).then_inc(bc_mm, 1)
                pe.wait_ge(st_lo, 3 * (h + 1))
                if h:
                    pe.wait_ge(wt_ok, 4 * h)
                m_scores(h, 0)
                m_scores(h, 1)
                m_scores(h, 3)
                if h >= 2:
                    pe.wait_ge(hg_ok, h - 1)
                if h >= 1:
                    pe.wait_ge(vx_ok, h)
                taken(pe, U_MV + h)
                for t in range(TT):
                    last = T.transpose(ps[:, 4, t * P:(t + 1) * P], mvT[:, t * P:(t + 1) * P], ident[:])
                last.then_inc(mv_t, 1)
                if h >= 1:
                    m_num(h - 1)

            def v_turn(j):
                taken(pe, U_ATT + 3 * j + 2)
                if j >= 1:
                    pe.wait_ge(pt_ok, j)
                for t in range(TT):
                    last = T.transpose(ps[:, 4, t * P:(t + 1) * P], vTp[:, t * P:(t + 1) * P], ident[:])
                last.then_inc(vt_mm, 1)

            def scores(j):
                pe.wait_ge(qk_n, 2 * (j + 1))
                if j >= 1:
                    pe.wait_ge(mx_ok, j)
                for t in range(TT):
                    q = qn[:, t * P:(t + 1) * P]
                    if j % NG == 0:
                        lo = P if t == 0 else 0
                        o = ps[:, 2 + t // 2, (t % 2) * 256 + lo:(t % 2) * 256 + 256]
                        last = T.matmul(o, q, kn[:, t * P - P + lo:(t + 1) * P], start=True, stop=True)
                    else:
                        last = T.matmul(ps[:, 2, t * P:(t + 1) * P], q, kn[:, t * P:(t + 1) * P], start=True, stop=True)
                last.then_inc(sc_mm, 1)

            def p_turn(j):
                pe.wait_ge(pr_ok, j + 1)
                pe.wait_ge(vt_ok, j + 1)
                slot = 0
                for t in range(TT):
                    for half in ((0, 1) if j % NG == 0 and t else (1,)):
                        c0 = half * P if j % NG == 0 else 0
                        last = T.transpose(ps[:, 4 + slot // 4, (slot % 4) * P:(slot % 4 + 1) * P],
                                           prob[:, t, c0:c0 + P], ident[:])
                        slot += 1
                last.then_inc(pt_mm, 1)

            def p_v(j):
                pe.wait_ge(pt_ok, j + 1)
                if j >= 1:
                    pe.wait_ge(o_ok, j)
                for t in range(TT):
                    o = ps[:, 7, t * P:(t + 1) * P]
                    if j % NG == 0 and t:
                        T.matmul(o, vtok[:, j % 2, t - 1], probT[:, 2 * t - 1], start=True, stop=False)
                        last = T.matmul(o, vtok[:, j % 2, t], probT[:, 2 * t], start=False, stop=True)
                    else:
                        last = T.matmul(o, vtok[:, j % 2, t], probT[:, t if j % NG else 0], start=True, stop=True)
                last.then_inc(pv_mm, 1)

            def sumsq(n):
                taken(pe, U_ATT + 3 * (n // 2) + n % 2)
                if n >= 1:
                    pe.wait_ge(qk_rs, n)
                else:
                    pe.wait_ge(hn_ok, MLH)
                pe.wait_ge(sq_lo, n + 1)
                T.matmul(ps[:, 6, :], onesr[:], sqhi[:, n % 2, :], start=True, stop=False)
                T.matmul(ps[:, 6, :], onesr[:], sqlo[:], start=False, stop=True).then_inc(qk_ss, 1)

            for s in range(36):
                j, part = divmod(s, 3)
                unit(U_ATT + s, uhi, ulo, amid=(lambda: m_scores(MLH - 1, 2)) if s == 0 else None)
                if s == 0:
                    m_turn(6)
                    m_num(7)
                if s == 1:
                    pe.wait_ge(hg_ok, 7)
                    m_turn(7)
                if part == 0 and j >= 1:
                    if j == 1:
                        pe.wait_ge(hg_ok, 8)
                    v_turn(j - 1)
                    scores(j - 1)
                if part == 0 and j >= 2:
                    p_v(j - 2)
                if part == 1:
                    sumsq(2 * j)
                if part == 2:
                    sumsq(2 * j + 1)
                    if j >= 1:
                        p_turn(j - 1)

            for t in range(16):
                n, part = divmod(t, 2)
                if part == 0:
                    unit(U_YML + t, uhi, ulo)
                else:
                    unit(U_YML + t, hhi, hlo, (h_lo, 0) if t == 1 else None)
                if t == 0:
                    v_turn(11)
                    scores(11)
                    p_v(10)
                if t == 2:
                    p_turn(11)
                if t == 3:
                    p_v(11)
                if t == 4:
                    pe.wait_ge(o_ok, NG * AH)
                    for g in range(NG):
                        for a in range(2):
                            for i in range(TT):
                                last = T.matmul(ps[0:AH, 2 + 2 * g + a, i * P:(i + 1) * P], stats[:, a, g, i, :],
                                                ident[:], start=True, stop=True)
                        last.then_inc(st_mm, 1)
                if t >= 8 and t % 2 == 0:
                    h = (t - 8) // 2
                    pe.wait_ge(mw_ok, 1)
                    if h:
                        pe.wait_ge(mb_rd, h)
                    for g in range(NG):
                        last = T.matmul(ps[:, 4 + g, :], selr[0:32 + AH, h:h + 1].to_broadcast([32 + AH, P]),
                                        mrr[:, g, :], start=True, stop=True)
                    last.then_inc(mb_mm, 1)
            for t in range(16):
                if t % 2 == 0:
                    unit(U_YATT + t, uhi, ulo)
                else:
                    unit(U_YATT + t, ahi, alo, (a_lo, 0) if t == 1 else None)
            for n in range(DC):
                unit(U_OUT + n, yhi, ylo, (y_lo, 0) if n == 0 else None)
                if n == 0:
                    pe.wait_ge(ada_acc, 24)
                    for i in range(16):
                        last = T.matmul(ps[:, 7, 32 + i:33 + i], ada3[:, i * P:(i + 1) * P], ones[:, 0:1], start=True,
                                        stop=True)
                    last.then_inc(ada_t, 1)
            pe.wait_ge(s2_add, DC - 2)
            T.matmul(ps[:, 6, :], ones[:], sqacc[:], start=True, stop=False)
            pe.wait_ge(s2_ok, DC)
            T.matmul(ps[:, 6, :], ones[:], sq2[:, (DC - 1) % 2, :], start=False, stop=True).then_inc(s2_mm, 1)
            keep_warm(4)

            def x_turn(n):
                taken(pe, U_FF + 56 + n)
                if n >= 2:
                    pe.wait_ge(xo_ok, n - 1)
                for t in range(TT):
                    last = T.transpose(ps[:, 4 + n % 2, t * P:(t + 1) * P], xT[:, n, t * P:(t + 1) * P], ident[:])
                last.then_inc(xo_mm, 1)

            for q in range(4):
                for j in range(8):
                    unit(U_FF + 16 * q + j, uhi, ulo, (v_lo, 0) if q == 0 and j == 0 else None)
                for j in range(8):
                    unit(U_FF + 16 * q + 8 + j, hhi, hlo, (f_lo, 8 * q) if j == 0 else None)
                    if q == 3 and j >= 1:
                        x_turn(j - 1)
            x_turn(DC - 1)


_INS = ['x', 'c', 'w_ada', 'b_ada', 'norm1_g', 'norm2_g', 'w_in', 'b_if', 'conv_w', 'conv_b', 'q_norm_g', 'k_norm_g',
        'rel_bias', 'mlstm_norm_g', 'w_att_out', 'w_ml_out', 'w_out', 'w_ff1', 'w_ff2']
_OUTS = [((1, SEQ, D), 'float32')]


def kernel(**inputs):
    import numpy as _np
    import concourse.bacc as _bacc
    from concourse import mybir as _mybir
    from concourse.bass_utils import run_bass_kernel_spmd as _run

    nc = _bacc.Bacc("TRN2", target_bir_lowering=False, num_devices=1)
    arrays, args = {}, []
    data = [(name, _np.ascontiguousarray(inputs[name])) for name in _INS] + [("one_hot", bucket_one_hot())]
    for name, a in data:
        arrays[f"in_{name}_dram"] = a
        args.append(nc.dram_tensor(f"in_{name}_dram", a.shape, _mybir.dt.from_np(a.dtype), kind="ExternalInput").ap())
    for i, (shape, dtype) in enumerate(_OUTS):
        dt = _mybir.dt.from_np(_np.dtype(dtype))
        args.append(nc.dram_tensor(f"out_{i}_dram", shape, dt, kind="ExternalOutput").ap())
    block_kernel(nc, *args)
    r = _run(nc, [arrays], core_ids=[0])
    got = tuple(r.results[0][f"out_{i}_dram"] for i in range(len(_OUTS)))
    return got[0]
```

```python
from contextlib import ExitStack
import math

import numpy as np

import concourse.bass as bass
from concourse import mybir

ALU = mybir.AluOpType
ACT = mybir.ActivationFunctionType
AX = mybir.AxisListType
F32 = mybir.dt.float32
F32R = mybir.dt.float32r

P = 128
KB = 1024
SEQ = 512
D = 1024
DC = D // P
TT = SEQ // P
NBUCK = 32
MAXDIST = 2048
GROUPS = ((128, 1), (512, 4), (2048, 16))
NG = 3
AH = 4
DH = 128
MLH = 8
DK = 64
DV = 128
TAPS = 4
EPS = 1e-6
NEG = -1e30
C_AQ, C_AK, C_AV = 0, NG * AH * DH, 2 * NG * AH * DH
C_MQ = 3 * NG * AH * DH
C_MV = C_MQ + 2 * MLH * DK
C_MO = C_MV + MLH * DV
C_MI = C_MO + MLH * DV
C_MF = C_MI + MLH
C_GA = C_MF + MLH
C_GB = C_GA + D
TW = (3 * P - 1, 2 * P - 1, 2 * P - 1)
TO = (0, TW[0], TW[0] + TW[1])
TSUM = sum(TW)

U_CONV = 0
U_MO = 8
U_MV = 16
U_ATT = 24
U_YML = 60
U_YATT = 76
U_OUT = 92
U_FF = 100
RING = 4
NQ = 4
QU = 2 * DC
QT = QU // RING
WARM = 5
WARM2 = 2


def bucket_of(dist):
    exact = NBUCK // 2
    d = np.maximum(dist, exact).astype(np.float32)
    large = exact + (np.log(d / np.float32(exact)) / np.float32(math.log(MAXDIST / exact))
                     * np.float32(NBUCK - exact)).astype(np.int32)
    return np.where(dist < exact, dist, np.minimum(large, NBUCK - 1))


def bucket_one_hot():
    m = np.zeros((NBUCK + 1, TSUM), np.float32)
    for g, (window, dil) in enumerate(GROUPS):
        for x in range(TW[g]):
            delta = (2 * P - 1 if g == 0 else P - 1) - x
            if 0 <= delta <= window // dil:
                m[int(bucket_of(np.array(delta * dil))), TO[g] + x] = 1.0
            else:
                m[NBUCK, TO[g] + x] = NEG
    return m


def block_kernel(nc, x, c, w_ada, b_ada, norm1_g, norm2_g, w_in, b_if, conv_w, conv_b, q_norm_g, k_norm_g,
                 rel_bias, mlstm_norm_g, w_att_out, w_ml_out, w_out, w_ff1, w_ff2, one_hot, out):
    base = nc.sbuf_base + (-nc.sbuf_base) % 64
    limit = nc.sbuf_usable_end

    def at(name, kb, shape, dt=F32):
        off = base + int(kb * KB)
        assert off + 4 * int(np.prod(shape[1:])) <= limit, name
        return nc.alloc_sbuf_tensor_at(name, shape, dt, offset=off)

    xT = at("xT", 0, [P, DC, SEQ])
    wraw = at("wraw", 16, [P, RING, DC, P])
    whi = at("whi", 32, [P, RING, DC, P], F32R)
    wlo = at("wlo", 48, [P, RING, DC, P], F32R)
    uhi = at("uhi", 64, [P, DC, SEQ], F32R)
    ulo = at("ulo", 80, [P, DC, SEQ], F32R)
    hhi = at("hhi", 96, [P, DC, SEQ], F32R)
    hlo = at("hlo", 112, [P, DC, SEQ], F32R)
    ada1 = at("ada1", 96, [P, 2 * D])
    ada2 = at("ada2", 96, [P, 2 * D])
    vrows = at("vrows", 120, [P, P])
    crow = at("crow", 194.25, [DC, P])
    flip = at("flip", 120, [P, P])
    rows = at("rows", 120.5, [P, 3, SEQ])
    onehot = at("onehot", 124, [NBUCK + 1, TSUM])
    relb = at("relb", 127.75, [NBUCK + 1, NG * AH])
    xtok = at("xtok", 128, [P, TT, D])
    xn = at("xn", 128, [P, DC, SEQ])
    ifraw = at("ifraw", 144, [P, DC, P])
    ifhi = at("ifhi", 148, [P, DC, P], F32R)
    iflo = at("iflo", 152, [P, DC, P], F32R)
    stage = at("stage", 144, [P, AH, 4 * P])
    n1sq = at("n1sq", 184, [P, 2, SEQ])
    n1t = at("n1t", 188, [P, 2, SEQ])
    n1rs = at("n1rs", 192, [P, SEQ])
    adabuf = at("adabuf", 160, [P, 3, 2 * D])
    adabuf3 = at("adabuf3", 104, [P, 3, 2 * D])
    ada3 = at("ada3", 96, [P, 2 * D])
    mqk = at("mqk", 128, [P, DC, SEQ])
    mo = at("mo", 144, [P, DC, SEQ])
    cpad = at("cpad", 184, [P, 2, SEQ + TAPS - 1])
    cacc = at("cacc", 188.0625, [P, 2, SEQ])
    csig = at("csig", 192.0625, [P, SEQ])
    csum = at("csum", 116, [MLH, SEQ])
    frow = at("frow", 156, [NG * AH, TSUM])
    negM = at("negM", 194.125, [32 + MLH, SEQ], F32R)
    EW = (0, 512, 896, 1152, 1280)
    expd = at("expd", 160, [P, TT, SEQ])
    dcl = at("dcl", 168, [P, TT, P])
    wts = at("wts", 170, [P, 2, EW[4]])
    vext = at("vext", 180, [P, 2, TT, DV + 1])
    mvT = at("mvT", 184.125, [P, SEQ])
    hn = at("hn", 186.125, [P, TT, DV])
    hg = at("hg", 188.125, [P, SEQ])
    kst = [at(f"kst{i}", o, [P, SEQ], F32R) for i, o in enumerate((108, 124))]
    qst = [at(f"qst{i}", o, [P, SEQ], F32R) for i, o in enumerate((110, 126))]
    qsw = [at(f"qsw{i}", o, [P, SEQ], F32R) for i, o in enumerate((190.125, 192.125))]
    qf = at("qf", 128, [P, 2, SEQ])
    sqhi = at("sqhi", 132, [P, 2, SEQ], F32R)
    sqf = at("sqf", 190.125, [P, SEQ])
    sqlo = at("sqlo", 192.125, [P, SEQ], F32R)
    rsb = at("rsb", 136, [P, 2, SEQ])
    qn = at("qn", 140, [P, SEQ])
    kn = at("kn", 142, [P, SEQ])
    outT = at("outT", 144, [P, NG * AH, SEQ])
    vTp = at("vTp", 168, [P, SEQ])
    vtok = at("vtok", 170, [P, 2, TT, DH])
    sbias = at("sbias", 174, [P, TT, 2 * P])
    prob = at("prob", 178, [P, TT, 2 * P])
    probT = at("probT", 182, [P, 7, P])
    bias0 = at("bias0", 196.125, [P, AH, 2 * P])
    bias1 = at("bias1", 200.125, [P, AH, P])
    bias2 = at("bias2", 202.125, [P, AH, P])
    ahi = at("ahi", 128, [P, AH, SEQ], F32R)
    alo = at("alo", 136, [P, AH, SEQ], F32R)
    mrow = at("mrow", 168, [AH, NG, SEQ])
    lrow = at("lrow", 174, [AH, NG, SEQ])
    mtop = at("mtop", 180, [AH, SEQ])
    mrec = at("mrec", 182, [AH, SEQ])
    mtmp = at("mtmp", 168, [P, 3, SEQ])
    mrr = at("mrr", 174, [32 + AH, NG, SEQ], F32R)
    gsig = at("gsig", 186, [P, SEQ])
    yml = at("yml", 188, [P, DC, SEQ])
    yhi = at("yhi", 144, [P, DC, SEQ], F32R)
    ylo = at("ylo", 160, [P, DC, SEQ], F32R)
    ybuf = at("ybuf", 176, [P, 2, SEQ])
    sq2 = at("sq2", 128, [P, 2, SEQ])
    rs2 = at("rs2", 132, [P, SEQ])
    sqacc = at("sqacc", 134, [P, SEQ])
    xa = at("xa", 96, [P, DC, SEQ])
    rbuf = at("rbuf", 138, [P, 2, SEQ])
    r2buf = at("r2buf", 142, [P, SEQ])
    obuf = at("obuf", 144, [P, 2, TT, P])
    CO = 204.25
    ident = at("ident", CO, [P, P])
    ones = at("ones", CO + 0.5, [P, P])
    cols = at("cols", CO + 1, [P, P])
    adac = at("adac", CO + 1.5, [P, 48])
    small = at("small", CO + 1.75, [P, 112])
    eT = at("eT", CO + 2.25, [P, 2, TT, MLH])
    stats = at("stats", CO + 2.5, [P, 2, NG, TT, AH])
    colb = at("colb", CO + 2.875, [P, 32])
    onesr = at("onesr", CO + 3, [P, P], F32R)
    selr = at("selr", CO + 3.5, [32 + MLH, MLH], F32R)

    sc = small[:, 0:8]
    scE = small[:, 8:16]
    a1, sh1 = small[:, 16:24], small[:, 24:32]
    a2, sh2 = small[:, 32:40], small[:, 40:48]
    gate1, gate2 = small[:, 48:56], small[:, 56:64]
    qgs = small[:, 64:65]
    emT = small[:, 72:104].rearrange("p (t h) -> p t h", t=TT)
    bif = small[:, 104:105]
    mx = small[:, 105:109]
    nq, nd, nr, ss, nv = (colb[:, 4 * i:4 * i + 4] for i in range(5))
    nf = colb[:, 20:24]

    K_BADA, K_N1, K_N2, K_CW, K_CB, K_QG, K_KG, K_MG = 0, 48, 56, 64, 96, 104, 105, 106
    N_VEC = 114

    ps = nc.alloc_psum_tensor("ps", [P, 8, 512], F32)
    f_dram = nc.dram_tensor("toeplitz_rows", (NG * AH, TSUM), F32)

    with ExitStack() as ctx:
        def sem(name):
            return ctx.enter_context(nc.semaphore(name))

        c_in = sem("c_in")
        c_transposed = sem("c_transposed")
        vec_in = sem("vec_in")
        x_in = sem("x_in")
        oh_in = sem("oh_in")
        if_in = sem("if_in")
        bif_in = sem("bif_in")
        frow_out = sem("frow_out")
        stage_in = sem("stage_in")
        consts_set = sem("consts_set")
        identity_made = sem("identity_made")
        if_zeroed = sem("if_zeroed")
        w_hi_ready = sem("w_hi_ready")
        w_lo_ready = sem("w_lo_ready")
        unit_done = sem("unit_done")
        vec_transposed = sem("vec_transposed")
        vec_columns = sem("vec_columns")
        silu_exp = sem("silu_exp")
        silu_ready = sem("silu_ready")
        ada_accumulated = sem("ada_accumulated")
        ada_transposed = sem("ada_transposed")
        ada_columns = sem("ada_columns")
        x_transposed = sem("x_transposed")
        x_squared = sem("x_squared")
        x_sumsq = sem("x_sumsq")
        x_rstd = sem("x_rstd")
        u_hi = sem("u_hi")
        u_lo = sem("u_lo")
        if_hi = sem("if_hi")
        if_lo = sem("if_lo")
        if_product = sem("if_product")
        lf_abs = sem("lf_abs")
        lf_log = sem("lf_log")
        rows_ready = sem("rows_ready")
        e_transposed = sem("e_transposed")
        e_columns = sem("e_columns")
        exp_neg_m = sem("exp_neg_m")
        frow_product = sem("frow_product")
        frow_sbuf = sem("frow_sbuf")
        bias_flipped = sem("bias_flipped")
        bias_ready = sem("bias_ready")
        conv_sum = sem("conv_sum")
        conv_sigmoid_sem = sem("conv_sigmoid_sem")
        mqk_ready = sem("mqk_ready")
        mv_transposed = sem("mv_transposed")
        v_ready = sem("v_ready")
        stack_hi = sem("stack_hi")
        stack_lo = sem("stack_lo")
        pad_zeroed = sem("pad_zeroed")
        negM_broadcast = sem("negM_broadcast")
        decay_clamped = sem("decay_clamped")
        decay_diagonal = sem("decay_diagonal")
        decay_exp = sem("decay_exp")
        decay_masked = sem("decay_masked")
        mlstm_scores_done = sem("mlstm_scores_done")
        mlstm_weights_ready = sem("mlstm_weights_ready")
        mlstm_numerator_done = sem("mlstm_numerator_done")
        nq_copied = sem("nq_copied")
        num_squares = sem("num_squares")
        num_var = sem("num_var")
        num_rstd = sem("num_rstd")
        hn_ready = sem("hn_ready")
        h_transposed = sem("h_transposed")
        h_gated = sem("h_gated")
        h_hi = sem("h_hi")
        h_lo = sem("h_lo")
        qk_sumsq = sem("qk_sumsq")
        qk_rstd = sem("qk_rstd")
        qk_normed = sem("qk_normed")
        v_transposed = sem("v_transposed")
        v_tokens = sem("v_tokens")
        scores_done = sem("scores_done")
        row_max_ready = sem("row_max_ready")
        probs_ready = sem("probs_ready")
        probs_transposed = sem("probs_transposed")
        probsT_ready = sem("probsT_ready")
        pv_done = sem("pv_done")
        o_copied = sem("o_copied")
        stats_turned = sem("stats_turned")
        stats_rows = sem("stats_rows")
        merge_diff = sem("merge_diff")
        merge_exp = sem("merge_exp")
        merge_weights = sem("merge_weights")
        weights_broadcast = sem("weights_broadcast")
        broadcast_read = sem("broadcast_read")
        att_ready = sem("att_ready")
        att_hi = sem("att_hi")
        att_lo = sem("att_lo")
        y_ready = sem("y_ready")
        y_hi = sem("y_hi")
        y_lo = sem("y_lo")
        x1_squared = sem("x1_squared")
        x1_sumsq = sem("x1_sumsq")
        x1_rstd = sem("x1_rstd")
        u2_even = sem("u2_even")
        u2_odd = sem("u2_odd")
        u2_hi = sem("u2_hi")
        u2_lo = sem("u2_lo")
        xn_ready = sem("xn_ready")
        squares_lo = sem("squares_lo")
        squares_added = sem("squares_added")
        x1_scaled = sem("x1_scaled")
        hdn_squared = sem("hdn_squared")
        hdn_hi = sem("hdn_hi")
        hdn_lo = sem("hdn_lo")
        x2_transposed = sem("x2_transposed")
        out_tile = sem("out_tile")
        dve_step = sem("dve_step")
        act_step = sem("act_step")
        pool_step = sem("pool_step")
        ada_in = [sem(f"ada_in{i}") for i in range(3)]
        w_in_sem = [sem(f"w_landed{i}") for i in range(RING)]
        out_done = [sem(f"out{i}_stored") for i in range(2)]
        bank_read = [sem(f"bank{i}_read") for i in range(2)]

        w_in2 = w_in[0]

        def slab(u):
            def cols_of(w, c0, kc=DC):
                return w[0:kc * P, c0:c0 + P].rearrange("(k p) n -> p k n", p=P), kc
            if u < U_MO:
                return cols_of(w_in2, C_MQ + u * P)
            if u < U_MV:
                return cols_of(w_in2, C_MO + (u - U_MO) * P)
            if u < U_ATT:
                return cols_of(w_in2, C_MV + (u - U_MV) * P)
            if u < U_YML:
                j, part = divmod(u - U_ATT, 3)
                h, g = divmod(j, NG)
                return cols_of(w_in2, (C_AQ, C_AK, C_AV)[part] + (g * AH + h) * DH)
            if u < U_YATT:
                n, part = divmod(u - U_YML, 2)
                return cols_of(w_ml_out[0], n * P) if part else cols_of(w_in2, C_GB + n * P)
            if u < U_OUT:
                n, part = divmod(u - U_YATT, 2)
                return cols_of(w_att_out[0], n * P, AH) if part else cols_of(w_in2, C_GA + n * P)
            return cols_of(w_out[0], (u - U_OUT) * P)

        def kchunks(u):
            return AH if U_YATT <= u < U_OUT and (u - U_YATT) % 2 else DC

        def taken(eng, u, turn=0):
            eng.wait_ge(bank_read[u % 2], u // 2 + 1 + RING // 2 * turn)

        diagonal = bass.AP(tensor=expd[:].tensor, offset=expd[:].offset, ap=[expd[:].ap[0], [SEQ + P, TT], [1, P]])

        block = ctx.enter_context(nc.Block())

        @block.sync
        def _(sp):
            sp.dma_start(crow[0:DC, :], c.rearrange("b (a p) -> (b a) p", p=P)).then_inc(c_in, 16)
            sp.dma_start(xtok[:], x[0].rearrange("(t p) d -> p t d", p=P)).then_inc(x_in, 16)

            def ada(i):
                if i >= 3:
                    sp.wait_ge(ada_accumulated, i - 2)
                g, k = divmod(i, 8)
                dst = adabuf if i < 16 else adabuf3
                sp.dma_start(dst[:, i % 3, :], w_ada[0, k * P:(k + 1) * P, 2 * D * g:2 * D * (g + 1)]).then_inc(
                    ada_in[i % 3], 16)

            def weights(u):
                if u >= RING:
                    sp.wait_ge(w_lo_ready, u - RING + 1)
                src, kc = slab(u)
                sp.dma_start(wraw[:, u % RING, 0:kc, :], src).then_inc(w_in_sem[u % RING], 16)

            for i in range(8):
                ada(i)
                if i == 2:
                    sp.wait_ge(if_zeroed, 2)
                    sp.dma_start(ifraw[:, :, 0:MLH],
                                 w_in2[:, C_MI:C_MI + MLH].rearrange("(k p) n -> p k n", p=P)).then_inc(if_in, 16)
                    sp.dma_start(ifraw[:, :, 32:32 + MLH],
                                 w_in2[:, C_MF:C_MF + MLH].rearrange("(k p) n -> p k n", p=P)).then_inc(if_in, 16)
            for u in range(RING):
                weights(u)
            for u in range(RING, U_FF):
                weights(u)
                if RING + 6 <= u < RING + 14:
                    ada(8 + u - RING - 6)
                if u == RING + 4:
                    sp.wait_ge(frow_sbuf, 1)
                    sp.dma_start(f_dram.ap(), frow[:]).then_inc(frow_out, 16)
                    sp.wait_ge(frow_out, 16)
                    sp.wait_ge(if_product, 1)
                    for g, (w, c0) in enumerate(((2 * P, 0), (P, 2 * P), (P, 3 * P))):
                        src = bass.AP(tensor=f_dram.ap().tensor, offset=g * AH * TSUM + TO[g],
                                      ap=[[1, P], [TSUM, AH], [1, w]])
                        sp.dma_start(stage[:, :, c0:c0 + w], src).then_inc(stage_in, 16)
                if U_YATT + 8 <= u < U_YATT + 16:
                    sp.wait_ge(unit_done, U_YATT)
                    ada(16 + u - U_YATT - 8)
            with sp.Fori(0, NQ) as q:
                for j in range(QU):
                    u = U_FF + j
                    sp.wait_ge(w_lo_ready, u - RING + 1 + QU * q)
                    if j < DC:
                        src = w_ff1[0][:, bass.ds(q * D + j * P, P)]
                    else:
                        src = w_ff2[0][bass.ds(q * D, D), (j - DC) * P:(j - DC + 1) * P]
                    sp.dma_start(wraw[:, u % RING], src.rearrange("(k p) n -> p k n", p=P)).then_inc(
                        w_in_sem[u % RING], 16)
            out_tok = out[0].rearrange("(t p) d -> p t d", p=P)
            for n in range(DC):
                sp.wait_ge(out_tile, n + 1)
                sp.dma_start(out_tok[:, :, n * P:(n + 1) * P], obuf[:, n % 2]).then_inc(out_done[n % 2], 16)
            for b in range(2):
                sp.wait_ge(out_done[b], 16 * DC // 2)

        @block.gpsimd
        def _(pool):
            nc.gpsimd.memset(ident[:], 0.0).then_inc(pool_step, 1)
            pool.wait_ge(pool_step, 1)
            nc.gpsimd.affine_select(out=ident[:], in_=ident[:], compare_op=ALU.not_equal, fill=1.0, base=0,
                                    pattern=[[1, P]], channel_multiplier=-1).then_inc(identity_made, 1)
            pool.wait_ge(vec_transposed, 1)
            nc.gpsimd.memset(flip[:], 0.0).then_inc(pool_step, 1)
            pool.wait_ge(pool_step, 2)
            nc.gpsimd.affine_select(out=flip[:], in_=flip[:], compare_op=ALU.not_equal, fill=1.0, base=1 - P,
                                    pattern=[[1, P]], channel_multiplier=1).then_inc(identity_made, 1)
            pool.wait_ge(if_hi, 1)
            nc.gpsimd.tensor_tensor(iflo[:], ifraw[:], ifhi[:].bitcast(F32), ALU.subtract).then_inc(if_lo, 1)

            def low(u, turn=0):
                pool.wait_ge(w_hi_ready, u + 1 + RING * turn)
                kc, s = kchunks(u), u % RING
                nc.gpsimd.tensor_tensor(wlo[:, s, 0:kc, :], wraw[:, s, 0:kc, :], whi[:, s, 0:kc, :].bitcast(F32),
                                        ALU.subtract).then_inc(w_lo_ready, 1)

            pool.wait_ge(x_rstd, 1)
            for d in range(DC):
                nc.gpsimd.tensor_tensor(xn[:, d, :], xT[:, d, :], n1rs[:], ALU.mult).then_inc(xn_ready, 1)
                if d == 5:
                    low(0)

            def mask(h):
                pool.wait_ge(decay_diagonal, h + 1)
                nc.gpsimd.affine_select(out=diagonal, in_=diagonal, compare_op=ALU.is_ge, fill=0.0, base=0,
                                        pattern=[[0, TT], [1, P]], channel_multiplier=-1).then_inc(decay_masked, 1)

            def m_stack(h):
                own, other = (slice(DK * b, DK * b + DK) for b in (h % 2, 1 - h % 2))
                pool.wait_ge(stack_hi, h + 1)
                pool.wait_ge(w_lo_ready, U_MV + 4 + h)
                if h >= 1:
                    pool.wait_ge(decay_masked, h)
                k, q = mqk[own, 4 + h // 2, :], mqk[own, h // 2, :]
                khi, qhi = kst[h % 2][own, :].bitcast(F32), qst[h % 2][own, :].bitcast(F32)
                for n, (dst, src, hi) in enumerate(((kst[h % 2][other, :], k, khi), (qst[h % 2][other, :], q, qhi),
                                                    (qsw[h % 2][own, :], q, qhi))):
                    nc.gpsimd.tensor_tensor(dst, src, hi, ALU.subtract).then_inc(stack_lo, 1)
                    pool.wait_ge(stack_lo, 3 * h + n + 1)

            for u in range(1, U_ATT + RING):
                low(u)
                if u == U_MV + 3:
                    m_stack(0)
                if U_MV + 4 <= u:
                    mask(u - U_MV - 4)
                    if u < U_MV + 3 + MLH:
                        m_stack(u - U_MV - 3)
            for u0, u1 in ((U_ATT + RING, U_YATT), (U_YATT, U_OUT), (U_OUT, U_FF)):
                with pool.Fori(0, (u1 - u0) // RING) as turn:
                    for i in range(RING):
                        low(u0 + i, turn)
            for j in range(RING - 1):
                low(U_FF + j)
            pool.wait_ge(x1_rstd, 1)
            for d in range(1, DC, 2):
                pool.wait_ge(x1_scaled, d + 1)
                nc.gpsimd.tensor_tensor(xa[:, d, :], xa[:, d, :], rs2[:], ALU.mult).then_inc(u2_odd, 1)
            for j in range(RING - 1, QU):
                low(U_FF + j)
            with pool.Fori(1, NQ) as q:
                for j in range(QU):
                    low(U_FF + j, QT * q)

        @block.scalar
        def _(act):
            count = [0]

            def link(ins):
                count[0] += 1
                ins.then_inc(act_step, 1)
                act.wait_ge(act_step, count[0])

            def high(u, turn=0):
                act.wait_ge(w_in_sem[u % RING], 16 * (u // RING + 1) + 16 * turn)
                if u >= RING:
                    act.wait_ge(unit_done, u - RING + 1 + RING * turn)
                kc, s = kchunks(u), u % RING
                nc.scalar.copy(whi[:, s, 0:kc, :], wraw[:, s, 0:kc, :]).then_inc(w_hi_ready, 1)

            G = lambda u: ps[:, u % 2, :]

            def rows_of(a, r0, n):
                act.dma_start(vrows[r0:r0 + n, :], a).then_inc(vec_in, 16)
            rows_of(b_ada.rearrange("b (a p) -> (b a) p", p=P), K_BADA, 48)
            rows_of(norm1_g.rearrange("b (a p) -> (b a) p", p=P), K_N1, DC)
            rows_of(norm2_g.rearrange("b (a p) -> (b a) p", p=P), K_N2, DC)
            rows_of(conv_w[0].rearrange("t (a p) -> (t a) p", p=P), K_CW, TAPS * DC)
            rows_of(conv_b.rearrange("b (a p) -> (b a) p", p=P), K_CB, DC)
            rows_of(q_norm_g, K_QG, 1)
            rows_of(k_norm_g, K_KG, 1)
            rows_of(mlstm_norm_g.rearrange("b (a p) -> (b a) p", p=P), K_MG, DC)
            act.dma_start(onehot[:], one_hot).then_inc(oh_in, 16)
            act.wait_ge(if_zeroed, 1)
            act.dma_start(relb[0:NBUCK, :], rel_bias).then_inc(oh_in, 16)
            act.dma_start(bif[0:MLH, :], b_if[0, 0:1, :].rearrange("a h -> h a")).then_inc(bif_in, 16)
            act.dma_start(bif[32:32 + MLH, :], b_if[0, 1:2, :].rearrange("a h -> h a")).then_inc(bif_in, 16)
            nc.scalar.preload_act_table_set("natural_log_exp_and_others")
            act.wait_ge(c_transposed, 1)
            nc.scalar.activation(scE, ps[:, 7, 0:DC], ACT.Exp, scale=-1.0).then_inc(silu_exp, 1)
            for d in range(DC):
                act.wait_ge(x_transposed, d + 1)
                nc.scalar.copy(xT[:, d, :], ps[:, d % 4, :])
                if d >= 2:
                    act.wait_ge(x_sumsq, d - 1)
                nc.scalar.activation(n1sq[:, d % 2, :], ps[:, d % 4, :], ACT.Square).then_inc(x_squared, 1)
            act.wait_ge(if_in, 32)
            nc.scalar.copy(ifhi[:], ifraw[:]).then_inc(if_hi, 1)
            act.wait_ge(x_sumsq, DC)
            act.wait_ge(consts_set, 3)
            link(nc.scalar.activation(n1rs[:], ps[:, 6, :], ACT.Ln, scale=1.0 / D, bias=small[:, 109:110]))
            nc.scalar.activation(n1rs[:], n1rs[:], ACT.Exp, scale=-0.5).then_inc(x_rstd, 1)
            act.wait_ge(vec_transposed, 1)
            nc.scalar.copy(cols[:, 0:N_VEC], ps[:, 4, 0:N_VEC]).then_inc(vec_columns, 1)
            act.wait_ge(frow_product, 1)
            nc.scalar.copy(frow[:, 0:512], ps[0:NG * AH, 5, :])
            nc.scalar.copy(frow[:, 512:TSUM], ps[0:NG * AH, 4, 0:TSUM - 512]).then_inc(frow_sbuf, 1)
            for u in range(RING - 1):
                high(u)
            act.wait_ge(ada_columns, 1)
            for d in range(DC):
                act.wait_ge(xn_ready, d + 1)
                nc.scalar.activation(uhi[:, d, :], xn[:, d, :], ACT.Identity, scale=a1[:, d:d + 1],
                                     bias=sh1[:, d:d + 1]).then_inc(u_hi, 1)
                if d == 1:
                    high(RING - 1)

            def after(u, turn=0, refill=True):
                act.wait_ge(unit_done, u + 1 + RING * turn)
                if refill:
                    high(u + RING, turn)

            def conv_sigmoid(u):
                act.wait_ge(conv_sum, u + 1)
                if u >= 1:
                    act.wait_ge(mqk_ready, u)
                nc.scalar.activation(csig[:], cacc[:, u % 2, :], ACT.Sigmoid).then_inc(conv_sigmoid_sem, 1)

            for u in range(U_CONV, U_MO):
                after(u)
                if u >= 2:
                    act.wait_ge(conv_sum, u - 1)
                else:
                    act.wait_ge(pad_zeroed, 1)
                nc.scalar.copy(cpad[:, u % 2, TAPS - 1:], G(u)).then_inc(bank_read[u % 2], 1)
                if u == 0:
                    act.wait_ge(lf_abs, 1)
                    link(nc.scalar.activation(rows[32:40, 1, :], rows[32:40, 1, :], ACT.Exp, scale=-1.0))
                    nc.scalar.activation(rows[32:40, 1, :], rows[32:40, 1, :], ACT.Ln, bias=1.0).then_inc(lf_log, 1)
                if u >= 1:
                    conv_sigmoid(u - 1)
            conv_sigmoid(U_MO - 1)

            def m_stack(h):
                own, other = (slice(DK * b, DK * b + DK) for b in (h % 2, 1 - h % 2))
                act.wait_ge(mqk_ready, 5 + h // 2)
                if h >= 2:
                    act.wait_ge(mlstm_scores_done, 4 * (h - 1))
                nc.scalar.copy(kst[h % 2][own, :], mqk[own, 4 + h // 2, :])
                nc.scalar.copy(qst[h % 2][own, :], mqk[own, h // 2, :])
                nc.scalar.copy(qsw[h % 2][other, :], mqk[own, h // 2, :]).then_inc(stack_hi, 1)

            for u in range(U_MO, U_MV):
                after(u)
                if u == U_MV - 1:
                    m_stack(0)
                if u == U_MO:
                    act.wait_ge(bias_ready, 1)
                nc.scalar.activation(mo[:, u - U_MO, :], G(u), ACT.Sigmoid).then_inc(bank_read[u % 2], 1)

            nc.scalar.preload_act_table_set("natural_log_exp_and_others")
            act.wait_ge(e_columns, 1)
            nc.scalar.activation(emT, eT[:, 1], ACT.Exp).then_inc(exp_neg_m, 1)

            def m_exp(h):
                if h >= 1:
                    act.wait_ge(mlstm_weights_ready, 4 * h)
                act.wait_ge(decay_clamped, h + 1)
                nc.scalar.activation(diagonal, dcl[:], ACT.Exp).then_inc(decay_diagonal, 1)
                for j in range(TT - 1):
                    last = nc.scalar.activation(expd[:, j, (j + 1) * P:], ps[:, 5, (j + 1) * P:SEQ], ACT.Exp,
                                                bias=eT[:, 0, j, h:h + 1])
                last.then_inc(decay_exp, 1)

            def m_high(h):
                act.wait_ge(h_gated, h + 1)
                nc.scalar.copy(hhi[:, h, :], hg[:]).then_inc(h_hi, 1)

            def m_norm(h):
                act.wait_ge(nq_copied, h + 1)
                for i in range(TT):
                    last = nc.scalar.activation(hn[:, i, :], ps[:, 6 + i // 2, (i % 2) * 256:(i % 2) * 256 + DV],
                                                ACT.Square, accum_out=ss[:, i:i + 1])
                last.then_inc(num_squares, 1)
                act.wait_ge(num_var, h + 1)
                link(nc.scalar.activation(nv, nv, ACT.Ln, scale=1.0 / DV, bias=small[:, 109:110]))
                nc.scalar.activation(nv, nv, ACT.Exp, scale=-0.5).then_inc(num_rstd, 1)

            for h in range(MLH):
                u = U_MV + h
                after(u)
                if h >= 1:
                    act.wait_ge(mv_transposed, h)
                nc.scalar.copy(mvT[:], G(u)).then_inc(bank_read[u % 2], 1)
                m_exp(h)
                if h < MLH - 1:
                    m_stack(h + 1)
                if h >= 2:
                    m_high(h - 2)
                if h >= 1:
                    m_norm(h - 1)

            def exps(j):
                g = j % NG
                h = j // NG
                act.wait_ge(row_max_ready, j + 1)
                for t in range(TT):
                    lo = P if g == 0 and t == 0 else 0
                    w = 2 * P if g == 0 else P
                    last = nc.scalar.activation(prob[:, t, lo:w], sbias[:, t, lo:w], ACT.Exp,
                                                bias=stats[:, 0, g, t, h:h + 1], accum_out=stats[:, 1, g, t, h:h + 1])
                last.then_inc(probs_ready, 1)

            def o_copy(j):
                g, h = j % NG, j // NG
                dil = GROUPS[g][1]
                act.wait_ge(pv_done, j + 1)
                nc.scalar.copy(outT[:, j, :].rearrange("p (s r) -> p s r", r=dil),
                               ps[:, 7, :].rearrange("p (r s) -> p s r", r=dil)).then_inc(o_copied, 1)

            def rstd(n):
                act.wait_ge(qk_sumsq, n + 1)
                if n >= 2:
                    act.wait_ge(qk_normed, n - 1)
                link(nc.scalar.activation(rsb[:, n % 2, :], ps[:, 6, :], ACT.Ln, scale=1.0 / DH,
                                           bias=small[:, 109:110]))
                nc.scalar.activation(rsb[:, n % 2, :], rsb[:, n % 2, :], ACT.Exp, scale=-0.5).then_inc(qk_rstd, 1)

            for s in range(36):
                u = U_ATT + s
                j, part = divmod(s, 3)
                after(u)
                if part < 2:
                    n = 2 * j + part
                    if n >= 2:
                        act.wait_ge(qk_normed, n - 1)
                        act.wait_ge(qk_sumsq, n - 1)
                    nc.scalar.copy(qf[:, part, :], G(u))
                    nc.scalar.activation(sqhi[:, part, :], G(u), ACT.Square).then_inc(bank_read[u % 2], 1)
                if part == 0:
                    if s == 0:
                        m_high(6)
                        m_norm(7)
                    if j >= 2:
                        o_copy(j - 2)
                    if j >= 1:
                        exps(j - 1)
                if part == 1:
                    if s == 1:
                        m_high(7)
                    rstd(2 * j)
                if part == 2:
                    rstd(2 * j + 1)

            for t in range(16):
                u = U_YML + t
                n, part = divmod(t, 2)
                if t == 5:
                    act.wait_ge(merge_diff, 1)
                    nc.scalar.activation(mrow[:], mrow[:], ACT.Exp).then_inc(merge_exp, 1)
                after(u)
                if t == 0:
                    o_copy(10)
                    exps(11)
                if t == 3:
                    o_copy(11)
                if part == 0:
                    if n >= 1:
                        taken(act, u - 1)
                    nc.scalar.activation(gsig[:], G(u), ACT.Sigmoid).then_inc(bank_read[u % 2], 1)
                if t == 4:
                    nc.scalar.preload_act_table_set("natural_log_exp_and_others")
                if t >= 9 and t % 2 == 1:
                    h = (t - 9) // 2
                    act.wait_ge(att_ready, h + 1)
                    nc.scalar.copy(ahi[:, h, :], mtmp[:, 0, :]).then_inc(att_hi, 1)
            for t in range(16):
                u = U_YATT + t
                n, part = divmod(t, 2)
                after(u)
                if part == 0:
                    taken(act, u - 1)
                    nc.scalar.activation(gsig[:], G(u), ACT.Sigmoid).then_inc(bank_read[u % 2], 1)
                else:
                    act.wait_ge(y_ready, n + 1)
                    nc.scalar.copy(yhi[:, n, :], ybuf[:, n % 2, :]).then_inc(y_hi, 1)
            nc.scalar.preload_act_table_set("natural_log_exp_and_others")
            for n in range(DC):
                if n < DC - 1:
                    after(U_OUT + n)
                taken(act, U_OUT + n)
                if n >= 3:
                    act.wait_ge(squares_added, n - 2)
                dst = sq2[:, n % 2, :] if n else sqacc[:]
                nc.scalar.activation(dst, xT[:, n, :], ACT.Square).then_inc(x1_squared, 1)
            after(U_OUT + DC - 1)
            act.wait_ge(x1_sumsq, 1)
            link(nc.scalar.activation(rs2[:], ps[:, 6, :], ACT.Ln, scale=1.0 / D, bias=small[:, 109:110]))
            nc.scalar.activation(rs2[:], rs2[:], ACT.Exp, scale=-0.5).then_inc(x1_rstd, 1)
            for d in range(DC):
                act.wait_ge((u2_even, u2_odd)[d % 2], d // 2 + 1)
                nc.scalar.activation(uhi[:, d, :], xa[:, d, :], ACT.Identity, bias=sh2[:, d:d + 1]).then_inc(u2_hi, 1)
            def quarter(q, first=False, last=False):
                for j in range(DC):
                    u = U_FF + j
                    act.wait_ge(unit_done, u + 1 + QU * q)
                    if j >= 2 or not first:
                        act.wait_ge(hdn_lo, j - 1 + DC * q)
                    nc.scalar.activation(rbuf[:, j % 2, :], G(u), ACT.Relu).then_inc(bank_read[u % 2], 1)
                    high(u + RING, QT * q)
                    taken(act, u, QT * q)
                    nc.scalar.activation(hhi[:, j, :], rbuf[:, j % 2, :], ACT.Square).then_inc(hdn_hi, 1)
                for j in range(DC):
                    after(U_FF + DC + j, QT * q, refill=not last or j < DC - RING)
                    if last and j >= 1:
                        n = j - 1
                        act.wait_ge(x2_transposed, n + 1)
                        if n >= 2:
                            act.wait_ge(out_done[n % 2], 16 * (n // 2))
                        nc.scalar.copy(obuf[:, n % 2],
                                       ps[:, 4 + n % 2, :].rearrange("p (t d) -> p t d", t=TT)).then_inc(
                            out_tile, 1)

            quarter(0, first=True)
            with act.Fori(1, NQ - 1) as q:
                quarter(q)
            quarter(NQ - 1, last=True)
            act.wait_ge(x2_transposed, DC)
            act.wait_ge(out_done[1], 16 * (DC // 2 - 1))
            nc.scalar.copy(obuf[:, 1], ps[:, 5, :].rearrange("p (t d) -> p t d", t=TT)).then_inc(out_tile, 1)

        @block.vector
        def _(dve):
            count = [0]
            V = nc.vector

            def link(ins):
                count[0] += 1
                ins.then_inc(dve_step, 1)
                dve.wait_ge(dve_step, count[0])

            G = lambda u: ps[:, u % 2, :]

            V.memset(relb[32:33, :], 1.0).then_inc(if_zeroed, 1)
            V.memset(ifraw[:], 0.0).then_inc(if_zeroed, 1)
            V.memset(ones[:], 1.0).then_inc(consts_set, 1)
            V.memset(selr[:].bitcast(F32), 0.0)
            dve.wait_ge(consts_set, 1)
            link(V.tensor_copy(onesr[:], ones[:]))
            dve.wait_ge(identity_made, 1)
            V.tensor_copy(selr[0:MLH, :], ident[0:MLH, 0:MLH])
            link(V.tensor_copy(selr[32:32 + MLH, :], ident[32:32 + MLH, 32:32 + MLH]))
            V.memset(small[:, 109:110], EPS).then_inc(consts_set, 1)
            V.memset(bias2[:], NEG).then_inc(consts_set, 1)
            dve.wait_ge(silu_exp, 1)
            link(V.tensor_scalar(scE, scE, 1.0, None, ALU.add))
            link(V.reciprocal(scE, scE))
            V.tensor_tensor(sc, ps[:, 7, 0:DC], scE, ALU.mult).then_inc(silu_ready, 1)
            dve.wait_ge(silu_ready, 1)

            def ada(i):
                dve.wait_ge(ada_in[i % 3], 16 * (i // 3 + 1))
                if i >= 1:
                    dve.wait_ge(ada_accumulated, i)
                g, k = divmod(i, 8)
                dst = (ada1, ada2, ada3)[g][:]
                src = (adabuf, adabuf, adabuf3)[g][:, i % 3, :]
                if k == 0:
                    V.tensor_scalar(dst, src, sc[:, k:k + 1], None, ALU.mult).then_inc(ada_accumulated, 1)
                else:
                    V.scalar_tensor_tensor(out=dst, in0=src, scalar=sc[:, k:k + 1], in1=dst,
                                           op0=ALU.mult, op1=ALU.add).then_inc(ada_accumulated, 1)

            for i in range(8):
                ada(i)
            dve.wait_ge(vec_columns, 1)
            V.tensor_scalar(qgs, cols[:, K_QG:K_QG + 1], DH ** -0.5, None, ALU.mult)
            dve.wait_ge(ada_transposed, 1)
            link(V.tensor_tensor(adac[:, 0:16], ps[:, 7, 0:16], cols[:, K_BADA:K_BADA + 16], ALU.add))
            V.tensor_copy(sh1, adac[:, 0:8])
            V.scalar_tensor_tensor(out=a1, in0=adac[:, 8:16], scalar=1.0, in1=cols[:, K_N1:K_N1 + DC],
                                   op0=ALU.add, op1=ALU.mult).then_inc(ada_columns, 1)
            dve.wait_ge(ada_columns, 1)
            for d in range(DC):
                dve.wait_ge(xn_ready, d + 1)
                if d >= 2:
                    dve.wait_ge(u_lo, d - 1)
                link(V.tensor_scalar(n1t[:, d % 2, :], xn[:, d, :], a1[:, d:d + 1], sh1[:, d:d + 1], ALU.mult,
                                     ALU.add))
                dve.wait_ge(u_hi, d + 1)
                V.tensor_tensor(ulo[:, d, :], n1t[:, d % 2, :], uhi[:, d, :].bitcast(F32), ALU.subtract).then_inc(
                    u_lo, 1)
            V.memset(rows[0:8, 2, :], 1.0)
            V.memset(negM[:].bitcast(F32), 0.0)
            V.memset(cpad[:, :, 0:TAPS - 1], 0.0).then_inc(pad_zeroed, 1)
            dve.wait_ge(pad_zeroed, 1)
            dve.wait_ge(if_product, 1)
            dve.wait_ge(bif_in, 32)
            z, az = rows[32:40, 0, :], rows[32:40, 1, :]
            link(V.tensor_scalar(z, ps[32:40, 2, :], bif[32:40, :], None, ALU.add))
            V.scalar_tensor_tensor(out=az, in0=z, scalar=-1.0, in1=z, op0=ALU.mult, op1=ALU.max).then_inc(lf_abs, 1)
            link(V.tensor_scalar(rows[0:8, 0, :], ps[0:8, 2, :], bif[0:8, :], None, ALU.add))
            link(V.tensor_scalar(z, z, 0.0, None, ALU.min))
            dve.wait_ge(lf_log, 1)
            link(V.tensor_tensor(rows[0:8, 1, :], z, az, ALU.subtract))
            link(V.tensor_tensor_scan(csum[:], rows[0:8, 2, :], rows[0:8, 1, :], 0.0, ALU.mult, ALU.add))
            link(V.tensor_tensor(rows[0:8, 0, :], rows[0:8, 0, :], csum[:], ALU.subtract))
            link(V.tensor_tensor_scan(rows[0:8, 1, :], rows[0:8, 2, :], rows[0:8, 0, :], 0.0, ALU.mult, ALU.max))
            link(V.scalar_tensor_tensor(out=rows[0:8, 2, :], in0=csum[:], scalar=-1.0, in1=rows[0:8, 1, :],
                                        op0=ALU.mult, op1=ALU.subtract))
            link(V.tensor_scalar(negM[0:MLH, :], rows[0:8, 1, :], -1.0, None, ALU.mult))
            V.scalar_tensor_tensor(out=negM[32:32 + MLH, :], in0=rows[0:8, 1, :], scalar=-1.0,
                                   in1=negM[0:MLH, :].bitcast(F32), op0=ALU.mult, op1=ALU.subtract).then_inc(
                                       rows_ready, 1)

            def silu_mul(u):
                dve.wait_ge(conv_sigmoid_sem, u + 1)
                V.scalar_tensor_tensor(out=mqk[:, u, :], in0=cacc[:, u % 2, :], scalar=1.0 if u < 4 else DK ** -0.5,
                                       in1=csig[:], op0=ALU.mult, op1=ALU.mult).then_inc(mqk_ready, 1)

            for u in range(U_CONV, U_MO):
                taken(dve, u)
                if u >= 2:
                    dve.wait_ge(mqk_ready, u - 1)
                cw = lambda t: cols[:, K_CW + DC * t + u:K_CW + DC * t + u + 1]
                link(V.tensor_scalar(cacc[:, u % 2, :], cpad[:, u % 2, TAPS - 1:], cw(TAPS - 1),
                                     cols[:, K_CB + u:K_CB + u + 1], ALU.mult, ALU.add))
                for t in range(TAPS - 1):
                    ins = V.scalar_tensor_tensor(out=cacc[:, u % 2, :], in0=cpad[:, u % 2, t:t + SEQ], scalar=cw(t),
                                                 in1=cacc[:, u % 2, :], op0=ALU.mult, op1=ALU.add)
                    if t < TAPS - 2:
                        link(ins)
                ins.then_inc(conv_sum, 1)
                if u >= 1:
                    silu_mul(u - 1)
                if u == 4:
                    dve.wait_ge(e_transposed, 1)
                    V.tensor_copy(eT[:], ps[:, 3, 0:64].rearrange("p (a t h) -> p a t h", a=2, t=TT)).then_inc(
                        e_columns, 1)
            silu_mul(7)
            for u in range(U_MO, U_MV):
                if u == U_MO:
                    dve.wait_ge(bias_flipped, 1)
                    V.tensor_copy(bias0[:, 0:2], ps[:, 3, :].rearrange("p (h w) -> p h w", h=2))
                    V.tensor_copy(bias0[:, 2:4], ps[:, 4, :].rearrange("p (h w) -> p h w", h=2))
                    V.tensor_copy(bias1[:], ps[:, 5, :].rearrange("p (h w) -> p h w", h=AH))
                    for b in range(4):
                        r = slice(32 * b, 32 * b + 32)
                        last = V.tensor_copy(bias2[r, :, r], ps[r, 6, :].rearrange("p (h w) -> p h w", h=AH)[:, :, r])
                    last.then_inc(bias_ready, 1)
                ada(8 + u - U_MO)
            dve.wait_ge(ada_transposed, 2)
            link(V.tensor_tensor(adac[:, 16:32], ps[:, 7, 16:32], cols[:, K_BADA + 16:K_BADA + 32], ALU.add))
            V.tensor_copy(gate1, adac[:, 16:24])
            V.tensor_copy(sh2, adac[:, 24:32])
            V.memset(vext[:, :, :, DV:DV + 1], 1.0).then_inc(ada_columns, 1)

            def m_gate(h):
                dve.wait_ge(h_transposed, h + 1)
                if h >= 1:
                    dve.wait_ge(h_hi, h)
                    dve.wait_ge(h_lo, h)
                V.scalar_tensor_tensor(out=hg[:], in0=ps[:, 4, :], scalar=cols[:, K_MG + h:K_MG + h + 1],
                                       in1=mo[:, h, :], op0=ALU.mult, op1=ALU.mult).then_inc(h_gated, 1)

            def m_low(h):
                dve.wait_ge(h_gated, h + 1)
                dve.wait_ge(h_hi, h + 1)
                V.tensor_tensor(hlo[:, h, :], hg[:], hhi[:, h, :].bitcast(F32), ALU.subtract).then_inc(h_lo, 1)

            def m_clamp(h):
                dve.wait_ge(negM_broadcast, h + 1)
                if h >= 1:
                    dve.wait_ge(decay_diagonal, h)
                for j in range(TT):
                    last = V.tensor_scalar(dcl[:, j, :], ps[:, 5, j * P:(j + 1) * P], eT[:, 0, j, h:h + 1], 0.0,
                                           ALU.add, ALU.min)
                last.then_inc(decay_clamped, 1)

            def m_weights(h, j):
                bank, c0 = ((2, 0), (3, 0), (2, 0), (3, 384))[j]
                w = SEQ - j * P
                dve.wait_ge(mlstm_scores_done, 4 * h + (1, 3, 4, 3)[j])
                dve.wait_ge(decay_masked, h + 1)
                dve.wait_ge(decay_exp, h + 1)
                if h >= 2:
                    dve.wait_ge(mlstm_numerator_done, h - 1)
                V.tensor_tensor(wts[:, h % 2, EW[j]:EW[j + 1]], ps[:, bank, c0:c0 + w],
                                expd[:, j, j * P:], ALU.mult).then_inc(mlstm_weights_ready, 1)

            def m_vext(h):
                dve.wait_ge(mv_transposed, h + 1)
                if h >= 2:
                    dve.wait_ge(mlstm_numerator_done, h - 1)
                V.tensor_copy(vext[:, h % 2, :, 0:DV], ps[:, 4, :].rearrange("p (t d) -> p t d", t=TT)).then_inc(
                    v_ready, 1)

            num = ps[:, 6:8, :].rearrange("p b (i w) -> p (b i) w", w=256)

            def m_norm(h):
                dve.wait_ge(mlstm_numerator_done, h + 1)
                V.tensor_copy(nq, num[:, :, DV]).then_inc(nq_copied, 1)
                dve.wait_ge(nq_copied, h + 1)
                link(V.scalar_tensor_tensor(out=nd, in0=nq, scalar=-1.0, in1=nq, op0=ALU.mult, op1=ALU.max))
                dve.wait_ge(exp_neg_m, 1)
                link(V.tensor_tensor(nd, nd, emT[:, :, h], ALU.max))
                link(V.reciprocal(nr, nd))
                link(V.tensor_tensor(nd, nr, nr, ALU.mult))
                dve.wait_ge(num_squares, h + 1)
                V.tensor_tensor(nv, ss, nd, ALU.mult).then_inc(num_var, 1)
                dve.wait_ge(num_rstd, h + 1)
                link(V.tensor_tensor(nf, nr, nv, ALU.mult))
                V.tensor_tensor(hn[:], num[:, :, 0:DV], nf.unsqueeze(2).to_broadcast([P, TT, DV]), ALU.mult).then_inc(
                    hn_ready, 1)

            for h in range(MLH):
                if h >= 2:
                    m_gate(h - 2)
                m_clamp(h)
                m_weights(h, 0)
                m_weights(h, 1)
                m_weights(h, 3)
                m_vext(h)
                if h >= 1:
                    m_norm(h - 1)
                m_weights(h, 2)
                if h >= 2:
                    m_low(h - 2)

            def scores(j):
                g, h = j % NG, j // NG
                dve.wait_ge(scores_done, j + 1)
                if j >= 1:
                    dve.wait_ge(probs_ready, j)
                if g == 0:
                    S = ps[:, 2:4, :].rearrange("p b (i w) -> p (b i) w", w=2 * P)
                    V.tensor_tensor(sbias[:, 0, P:], S[:, 0, P:], bias0[:, h, P:], ALU.add)
                    link(V.tensor_tensor(sbias[:, 1:], S[:, 1:], bias0[:, h:h + 1, :].to_broadcast([P, 3, 2 * P]),
                                         ALU.add))
                    V.tensor_reduce(mx[:, 0:1], sbias[:, 0, P:], AX.X, ALU.max)
                    link(V.tensor_reduce(mx[:, 1:4], sbias[:, 1:], AX.X, ALU.max))
                else:
                    S = ps[:, 2, :].rearrange("p (i w) -> p i w", w=P)
                    b = (bias1 if g == 1 else bias2)[:, h:h + 1, :]
                    link(V.tensor_tensor(sbias[:, :, 0:P], S, b.to_broadcast([P, TT, P]), ALU.add))
                    link(V.tensor_reduce(mx, sbias[:, :, 0:P], AX.X, ALU.max))
                V.tensor_scalar(stats[:, 0, g, :, h], mx, -1.0, None, ALU.mult).then_inc(row_max_ready, 1)

            def normed(n):
                j, part = divmod(n, 2)
                dil = GROUPS[j % NG][1]
                dve.wait_ge(qk_rstd, n + 1)
                if j >= 1:
                    dve.wait_ge(scores_done, j)
                dst, gain = ((qn, qgs), (kn, cols[:, K_KG:K_KG + 1]))[part]
                view = lambda a: a.rearrange("p (s r) -> p s r", r=dil)
                V.scalar_tensor_tensor(out=dst[:].rearrange("p (r s) -> p s r", r=dil), in0=view(qf[:, part, :]),
                                       scalar=gain, in1=view(rsb[:, part, :]), op0=ALU.mult, op1=ALU.mult).then_inc(
                    qk_normed, 1)

            def sq_low(n):
                u = U_ATT + 3 * (n // 2) + n % 2
                taken(dve, u)
                if n >= 1:
                    dve.wait_ge(qk_sumsq, n)
                link(V.tensor_tensor(sqf[:], qf[:, n % 2, :], qf[:, n % 2, :], ALU.mult))
                V.tensor_tensor(sqlo[:], sqf[:], sqhi[:, n % 2, :].bitcast(F32), ALU.subtract).then_inc(squares_lo, 1)
                dve.wait_ge(squares_lo, n + 1)

            def v_copy(j):
                u = U_ATT + 3 * j + 2
                dil = GROUPS[j % NG][1]
                dve.wait_ge(unit_done, u + 1)
                if j >= 1:
                    dve.wait_ge(v_transposed, j)
                V.tensor_copy(vTp[:].rearrange("p (r s) -> p s r", r=dil),
                              G(u).rearrange("p (s r) -> p s r", r=dil)).then_inc(bank_read[u % 2], 1)

            def v_tok(j):
                dve.wait_ge(v_transposed, j + 1)
                if j >= 2:
                    dve.wait_ge(pv_done, j - 1)
                V.tensor_copy(vtok[:, j % 2], ps[:, 4, :].rearrange("p (t d) -> p t d", t=TT)).then_inc(v_tokens, 1)

            def p_copy(j):
                n = 7 if j % NG == 0 else 4
                dve.wait_ge(probs_transposed, j + 1)
                if j >= 1:
                    dve.wait_ge(pv_done, j)
                V.tensor_copy(probT[:, 0:n, :],
                              ps[:, 4:6, :].rearrange("p b (i w) -> p (b i) w", w=P)[:, 0:n]).then_inc(probsT_ready, 1)

            for s in range(36):
                j, part = divmod(s, 3)
                if s == 0:
                    m_gate(6)
                    m_low(6)
                    m_norm(7)
                if s == 1:
                    m_gate(7)
                    m_low(7)
                if part == 0:
                    sq_low(2 * j)
                if part == 0 and j >= 1:
                    v_tok(j - 1)
                    scores(j - 1)
                if part == 1:
                    sq_low(2 * j + 1)
                    normed(2 * j)
                if part == 2:
                    v_copy(j)
                    normed(2 * j + 1)
                    if j >= 1:
                        p_copy(j - 1)

            def turn(g):
                dil = GROUPS[g][1]
                dve.wait_ge(stats_turned, g + 1)
                for dst, b in ((mrow, 2 + 2 * g), (lrow, 3 + 2 * g)):
                    last = V.tensor_copy(dst[:, g, :].rearrange("p (s r) -> p s r", r=dil),
                                         ps[0:AH, b, :].rearrange("p (r s) -> p s r", r=dil))
                last.then_inc(stats_rows, 1)

            def weigh_exponents():
                dve.wait_ge(stats_rows, NG)
                link(V.tensor_tensor(mtop[:], mrow[:, 0], mrow[:, 1], ALU.min))
                link(V.tensor_tensor(mtop[:], mtop[:], mrow[:, 2], ALU.min))
                V.tensor_tensor(mrow[:], mtop[:].unsqueeze(1).to_broadcast([AH, NG, SEQ]), mrow[:],
                                ALU.subtract).then_inc(
                    merge_diff, 1)

            def weigh_sum():
                dve.wait_ge(merge_exp, 1)
                link(V.tensor_tensor(lrow[:], lrow[:], mrow[:], ALU.mult))
                link(V.tensor_tensor(mtop[:], lrow[:, 0], lrow[:, 1], ALU.add))
                link(V.tensor_tensor(mtop[:], mtop[:], lrow[:, 2], ALU.add))
                link(V.reciprocal(mrec[:], mtop[:]))
                link(V.tensor_tensor(mrow[:], mrow[:], mrec[:].unsqueeze(1).to_broadcast([AH, NG, SEQ]), ALU.mult))
                link(V.memset(mrr[:].bitcast(F32), 0.0))

            def weigh_split():
                link(V.tensor_copy(mrr[0:AH], mrow[:]))
                V.tensor_tensor(mrr[32:32 + AH], mrow[:], mrr[0:AH].bitcast(F32), ALU.subtract).then_inc(
                    merge_weights, 1)

            def merge(h):
                dve.wait_ge(merge_weights, 1)
                dve.wait_ge(weights_broadcast, h + 1)
                if h >= 1:
                    dve.wait_ge(att_hi, h)
                    dve.wait_ge(att_lo, h)
                else:
                    dve.wait_ge(o_copied, NG * AH)
                for g in range(NG):
                    last = V.tensor_tensor(mtmp[:, g, :], ps[:, 4 + g, :], outT[:, NG * h + g, :], ALU.mult)
                last.then_inc(broadcast_read, 1)
                dve.wait_ge(broadcast_read, h + 1)
                link(V.tensor_tensor(mtmp[:, 0, :], mtmp[:, 0, :], mtmp[:, 1, :], ALU.add))
                V.tensor_tensor(mtmp[:, 0, :], mtmp[:, 0, :], mtmp[:, 2, :], ALU.add).then_inc(att_ready, 1)

            for t in range(16):
                u = U_YML + t
                n, part = divmod(t, 2)
                if part == 1:
                    dve.wait_ge(unit_done, u + 1)
                    taken(dve, u - 1)
                    V.tensor_tensor(yml[:, n, :], G(u), gsig[:], ALU.mult).then_inc(bank_read[u % 2], 1)
                if t == 5:
                    weigh_sum()
                if t == 7:
                    weigh_split()
                if t == 0:
                    v_tok(11)
                    scores(11)
                if t == 2:
                    p_copy(11)
                if t == 4:
                    for g in range(NG):
                        turn(g)
                    weigh_exponents()
                if t >= 8 and t % 2 == 0:
                    merge((t - 8) // 2)
                if t >= 9 and t % 2 == 1:
                    h = (t - 9) // 2
                    dve.wait_ge(att_hi, h + 1)
                    V.tensor_tensor(alo[:, h, :], mtmp[:, 0, :], ahi[:, h, :].bitcast(F32), ALU.subtract).then_inc(
                        att_lo, 1)
            for n in range(DC):
                u = U_YATT + 2 * n + 1
                dve.wait_ge(unit_done, u + 1)
                taken(dve, u - 1)
                yb = ybuf[:, n % 2, :]
                if n >= 2:
                    dve.wait_ge(y_hi, n - 1)
                    dve.wait_ge(y_lo, n - 1)
                V.tensor_tensor(yb, G(u), gsig[:], ALU.mult).then_inc(bank_read[u % 2], 1)
                taken(dve, u)
                V.tensor_tensor(yb, yb, yml[:, n, :], ALU.add).then_inc(y_ready, 1)
                dve.wait_ge(y_ready, n + 1)
                dve.wait_ge(y_hi, n + 1)
                V.tensor_tensor(ylo[:, n, :], yb, yhi[:, n, :].bitcast(F32), ALU.subtract).then_inc(y_lo, 1)
                ada(16 + n)
            dve.wait_ge(ada_transposed, 3)
            link(V.tensor_tensor(adac[:, 32:48], ps[:, 7, 32:48], cols[:, K_BADA + 32:K_BADA + 48], ALU.add))
            link(V.scalar_tensor_tensor(out=a2, in0=adac[:, 32:40], scalar=1.0, in1=cols[:, K_N2:K_N2 + DC],
                                        op0=ALU.add, op1=ALU.mult))
            link(V.tensor_copy(gate2, adac[:, 40:48]))
            for n in range(DC):
                u = U_OUT + n
                dve.wait_ge(unit_done, u + 1)
                V.scalar_tensor_tensor(out=xT[:, n, :], in0=G(u), scalar=gate1[:, n:n + 1], in1=xT[:, n, :],
                                       op0=ALU.mult, op1=ALU.add).then_inc(bank_read[u % 2], 1)
                taken(dve, u)
                V.tensor_scalar(xa[:, n, :], xT[:, n, :], a2[:, n:n + 1], None, ALU.mult).then_inc(x1_scaled, 1)
                if 1 <= n < DC - 1:
                    dve.wait_ge(x1_squared, n + 1)
                    V.tensor_tensor(sqacc[:], sqacc[:], sq2[:, n % 2, :], ALU.add).then_inc(squares_added, 1)
                    dve.wait_ge(squares_added, n)
            dve.wait_ge(x1_rstd, 1)
            for d in range(DC + 2):
                if d < DC and d % 2 == 0:
                    V.tensor_tensor(xa[:, d, :], xa[:, d, :], rs2[:], ALU.mult).then_inc(u2_even, 1)
                if d >= 2:
                    k = d - 2
                    dve.wait_ge(u2_hi, k + 1)
                    V.scalar_tensor_tensor(out=ulo[:, k, :], in0=xa[:, k, :], scalar=sh2[:, k:k + 1],
                                           in1=uhi[:, k, :].bitcast(F32), op0=ALU.add, op1=ALU.subtract).then_inc(
                        u2_lo, 1)
            with dve.Fori(0, NQ) as q:
                for j in range(DC):
                    n = DC * q + j
                    taken(dve, U_FF + j, QT * q)
                    V.tensor_tensor(r2buf[:], rbuf[:, j % 2, :], rbuf[:, j % 2, :], ALU.mult).then_inc(hdn_squared, 1)
                    dve.wait_ge(hdn_squared, n + 1)
                    dve.wait_ge(hdn_hi, n + 1)
                    V.tensor_tensor(hlo[:, j, :], r2buf[:], hhi[:, j, :].bitcast(F32), ALU.subtract).then_inc(hdn_lo, 1)
                    dve.wait_ge(hdn_lo, n + 1)
                for j in range(DC):
                    u = U_FF + DC + j
                    dve.wait_ge(unit_done, u + 1 + QU * q)
                    taken(dve, u - QU, QT * q)
                    V.scalar_tensor_tensor(out=xT[:, j, :], in0=G(u), scalar=gate2[:, j:j + 1], in1=xT[:, j, :],
                                           op0=ALU.mult, op1=ALU.add).then_inc(bank_read[u % 2], 1)

        @block.tensor
        def _(pe):
            T = nc.tensor
            pe.wait_ge(c_in, 16)
            pe.wait_ge(identity_made, 1)
            T.transpose(ps[:, 7, 0:DC], crow[:], ident[0:DC, 0:DC]).then_inc(c_transposed, 1)
            pe.wait_ge(x_in, 16)
            pe.wait_ge(consts_set, 1)
            for d in range(DC):
                if d >= 4:
                    pe.wait_ge(x_squared, d - 3)
                for t in range(TT):
                    last = T.transpose(ps[:, d % 4, t * P:(t + 1) * P], xtok[:, t, d * P:(d + 1) * P], ident[:])
                last.then_inc(x_transposed, 1)
                if d >= 1:
                    pe.wait_ge(x_squared, d)
                    T.matmul(ps[:, 6, :], ones[:], n1sq[:, (d - 1) % 2, :], start=d == 1, stop=False).then_inc(
                        x_sumsq, 1)
            pe.wait_ge(x_squared, DC)
            T.matmul(ps[:, 6, :], ones[:], n1sq[:, (DC - 1) % 2, :], start=False, stop=True).then_inc(x_sumsq, 1)
            pe.wait_ge(vec_in, 16 * 8)
            T.transpose(ps[:, 4, 0:N_VEC], vrows[0:N_VEC, :], ident[0:N_VEC, 0:N_VEC]).then_inc(vec_transposed, 1)
            pe.wait_ge(oh_in, 32)
            pe.wait_ge(vec_columns, 1)
            T.matmul(ps[0:NG * AH, 5, :], relb[:], onehot[:, 0:512], start=True, stop=True)
            T.matmul(ps[0:NG * AH, 4, 0:TSUM - 512], relb[:], onehot[:, 512:TSUM], start=True, stop=True).then_inc(
                frow_product, 1)
            def keep_warm(n):
                for _ in range(n):
                    T.matmul(ps[:, 3, :], ones[:], xT[:, 0, :], start=True, stop=True)

            keep_warm(WARM)
            pe.wait_ge(ada_accumulated, 8)
            for i in range(16):
                last = T.matmul(ps[:, 7, i:i + 1], ada1[:, i * P:(i + 1) * P], ones[:, 0:1], start=True, stop=True)
            last.then_inc(ada_transposed, 1)
            keep_warm(WARM2)
            pe.wait_ge(if_lo, 1)
            for k in range(DC):
                pe.wait_ge(u_lo, k + 1)
                for bank, hi, lo, done in ((2, ifhi[:, k, :], iflo[:, k, :], if_product),
                                           (0, whi[:, 0, k, :], wlo[:, 0, k, :], unit_done)):
                    if k == 0 and bank == 0:
                        pe.wait_ge(w_lo_ready, 1)
                    T.matmul(ps[:, bank, :], hi, uhi[:, k, :], start=k == 0, stop=False)
                    T.matmul(ps[:, bank, :], hi, ulo[:, k, :], start=False, stop=False)
                    last = T.matmul(ps[:, bank, :], lo, uhi[:, k, :], start=False, stop=k == DC - 1)
                    if k == DC - 1:
                        last.then_inc(done, 1)

            def unit(u, mhi, mlo, ready=None, amid=None, turn=0):
                pe.wait_ge(w_lo_ready, u + 1 + RING * turn)
                if u >= 2:
                    taken(pe, u - 2, turn)
                kc, s, b = kchunks(u), u % RING, u % 2
                for k in range(kc):
                    if ready is not None:
                        pe.wait_ge(ready[0], ready[1] + k + 1)
                    T.matmul(ps[:, b, :], whi[:, s, k, :], mhi[:, k, :], start=k == 0, stop=False)
                    T.matmul(ps[:, b, :], whi[:, s, k, :], mlo[:, k, :], start=False, stop=False)
                    last = T.matmul(ps[:, b, :], wlo[:, s, k, :], mhi[:, k, :], start=False, stop=k == kc - 1)
                    if amid:
                        amid(k)
                last.then_inc(unit_done, 1)

            for u in range(U_CONV + 1, U_MO):
                unit(u, uhi, ulo)
                if u == 4:
                    pe.wait_ge(rows_ready, 1)
                    for a, r in ((0, 0), (1, 2)):
                        for t in range(TT):
                            last = T.transpose(ps[:, 3, 32 * a + 8 * t:32 * a + 8 * t + 8],
                                               rows[0:8, r, t * P:(t + 1) * P], ident[0:8, 0:8])
                    last.then_inc(e_transposed, 1)
                if u == 7:
                    pe.wait_ge(stage_in, 48)
                    pe.wait_ge(identity_made, 2)
                    pe.wait_ge(e_columns, 1)
                    for h in range(AH):
                        T.matmul(ps[:, 3 + h // 2, 256 * (h % 2):256 * (h % 2) + 256], flip[:], stage[:, h, 0:2 * P],
                                 start=True, stop=True)
                    for h in range(AH):
                        T.matmul(ps[:, 5, P * h:P * h + P], flip[:], stage[:, h, 2 * P:3 * P], start=True, stop=True)
                    for h in range(AH):
                        last = T.matmul(ps[:, 6, P * h:P * h + P], flip[:], stage[:, h, 3 * P:], start=True, stop=True)
                    last.then_inc(bias_flipped, 1)

            with pe.Fori(0, (U_MV - U_MO) // RING) as turn:
                for i in range(RING):
                    unit(U_MO + i, uhi, ulo, turn=turn)

            def columns(g, k, k0):
                if not k0 <= k < k0 + 4:
                    return
                if k == k0:
                    pe.wait_ge(ada_accumulated, 8 * (g + 1))
                for i in range(4 * (k - k0), 4 * (k - k0) + 4):
                    last = T.matmul(ps[:, 7, 16 * g + i:16 * g + i + 1], (ada2, ada3)[g - 1][:, i * P:(i + 1) * P],
                                    ones[:, 0:1], start=True, stop=True)
                if k == k0 + 3:
                    last.then_inc(ada_transposed, 1)

            def m_scores(h, j):
                bank, c0 = ((2, 0), (3, 0), (2, 0), (3, 384))[j]
                w = SEQ - j * P
                if j == 2:
                    pe.wait_ge(mlstm_weights_ready, 4 * h + 1)
                k = kst[h % 2][:, j * P:(j + 1) * P]
                T.matmul(ps[:, bank, c0:c0 + w], k, qst[h % 2][:, j * P:], start=True, stop=False)
                T.matmul(ps[:, bank, c0:c0 + w], k, qsw[h % 2][:, j * P:], start=False, stop=True).then_inc(
                    mlstm_scores_done, 1)

            def m_turn(h):
                pe.wait_ge(hn_ready, h + 1)
                for t in range(TT):
                    last = T.transpose(ps[:, 4, t * P:(t + 1) * P], hn[:, t, :], ident[:])
                last.then_inc(h_transposed, 1)

            def m_num(h):
                pe.wait_ge(mlstm_weights_ready, 4 * (h + 1))
                pe.wait_ge(v_ready, h + 1)
                if h >= 1:
                    pe.wait_ge(hn_ready, h)
                for i in range(TT):
                    for j in range(i + 1):
                        c0 = EW[j] + (i - j) * P
                        last = T.matmul(ps[:, 6 + i // 2, (i % 2) * 256:(i % 2) * 256 + DV + 1],
                                        wts[:, h % 2, c0:c0 + P],
                                        vext[:, h % 2, j, :], start=j == 0, stop=j == i)
                last.then_inc(mlstm_numerator_done, 1)

            for h in range(MLH):
                def amid(k, h=h):
                    if h == 0:
                        columns(1, k, DC - 4)
                    elif k == 2:
                        m_scores(h - 1, 2)

                unit(U_MV + h, uhi, ulo, amid=amid)
                if h == 0:
                    pe.wait_ge(bias_ready, 1)
                else:
                    pe.wait_ge(decay_exp, h)
                if h >= 2:
                    m_turn(h - 2)
                T.matmul(ps[:, 5, :], selr[:, h:h + 1].to_broadcast([32 + MLH, P]), negM[:], start=True,
                         stop=True).then_inc(negM_broadcast, 1)
                pe.wait_ge(stack_lo, 3 * (h + 1))
                if h:
                    pe.wait_ge(mlstm_weights_ready, 4 * h)
                m_scores(h, 0)
                m_scores(h, 1)
                m_scores(h, 3)
                if h >= 2:
                    pe.wait_ge(h_gated, h - 1)
                if h >= 1:
                    pe.wait_ge(v_ready, h)
                taken(pe, U_MV + h)
                for t in range(TT):
                    last = T.transpose(ps[:, 4, t * P:(t + 1) * P], mvT[:, t * P:(t + 1) * P], ident[:])
                last.then_inc(mv_transposed, 1)
                if h == 1:
                    pe.wait_ge(ada_columns, 2)
                if h >= 1:
                    m_num(h - 1)

            def v_turn(j):
                taken(pe, U_ATT + 3 * j + 2)
                if j >= 1:
                    pe.wait_ge(probsT_ready, j)
                for t in range(TT):
                    last = T.transpose(ps[:, 4, t * P:(t + 1) * P], vTp[:, t * P:(t + 1) * P], ident[:])
                last.then_inc(v_transposed, 1)

            def scores(j):
                pe.wait_ge(qk_normed, 2 * (j + 1))
                if j >= 1:
                    pe.wait_ge(row_max_ready, j)
                for t in range(TT):
                    q = qn[:, t * P:(t + 1) * P]
                    if j % NG == 0:
                        lo = P if t == 0 else 0
                        o = ps[:, 2 + t // 2, (t % 2) * 256 + lo:(t % 2) * 256 + 256]
                        last = T.matmul(o, q, kn[:, t * P - P + lo:(t + 1) * P], start=True, stop=True)
                    else:
                        last = T.matmul(ps[:, 2, t * P:(t + 1) * P], q, kn[:, t * P:(t + 1) * P], start=True, stop=True)
                last.then_inc(scores_done, 1)

            def p_turn(j):
                pe.wait_ge(probs_ready, j + 1)
                pe.wait_ge(v_tokens, j + 1)
                slot = 0
                for t in range(TT):
                    for half in ((0, 1) if j % NG == 0 and t else (1,)):
                        c0 = half * P if j % NG == 0 else 0
                        last = T.transpose(ps[:, 4 + slot // 4, (slot % 4) * P:(slot % 4 + 1) * P],
                                           prob[:, t, c0:c0 + P], ident[:])
                        slot += 1
                last.then_inc(probs_transposed, 1)

            def p_v(j):
                pe.wait_ge(probsT_ready, j + 1)
                if j >= 1:
                    pe.wait_ge(o_copied, j)
                for t in range(TT):
                    o = ps[:, 7, t * P:(t + 1) * P]
                    if j % NG == 0 and t:
                        T.matmul(o, vtok[:, j % 2, t - 1], probT[:, 2 * t - 1], start=True, stop=False)
                        last = T.matmul(o, vtok[:, j % 2, t], probT[:, 2 * t], start=False, stop=True)
                    else:
                        last = T.matmul(o, vtok[:, j % 2, t], probT[:, t if j % NG else 0], start=True, stop=True)
                last.then_inc(pv_done, 1)

            def sumsq(n):
                taken(pe, U_ATT + 3 * (n // 2) + n % 2)
                if n >= 1:
                    pe.wait_ge(qk_rstd, n)
                else:
                    pe.wait_ge(hn_ready, MLH)
                pe.wait_ge(squares_lo, n + 1)
                T.matmul(ps[:, 6, :], onesr[:], sqhi[:, n % 2, :], start=True, stop=False)
                T.matmul(ps[:, 6, :], onesr[:], sqlo[:], start=False, stop=True).then_inc(qk_sumsq, 1)

            def last_scores(k):
                if k == 2:
                    m_scores(MLH - 1, 2)

            for s in range(36):
                j, part = divmod(s, 3)
                unit(U_ATT + s, uhi, ulo, amid=last_scores if s == 0 else None)
                if s == 0:
                    m_turn(6)
                    m_num(7)
                if s == 1:
                    pe.wait_ge(h_gated, 7)
                    m_turn(7)
                if part == 0 and j >= 1:
                    if j == 1:
                        pe.wait_ge(h_gated, 8)
                    v_turn(j - 1)
                    scores(j - 1)
                if part == 0 and j >= 2:
                    p_v(j - 2)
                if part == 1:
                    sumsq(2 * j)
                if part == 2:
                    sumsq(2 * j + 1)
                    if j >= 1:
                        p_turn(j - 1)

            for t in range(16):
                n, part = divmod(t, 2)
                if part == 0:
                    unit(U_YML + t, uhi, ulo)
                else:
                    unit(U_YML + t, hhi, hlo, (h_lo, 0) if t == 1 else None)
                if t == 0:
                    v_turn(11)
                    scores(11)
                    p_v(10)
                if t == 2:
                    p_turn(11)
                if t == 3:
                    p_v(11)
                if t == 4:
                    pe.wait_ge(o_copied, NG * AH)
                    for g in range(NG):
                        for a in range(2):
                            for i in range(TT):
                                last = T.matmul(ps[0:AH, 2 + 2 * g + a, i * P:(i + 1) * P], stats[:, a, g, i, :],
                                                ident[:], start=True, stop=True)
                        last.then_inc(stats_turned, 1)
                if t >= 8 and t % 2 == 0:
                    h = (t - 8) // 2
                    pe.wait_ge(merge_weights, 1)
                    if h:
                        pe.wait_ge(broadcast_read, h)
                    for g in range(NG):
                        last = T.matmul(ps[:, 4 + g, :], selr[0:32 + AH, h:h + 1].to_broadcast([32 + AH, P]),
                                        mrr[:, g, :], start=True, stop=True)
                    last.then_inc(weights_broadcast, 1)
            def y_att(first, turn):
                for i in range(RING):
                    if i % 2 == 0:
                        unit(U_YATT + i, uhi, ulo, turn=turn)
                    else:
                        unit(U_YATT + i, ahi, alo, (att_lo, 0) if first and i == 1 else None, turn=turn)

            y_att(True, 0)
            with pe.Fori(1, (U_OUT - U_YATT) // RING) as turn:
                y_att(False, turn)
            for n in range(DC):
                unit(U_OUT + n, yhi, ylo, (y_lo, 0) if n == 0 else None,
                     amid=(lambda k: columns(2, k, 0)) if n == 1 else None)
            pe.wait_ge(squares_added, DC - 2)
            T.matmul(ps[:, 6, :], ones[:], sqacc[:], start=True, stop=False)
            pe.wait_ge(x1_squared, DC)
            T.matmul(ps[:, 6, :], ones[:], sq2[:, (DC - 1) % 2, :], start=False, stop=True).then_inc(x1_sumsq, 1)
            keep_warm(4)

            def x_turn(n):
                taken(pe, U_FF + 56 + n)
                if n >= 2:
                    pe.wait_ge(out_tile, n - 1)
                for t in range(TT):
                    last = T.transpose(ps[:, 4 + n % 2, t * P:(t + 1) * P], xT[:, n, t * P:(t + 1) * P], ident[:])
                last.then_inc(x2_transposed, 1)

            def quarter(q, first=False, last=False):
                if first:
                    for k in range(DC):
                        pe.wait_ge(u2_lo, k + 1)
                        for u in (U_FF, U_FF + 1):
                            if k == 0:
                                pe.wait_ge(w_lo_ready, u + 1)
                                taken(pe, u - 2)
                            hi, lo, b = whi[:, u % RING, k, :], wlo[:, u % RING, k, :], u % 2
                            T.matmul(ps[:, b, :], hi, uhi[:, k, :], start=k == 0, stop=False)
                            T.matmul(ps[:, b, :], hi, ulo[:, k, :], start=False, stop=False)
                            ins = T.matmul(ps[:, b, :], lo, uhi[:, k, :], start=False, stop=k == DC - 1)
                            if k == DC - 1:
                                ins.then_inc(unit_done, 1)
                for j in range(2 if first else 0, DC):
                    unit(U_FF + j, uhi, ulo, turn=QT * q)
                for j in range(DC):
                    unit(U_FF + DC + j, hhi, hlo, (hdn_lo, DC * q) if j == 0 else None, turn=QT * q)
                    if last and j >= 1:
                        x_turn(j - 1)

            quarter(0, first=True)
            with pe.Fori(1, NQ - 1) as q:
                quarter(q)
            quarter(NQ - 1, last=True)
            x_turn(DC - 1)


_INS = ['x', 'c', 'w_ada', 'b_ada', 'norm1_g', 'norm2_g', 'w_in', 'b_if', 'conv_w', 'conv_b', 'q_norm_g', 'k_norm_g',
        'rel_bias', 'mlstm_norm_g', 'w_att_out', 'w_ml_out', 'w_out', 'w_ff1', 'w_ff2']
_OUTS = [((1, SEQ, D), 'float32')]


def kernel(**inputs):
    import numpy as _np
    import concourse.bacc as _bacc
    from concourse import mybir as _mybir
    from concourse.bass_utils import run_bass_kernel_spmd as _run

    nc = _bacc.Bacc("TRN2", target_bir_lowering=False, num_devices=1)
    arrays, args = {}, []
    data = [(name, _np.ascontiguousarray(inputs[name])) for name in _INS] + [("one_hot", bucket_one_hot())]
    for name, a in data:
        arrays[f"in_{name}_dram"] = a
        args.append(nc.dram_tensor(f"in_{name}_dram", a.shape, _mybir.dt.from_np(a.dtype), kind="ExternalInput").ap())
    for i, (shape, dtype) in enumerate(_OUTS):
        dt = _mybir.dt.from_np(_np.dtype(dtype))
        args.append(nc.dram_tensor(f"out_{i}_dram", shape, dt, kind="ExternalOutput").ap())
    block_kernel(nc, *args)
    r = _run(nc, [arrays], core_ids=[0])
    got = tuple(r.results[0][f"out_{i}_dram"] for i in range(len(_OUTS)))
    return got[0]
```
